# Optimizing a Trainium2 kernel written in Bass

```python
import jax, jax.numpy as jnp
from jax import lax
import numpy as np

D_MODEL = 1024
BATCH = 1
SEQ = 256
DEPTH = 2

CHUNK = 64
N_MEM = 256
EPS = 1e-6

MEM_HEADS = 4
MEM_HEAD_DIM = 64
MEM_WIDTH = MEM_HEADS * MEM_HEAD_DIM
MAIN_WIDTH = D_MODEL - MEM_WIDTH

GLA_HEADS = 4
GLA_KEY_WIDTH = MAIN_WIDTH // 2
GLA_DK = GLA_KEY_WIDTH // GLA_HEADS
GLA_DV = MAIN_WIDTH // GLA_HEADS
GLA_GATE_RANK = 16
GLA_GATE_TAU = 16.0

FOX_HEADS = 12
FOX_HEAD_DIM = MAIN_WIDTH // FOX_HEADS
FOX_QBLOCK = 128

D_FF = 2816
N_EXPERTS = 8
TOP_K = 2

N_A_LAYERS = DEPTH // 2
N_B_LAYERS = DEPTH - N_A_LAYERS
N_DENSE = (DEPTH + 1) // 2
N_MOE = DEPTH // 2

A_IN_WIDTH = 2 * GLA_KEY_WIDTH + 2 * MAIN_WIDTH + GLA_GATE_RANK + MEM_WIDTH
B_IN_WIDTH = MAIN_WIDTH + MEM_WIDTH
KV_WIDTH = 2 * MAIN_WIDTH + FOX_HEADS

kernel_name = 'hybrid_gla_fox_yoco_moe_encoder'

def rmsnorm(x, g):
    xf = x.astype(jnp.float32)
    y = xf * lax.rsqrt(jnp.mean(xf * xf, axis=-1, keepdims=True) + EPS)
    return (y * g.astype(jnp.float32)).astype(x.dtype)

def split_cols(t, widths):
    out, start = [], 0
    for w in widths:
        out.append(t[..., start:start + w])
        start += w
    return out

def swiglu(h, w_gate, w_up, w_down):
    return (jax.nn.silu(h @ w_gate) * (h @ w_up)) @ w_down

def gla_scan(q, k, v, log_a):
    bsz, seq, heads, dk = q.shape
    dv = v.shape[-1]
    nc = seq // CHUNK

    def to_chunks(t):
        return t.astype(jnp.float32).reshape(bsz, nc, CHUNK, heads, t.shape[-1]).transpose(1, 0, 3, 2, 4)

    qc, kc, vc = to_chunks(q), to_chunks(k), to_chunks(v)
    bc = jnp.cumsum(to_chunks(log_a), axis=-2)
    causal = jnp.tril(jnp.ones((CHUNK, CHUNK), dtype=bool))

    def step(state, inp):
        q_, k_, v_, b_ = inp
        o_inter = jnp.einsum('bhtk,bhkv->bhtv', q_ * jnp.exp(b_), state)
        diff = b_[:, :, :, None, :] - b_[:, :, None, :, :]
        decay = jnp.exp(jnp.where(causal[:, :, None], diff, -jnp.inf))
        scores = jnp.sum(q_[:, :, :, None, :] * k_[:, :, None, :, :] * decay, axis=-1)
        o_intra = jnp.einsum('bhts,bhsv->bhtv', scores, v_)
        b_last = b_[:, :, -1:, :]
        state = state * jnp.exp(b_last[:, :, 0, :, None]) + jnp.einsum(
            'bhsk,bhsv->bhkv', k_ * jnp.exp(b_last - b_), v_)
        return state, o_inter + o_intra

    state0 = jnp.zeros((bsz, heads, dk, dv), jnp.float32)
    _, o = lax.scan(step, state0, (qc, kc, vc, bc))
    return o.transpose(1, 0, 3, 2, 4).reshape(bsz, seq, heads, dv).astype(v.dtype)

def fox_attention(q, k, v, c):
    bsz, seq, heads, dh = q.shape
    nb = seq // FOX_QBLOCK
    qb = q.reshape(bsz, nb, FOX_QBLOCK, heads, dh).transpose(1, 0, 3, 2, 4)
    cb = c.reshape(bsz, heads, nb, FOX_QBLOCK).transpose(2, 0, 1, 3)
    kpos = jnp.arange(seq)
    scale = dh ** -0.5

    def block(args):
        i, q_, c_ = args
        s = jnp.einsum('bhqd,bshd->bhqs', q_, k).astype(jnp.float32) * scale
        s = s + c_[..., None] - c[:, :, None, :]
        qpos = i * FOX_QBLOCK + jnp.arange(FOX_QBLOCK)
        s = jnp.where(kpos[None, :] <= qpos[:, None], s, -jnp.inf)
        p = jax.nn.softmax(s, axis=-1).astype(v.dtype)
        return jnp.einsum('bhqs,bshd->bhqd', p, v)

    o = lax.map(block, (jnp.arange(nb), qb, cb))
    return o.transpose(1, 0, 3, 2, 4).reshape(bsz, seq, heads * dh)

def mem_attention(q, mem_n, w_mem_kv):
    bsz, seq, _ = q.shape
    k, v = split_cols(mem_n @ w_mem_kv, (MEM_WIDTH, MEM_WIDTH))
    k = k.reshape(bsz, -1, MEM_HEADS, MEM_HEAD_DIM)
    v = v.reshape(bsz, -1, MEM_HEADS, MEM_HEAD_DIM)
    qh = q.reshape(bsz, seq, MEM_HEADS, MEM_HEAD_DIM)
    s = jnp.einsum('bshd,bmhd->bhsm', qh, k).astype(jnp.float32) * (MEM_HEAD_DIM ** -0.5)
    p = jax.nn.softmax(s, axis=-1).astype(v.dtype)
    return jnp.einsum('bhsm,bmhd->bshd', p, v).reshape(bsz, seq, MEM_WIDTH)

def moe_swiglu(h, w_router, w_gate, w_up, w_down):
    logits = (h @ w_router).astype(jnp.float32)
    top_val, top_idx = lax.top_k(logits, TOP_K)
    top_w = jax.nn.softmax(top_val, axis=-1)
    gates = jnp.sum(jax.nn.one_hot(top_idx, N_EXPERTS, dtype=jnp.float32) * top_w[..., None],
                    axis=-2).astype(h.dtype)
    y = jnp.zeros_like(h)
    for e in range(N_EXPERTS):
        y = y + gates[..., e:e + 1] * swiglu(h, w_gate[e], w_up[e], w_down[e])
    return y

def setup_inputs(seed: int = 0) -> dict:
    key = jax.random.key(seed)
    ks = jax.random.split(key, 24)
    f32 = jnp.float32

    def nrm(k, shape, fan_in):
        return jax.random.normal(k, shape, f32) * (fan_in ** -0.5)

    def gain(k, shape):
        return 1.0 + 0.02 * jax.random.normal(k, shape, f32)

    return {
        'x': jax.random.normal(ks[0], (BATCH, SEQ, D_MODEL), f32),
        'mem': jax.random.normal(ks[1], (BATCH, N_MEM, D_MODEL), f32),
        'norm_mix': gain(ks[2], (DEPTH, D_MODEL)),
        'norm_mem': gain(ks[3], (DEPTH, D_MODEL)),
        'norm_ffn': gain(ks[4], (DEPTH, D_MODEL)),
        'norm_kv': gain(ks[5], (D_MODEL,)),
        'norm_final': gain(ks[6], (D_MODEL,)),
        'w_in_a': nrm(ks[7], (N_A_LAYERS, D_MODEL, A_IN_WIDTH), D_MODEL),
        'w_gla_gate2': nrm(ks[8], (N_A_LAYERS, GLA_GATE_RANK, GLA_KEY_WIDTH), GLA_GATE_RANK),
        'b_gla_gate2': 0.01 * jax.random.normal(ks[9], (N_A_LAYERS, GLA_KEY_WIDTH), f32),
        'gla_onorm': gain(ks[10], (N_A_LAYERS, GLA_DV)),
        'w_in_b': nrm(ks[11], (N_B_LAYERS, D_MODEL, B_IN_WIDTH), D_MODEL),
        'w_kv': nrm(ks[12], (D_MODEL, KV_WIDTH), D_MODEL),
        'b_forget': 3.0 + 0.5 * jax.random.normal(ks[13], (FOX_HEADS,), f32),
        'w_mem_kv': nrm(ks[14], (DEPTH, D_MODEL, 2 * MEM_WIDTH), D_MODEL),
        'w_out': nrm(ks[15], (DEPTH, MAIN_WIDTH + MEM_WIDTH, D_MODEL), MAIN_WIDTH + MEM_WIDTH),
        'w_ff_gate': nrm(ks[16], (N_DENSE, D_MODEL, D_FF), D_MODEL),
        'w_ff_up': nrm(ks[17], (N_DENSE, D_MODEL, D_FF), D_MODEL),
        'w_ff_down': nrm(ks[18], (N_DENSE, D_FF, D_MODEL), D_FF),
        'w_router': nrm(ks[19], (N_MOE, D_MODEL, N_EXPERTS), D_MODEL),
        'w_moe_gate': nrm(ks[20], (N_MOE, N_EXPERTS, D_MODEL, D_FF), D_MODEL),
        'w_moe_up': nrm(ks[21], (N_MOE, N_EXPERTS, D_MODEL, D_FF), D_MODEL),
        'w_moe_down': nrm(ks[22], (N_MOE, N_EXPERTS, D_FF, D_MODEL), D_FF),
    }

def reference(x, mem, norm_mix, norm_mem, norm_ffn, norm_kv, norm_final, w_in_a, w_gla_gate2,
              b_gla_gate2, gla_onorm, w_in_b, w_kv, b_forget, w_mem_kv, w_out, w_ff_gate, w_ff_up,
              w_ff_down, w_router, w_moe_gate, w_moe_up, w_moe_down):
    bsz, seq, _ = x.shape
    k_sh = v_sh = c_sh = None
    for layer in range(DEPTH):
        if layer == N_A_LAYERS:
            kvp = rmsnorm(x, norm_kv) @ w_kv
            k_sh, v_sh, f_logit = split_cols(kvp, (MAIN_WIDTH, MAIN_WIDTH, FOX_HEADS))
            k_sh = k_sh.reshape(bsz, seq, FOX_HEADS, FOX_HEAD_DIM)
            v_sh = v_sh.reshape(bsz, seq, FOX_HEADS, FOX_HEAD_DIM)
            log_f = jax.nn.log_sigmoid((f_logit + b_forget).astype(jnp.float32))
            c_sh = jnp.cumsum(log_f, axis=1).transpose(0, 2, 1)

        hn = rmsnorm(x, norm_mix[layer])
        mem_n = rmsnorm(mem, norm_mem[layer])
        if layer < N_A_LAYERS:
            i = layer
            q, k, v, r, glr, mq = split_cols(
                hn @ w_in_a[i],
                (GLA_KEY_WIDTH, GLA_KEY_WIDTH, MAIN_WIDTH, MAIN_WIDTH, GLA_GATE_RANK, MEM_WIDTH))
            log_a = jax.nn.log_sigmoid(
                (glr @ w_gla_gate2[i] + b_gla_gate2[i]).astype(jnp.float32)) / GLA_GATE_TAU
            o = gla_scan(
                q.reshape(bsz, seq, GLA_HEADS, GLA_DK) * (GLA_DK ** -0.5),
                k.reshape(bsz, seq, GLA_HEADS, GLA_DK),
                v.reshape(bsz, seq, GLA_HEADS, GLA_DV),
                log_a.reshape(bsz, seq, GLA_HEADS, GLA_DK))
            o = rmsnorm(o, gla_onorm[i]) * jax.nn.silu(r.reshape(bsz, seq, GLA_HEADS, GLA_DV))
            main = o.reshape(bsz, seq, MAIN_WIDTH)
        else:
            j = layer - N_A_LAYERS
            qf, mq = split_cols(hn @ w_in_b[j], (MAIN_WIDTH, MEM_WIDTH))
            main = fox_attention(qf.reshape(bsz, seq, FOX_HEADS, FOX_HEAD_DIM), k_sh, v_sh, c_sh)
        mixed = jnp.concatenate([main, mem_attention(mq, mem_n, w_mem_kv[layer])], axis=-1)
        x = x + mixed @ w_out[layer]

        hn = rmsnorm(x, norm_ffn[layer])
        f = layer // 2
        if layer % 2 == 0:
            x = x + swiglu(hn, w_ff_gate[f], w_ff_up[f], w_ff_down[f])
        else:
            x = x + moe_swiglu(hn, w_router[f], w_moe_gate[f], w_moe_up[f], w_moe_down[f])
    return rmsnorm(x, norm_final)


_drawn_inputs = setup_inputs


def setup_inputs(seed=0):
    import zlib

    import numpy as np

    out = dict(_drawn_inputs(seed))
    spreads = {}
    factors = {'norm_mem': 3.531,
     'norm_kv': 3.634,
     'norm_final': 20.676,
     'b_gla_gate2': 13.149,
     'gla_onorm': 3.046,
     'norm_ffn': 2.976}
    for name, (base, spread) in spreads.items():
        noise = np.random.default_rng([zlib.crc32(name.encode()), seed]).standard_normal(out[name].shape)
        drawn = base * np.exp(spread * noise) if base else spread * noise
        out[name] = __import__('jax').numpy.asarray(drawn.astype(out[name].dtype))
    for name, factor in factors.items():
        out[name] = (out[name] * factor).astype(out[name].dtype)
    return out
```

```python
import concourse.bass as bass
from concourse import mybir
from contextlib import ExitStack
import numpy as np

F32 = mybir.dt.float32
I32 = mybir.dt.int32
U32 = mybir.dt.uint32
ALU = mybir.AluOpType
ACT = mybir.ActivationFunctionType
AX = mybir.AxisListType.X

P = 128
D = 1024
KC = D // P
S = 256
TB = S // P
EPS = 1e-6
MAIN = 768
MEMW = 256
MH, MD = 4, 64
GH, DK, DV = 4, 96, 192
RANK = 16
CHUNK = 64
LEVELS = 6
FH, FD = 12, 64
DFF = 2816
FC = 256
NF = DFF // FC
NE = 8
CAP = 128
SLOT = 6144
RING_PRE, RING_MOE = 3, 6
NEG = -1e30


def constant_columns():
    at, cols = {}, 0
    for name, n in (("ident", P), ("tri16", P), ("tri", P), ("ones", P), ("levels", LEVELS * P),
                    ("causal", 3 * P), ("slots", 2 * P), ("earlier", NE * NE), ("mhalf", 8)):
        at[name] = (cols, n)
        cols += n
    return at, cols


def constant_table():
    at, cols = constant_columns()
    c = np.zeros((P, cols), np.float32)
    i = np.arange(P)
    s, t = i[:, None], i[None, :]

    def put(name, value):
        c[:, at[name][0]:at[name][0] + at[name][1]] = value

    put("ident", s == t)
    put("tri16", ((s <= t) & (s // CHUNK == t // CHUNK)) / 16.0)
    put("tri", s <= t)
    put("ones", 1.0)
    put("levels", np.concatenate(
        [(s // (2 * h) == t // (2 * h)) & (s % (2 * h) < h) & (t % (2 * h) >= h)
         for h in (CHUNK // 2 >> n for n in range(LEVELS))], axis=1))
    later = np.where(t <= s, 0.0, NEG)
    put("causal", np.concatenate([later, 0.0 * later, later], axis=1))
    put("slots", np.arange(2 * P)[None, :])
    e = np.arange(NE)
    put("earlier", (e[None, :] < e[:, None]).reshape(1, -1))
    put("mhalf", -0.5)
    return c


def early_jobs():
    names = [f"TX{i}" for i in range(4)] + ["GLR", "Z0", "Z1", "Q0", "Q1", "K0", "K1"]
    names += [f"TM{i}" for i in range(4)] + ["B0", "B1", "MQ", "KM0", "VM0"]
    names += ["L0_0", "L0_1", "V00", "V01", "L1_0", "L1_1", "V10", "V11", "L2_0", "L2_1"]
    names += ["KM1", "L3_0", "L3_1", "VM1", "L4_0", "L4_1", "SM0", "SM1", "L5_0", "L5_1"]
    names += ["SM2", "SM3", "L6_0", "L6_1", "KH0", "KH1", "R00", "R01", "R10", "R11"]
    names += [f"U{c}_{hp}" for c in range(3) for hp in range(2)]
    names += [f"PM{i}" for i in range(4)] + ["MV"]
    names += ["O00", "O01", "O10", "O11"]
    names += [f"TO{i}" for i in range(4)] + ["WA0", "WA1", "WB0", "WB1"]
    names += [f"TF{i}" for i in range(4)]
    jobs = [(n, i % 8) for i, n in enumerate(names)]
    jobs += [(f"Y{i}", i) for i in range(4)]
    for f in range(NF):
        jobs += [(f"G{f}_{b}", 4 + b) for b in range(TB)] + [(f"T{f}", 6 + f % 2)]
    names = [f"TK{i}" for i in range(4)] + ["FG", "FK0", "FK1", "FK2", "CC"]
    names += ["FV00", "FV01", "FV10", "FV11", "FQ0", "FQ1", "FQ2", "MQ1"]
    names += [f"N{i}" for i in range(4)]
    names += [f"S{h}" for h in range(FH)] + [f"PN{i}" for i in range(4)] + ["MW"]
    for h in range(FH):
        names += [f"PF{h}"] + ([f"FO{(h - 2) // 4}"] if h >= 2 and (h - 2) % 4 == 0 else [])
    names += [f"TP{i}" for i in range(4)] + ["XA0", "XA1", "XB0", "XB1"]
    names += [f"TR{i}" for i in range(4)] + ["RL", "POS", "CNT"]
    jobs += [(n, i % 8) for i, n in enumerate(names)]
    return jobs


def expert_jobs():
    jobs = [("GA0", 5), ("GA1", 6), ("ST", 7), ("D0", 0), ("D1", 1)]
    for f in range(NF):
        jobs += [(f"G{f}", 2 + f % 2), (f"T{f}", 4)]
    jobs += [("SC0", 5), ("SC1", 6), ("SC2", 7), ("SC3", 5)]
    return jobs


def program(nc, a, table, out):
    at, ncols = constant_columns()
    ctx = ExitStack()
    with ctx:
        def sb(name, shape, dt=F32):
            return ctx.enter_context(nc.sbuf_tensor(name, shape, dt))

        sems = {}

        def sem(name):
            if name not in sems:
                sems[name] = ctx.enter_context(nc.semaphore(name))
            return sems[name]

        ring = sb("ring", [P, RING_MOE, SLOT])
        consts = sb("consts", [P, ncols])
        x = sb("x", [P, TB, D])
        xs = sb("xs", [P, TB, D])
        hT = sb("hT", [P, KC, S])
        mixed = sb("mixed", [P, TB, D])
        extra = sb("extra", [P, 5120])
        small = sb("small", [P, 640])
        psum = [ctx.enter_context(nc.psum_tensor(f"bank{i}", [P, 512], F32)) for i in range(8)]
        counts = sb("counts", [1, 16])
        over = sb("over", [1, 2], I32)

        class Carve:
            def __init__(self, base):
                self.base, self.n = base, 0

            def __call__(self, n, at=None):
                lo = self.n if at is None else at
                self.n = lo + n
                assert self.n <= self.base.shape[1], (self.n, self.base.shape)
                return self.base[:, lo:lo + n]

        def const(name):
            lo, n = at[name]
            return consts[:, lo:lo + n]

        ident = const("ident")
        arena = ring[:, RING_PRE:RING_MOE, :].rearrange("p a n -> p (a n)")
        g = Carve(arena)
        mT0 = g(2048).rearrange("p (c s) -> p c s", c=KC)
        mT1 = g(2048).rearrange("p (c s) -> p c s", c=KC)
        zbuf = g(2304)
        qT, kT, bT = (g(1024) for _ in range(3))
        decay = g(1024)
        prod = [g(1024), g(1024)]
        scoreT = g(1024).rearrange("p (b h t) -> p b h t", b=TB, h=GH)
        khat = g(768).rearrange("p (b h k) -> p b h k", b=TB, h=GH)
        kmT0 = g(1024).rearrange("p (h s) -> p h s", h=MH)
        mqT0 = g(1024).rearrange("p (h s) -> p h s", h=MH)
        vm0 = g(512).rearrange("p (b n) -> p b n", b=TB)
        alast, blast = g(16), g(16)
        zz, ez, la = (zbuf[:, 768 * i:768 * i + 768] for i in range(3))
        la_v = la.rearrange("p (b n) -> p b n", b=TB)
        state = zbuf.rearrange("p (c h v) -> p c h v", c=3, h=GH)
        pm0 = mT0.rearrange("p c s -> p (c s)").rearrange("p (b h m) -> p b h m", b=TB, h=MH)
        pmT0 = mT1.rearrange("p c s -> p (c s)").rearrange("p (m b h t) -> p m b h t", m=2, b=TB, h=MH)

        f = Carve(arena)
        fqT = f(FH * S).rearrange("p (h s) -> p h s", h=FH)
        fkT = f(FH * S).rearrange("p (h s) -> p h s", h=FH)
        logits = f(FH * 384).rearrange("p (h s) -> p h s", h=FH)
        probT = [f(384) for _ in range(4)]
        cT = f(256)
        negcT = f(256)
        hT2 = logits[:, 0:6, :].rearrange("p h s -> p (h s)")[:, 0:KC * S].rearrange("p (c s) -> p c s", c=KC)
        mqT1 = f(1024).rearrange("p (h s) -> p h s", h=MH)
        pm1 = f(2048).rearrange("p (b h m) -> p b h m", b=TB, h=MH)
        pmT1 = f(2048).rearrange("p (m b h t) -> p m b h t", m=2, b=TB, h=MH)

        d = Carve(arena)
        d_sg = d(512).rearrange("p (b n) -> p b n", b=TB)
        d_h = d(512).rearrange("p (b n) -> p b n", b=TB)
        d_hT = [d(512).rearrange("p (j t) -> p j t", j=2) for _ in range(2)]

        v = Carve(extra)
        kmT1 = v(1024).rearrange("p (h s) -> p h s", h=MH)
        vm1 = v(512).rearrange("p (b n) -> p b n", b=TB)
        val = v(1536).rearrange("p (b n) -> p b n", b=TB)
        glrT = v(256)
        w2 = v(384)
        final_row = v(1024)
        wf = v(96).rearrange("p (c n) -> p c n", c=KC)
        wr = v(64).rearrange("p (c n) -> p c n", c=KC)
        bf = v(12)

        m = Carve(mixed[:, :, :].rearrange("p b d -> p (b d)"))
        e_sg, e_h = m(256), m(256)
        e_hT = m(2 * CAP).rearrange("p (j t) -> p j t", j=2)
        perm = m(2 * CAP).rearrange("p (b s) -> p b s", b=TB)
        wperm = m(2 * CAP).rearrange("p (b s) -> p b s", b=TB)
        scat = m(256).rearrange("p (b t) -> p b t", b=TB)
        hTe = hT[:, :, :].rearrange("p c s -> p (c s)")[:, 0:KC * CAP].rearrange("p (c s) -> p c s", c=KC)
        yE = hT[:, :, :].rearrange("p c s -> p (c s)")[:, 1024:2048]

        w = Carve(small)
        GAINS = ("mix0", "mem0", "mem1", "mix1", "ffn0", "ffn1", "kv", "onorm")
        gains = {n: w(KC) for n in GAINS}
        square = {n: w(2) for n in ("x", "mem", "ffn0", "kv", "ffn1", "final")}
        mean = {n: w(2) for n in square}
        rstd = {n: w(2) for n in square}
        o_sq, o_mean, o_rstd = (w(8) for _ in range(3))
        m_max = [w(8).rearrange("p (b h) -> p b h", b=TB) for _ in range(2)]
        m_sum = [w(8) for _ in range(2)]
        m_inv = [w(8) for _ in range(2)]
        f_max, f_sum, f_inv = (w(24) for _ in range(3))
        fz, fe = w(24), w(24)
        fl = w(24).rearrange("p (b h) -> p b h", b=TB)
        lg, ex, sel, gate_u = (w(16).rearrange("p (b e) -> p b e", b=TB) for _ in range(4))
        gt, eq = w(64).rearrange("p (e o) -> p e o", e=NE), w(64).rearrange("p (e o) -> p e o", e=NE)
        top, den, rden = w(2), w(2), w(2)
        r_mean = w(2)
        pos = w(18).rearrange("p (b e) -> p b e", b=TB)
        gate = w(18).rearrange("p (b e) -> p b e", b=TB)
        rank = w(8)

        fill, fills = {}, [0] * 8
        for name, bank in early_jobs():
            fills[bank] += 1
            fill[name] = (bank, fills[bank])
        before = list(fills)
        e_fill, per = {}, [0] * 8
        for name, bank in expert_jobs():
            per[bank] += 1
            e_fill[name] = (bank, per[bank])

        def bank(name):
            return psum[fill[name][0]]

        def filled(eng, name):
            b, n = fill[name]
            eng.wait_ge(sem(f"bank{b}_full"), n)

        def read(eng, name):
            b, n = fill[name]
            eng.wait_ge(sem(f"bank{b}_read"), n)

        def free(eng, name):
            b, n = fill[name]
            if n > 1:
                eng.wait_ge(sem(f"bank{b}_read"), n - 1)

        def full_sem(name):
            return sem(f"bank{fill[name][0]}_full")

        def read_sem(name):
            return sem(f"bank{fill[name][0]}_read")

        def e_bank(name):
            return psum[e_fill[name][0]]

        def e_filled(eng, n, name):
            b, k = e_fill[name]
            eng.wait_ge(sem(f"bank{b}_full"), n * per[b] + (before[b] + k))

        def e_read(eng, n, name):
            b, k = e_fill[name]
            eng.wait_ge(sem(f"bank{b}_read"), n * per[b] + (before[b] + k))

        def e_free(eng, n, name):
            b, k = e_fill[name]
            eng.wait_ge(sem(f"bank{b}_read"), n * per[b] + (before[b] + k - 1))

        def e_filled_before(eng, n, name):
            b, k = e_fill[name]
            assert before[b] + k > per[b]
            eng.wait_ge(sem(f"bank{b}_full"), n * per[b] + (before[b] + k - per[b]))

        def e_read_before(eng, n, name):
            b, k = e_fill[name]
            assert before[b] + k > per[b]
            eng.wait_ge(sem(f"bank{b}_read"), n * per[b] + (before[b] + k - per[b]))

        def e_full_sem(name):
            return sem(f"bank{e_fill[name][0]}_full")

        def e_read_sem(name):
            return sem(f"bank{e_fill[name][0]}_read")

        def cols(wt, lo, hi):
            return wt.rearrange("(p c) n -> p c n", c=KC)[:, :, lo:hi]

        w_in_a, w_in_b = a["w_in_a"][0], a["w_in_b"][0]
        LOADS = [
            ([(0, cols(w_in_a, 2304, 2576))], "MQ"),
            ([(0, cols(w_in_a, 0, 768))], "K1"),
            ([(0, cols(a["w_mem_kv"][0], 0, 512))], "VM0"),
            ([(0, cols(w_in_a, 768, 1536))], "V11"),
            ([(0, cols(a["w_mem_kv"][1], 0, 512))], "VM1"),
            ([(0, cols(w_in_a, 1536, 2304))], "R11"),
            ([(0, cols(a["w_out"][0], 0, 512))], "WA1"),
            ([(0, cols(a["w_out"][0], 512, 1024))], "WB1"),
        ]

        def ffn_pieces(wg, wu, wd, lo):
            return [(0, cols(wg, lo, lo + FC)), (2048, cols(wu, lo, lo + FC)),
                    (4096, wd[lo:lo + FC, :].rearrange("(p j) n -> p j n", j=2))]

        FIRST_FFN = len(LOADS)
        for i in range(NF):
            LOADS.append((ffn_pieces(a["w_ff_gate"][0], a["w_ff_up"][0], a["w_ff_down"][0], i * FC), f"chunk{i}"))
        LOADS += [
            ([(0, cols(a["w_kv"], 0, 768))], "FK2"),
            ([(0, cols(a["w_kv"], 768, 1536))], "FV11"),
            ([(0, cols(w_in_b, 0, 768))], "FQ2"),
            ([(0, cols(w_in_b, 768, 1024))], "MQ1"),
            ([(0, cols(a["w_out"][1], 0, 512))], "XA1"),
            ([(0, cols(a["w_out"][1], 512, 1024))], "XB1"),
        ]
        KV_K, KV_V, INB_Q, INB_M, OUT1A, OUT1B = range(FIRST_FFN + NF, FIRST_FFN + NF + 6)
        arrived, total = [], [0] * RING_MOE
        for i, (pieces, _) in enumerate(LOADS):
            total[i % RING_PRE] += 16 * len(pieces)
            arrived.append((i % RING_PRE, total[i % RING_PRE]))
        slot_fills = [len(range(s_, NF, RING_MOE)) for s_ in range(RING_MOE)]

        def weights(eng, i):
            s_, n = arrived[i]
            eng.wait_ge(sem(f"slot{s_}_loaded"), n)
            return ring[:, s_, :]

        def piece(slot, lo, nc_, n):
            return slot[:, lo:lo + nc_ * n].rearrange("p (c n) -> p c n", c=nc_)

        def released(eng, last):
            if last.startswith("chunk"):
                i = int(last[5:])
                if i < NF - 1:
                    eng.wait_ge(sem("dense_chunks"), i + 1)
                else:
                    filled(eng, "Y3")
            else:
                filled(eng, last)

        def fox_head_done(eng, h):
            if h % 4 == 3:
                filled(eng, f"FO{h // 4}")
            else:
                eng.wait_ge(sem("fox_heads"), 3 * (h // 4) + h % 4 + 1)

        SMALL = 16 * 17
        def overflow(eng, second_pass):
            eng.wait_ge(sem("overflow_known"), 1)
            most = eng.value_load(over[0:1, 0:1], min_val=0, max_val=S)
            with eng.If(most > CAP):
                second_pass()

        block = ctx.enter_context(nc.Block())

        @block.sync
        def _(sp):
            for i, (pieces, _) in enumerate(LOADS):
                if i >= RING_PRE:
                    released(sp, LOADS[i - RING_PRE][1])
                s_ = i % RING_PRE
                for lo, src in pieces:
                    n = src.shape[1] * src.shape[2]
                    dst = ring[:, s_, lo:lo + n].rearrange("p (c n) -> p c n", c=src.shape[1])
                    sp.dma_start(dst, src).then_inc(sem(f"slot{s_}_loaded"), 16)

            def expert_chunk(e, i):
                for lo, wt in ((0, "w_moe_gate"), (2048, "w_moe_up")):
                    src = a[wt][0, bass.ds(e, 1), :, i * FC:(i + 1) * FC].rearrange("a (p c) n -> (a p) c n", c=KC)
                    dst = ring[:, i % RING_MOE, lo:lo + 2048].rearrange("p (c n) -> p c n", c=KC)
                    sp.dma_start(dst, src).then_inc(sem(f"slot{i % RING_MOE}_loaded"), 16)
                src = a["w_moe_down"][0, bass.ds(e, 1), i * FC:(i + 1) * FC, :].rearrange("a (p j) n -> (a p) j n", j=2)
                dst = ring[:, i % RING_MOE, 4096:6144].rearrange("p (j n) -> p j n", j=2)
                sp.dma_start(dst, src).then_inc(sem(f"slot{i % RING_MOE}_loaded"), 16)

            def experts(k):
                def expert(e, first):
                    n = e + k * NE
                    for i in range(NF):
                        if i >= RING_MOE:
                            sp.wait_ge(sem("expert_chunks"), n * (NF - 1) + (i - RING_MOE + 1))
                        elif not first:
                            last = i + RING_MOE if i + RING_MOE < NF else i
                            if last == NF - 1:
                                e_filled(sp, n - 1, "D1")
                            else:
                                sp.wait_ge(sem("expert_chunks"), n * (NF - 1) - (NF - 1) + (last + 1))
                        elif i < RING_PRE:
                            last = max(j for j in range(len(LOADS)) if j % RING_PRE == i)
                            released(sp, LOADS[last][1])
                        elif i == RING_PRE:
                            filled(sp, "FO2")
                            read(sp, "FO2")
                        expert_chunk(e, i)

                if k == 0:
                    expert(0, True)
                    with sp.Fori(1, NE) as e:
                        expert(e, False)
                else:
                    with sp.Fori(0, NE) as e:
                        expert(e, False)

            experts(0)
            overflow(sp, lambda: experts(1))
            for b in range(TB):
                sp.wait_ge(sem("out_ready"), b + 1)
                sp.dma_start(out[0, b * P:(b + 1) * P, :], xs[:, b, :]).then_inc(sem("stored"), 16)
            sp.wait_ge(sem("stored"), 32)

        @block.scalar
        def _(act):
            act.dma_start(x[:, :, :], a["x"].rearrange("a (b p) d -> p (a b) d", p=P)).then_inc(sem("x_loaded"), 16)
            act.dma_start(mixed[:, :, :], a["mem"].rearrange("a (b p) d -> p (a b) d", p=P)).then_inc(sem("mem_loaded"), 16)

            def evacuate(name, outs_ins):
                filled(act, name)
                for o, i, sc in outs_ins:
                    last = nc.scalar.activation(o, i, ACT.Copy, scale=sc)
                last.then_inc(read_sem(name), 1)

            for name, src in (("x", x), ("mem", mixed)):
                act.wait_ge(sem(f"{name}_loaded"), 16)
                for b in range(TB):
                    if name == "mem":
                        act.wait_ge(sem("squares_x"), b + 1)
                    nc.scalar.activation(prod[b], src[:, b, :], ACT.Square,
                                         accum_out=square[name][:, b:b + 1]).then_inc(sem(f"squares_{name}"), 1)

            act.wait_ge(sem("small_loaded"), SMALL)
            def two_chunks(name, dst, gain, i):
                return [(dst[:, 2 * i + j, :], bank(name)[:, 256 * j:256 * j + 256], gains[gain][:, 2 * i + j:2 * i + j + 1])
                        for j in range(2)]
            for i in (0, 2):
                evacuate(f"TX{i}", two_chunks(f"TX{i}", hT, "mix0", i))
            act.wait_ge(sem("gate_abs"), 1)
            nc.scalar.activation(ez, ez, ACT.Exp).then_inc(sem("gate_exp"), 1)
            act.wait_ge(sem("gate_exp"), 1)
            nc.scalar.activation(ez, ez, ACT.Ln, bias=1.0).then_inc(sem("gate_log"), 1)
            for i in range(2):
                evacuate(f"Q{i}", [(qT[0:DK, 512 * i:512 * i + 512], bank(f"Q{i}")[0:DK, :], DK ** -0.5)])
            for i in range(2):
                evacuate(f"K{i}", [(kT[0:DK, 512 * i:512 * i + 512], bank(f"K{i}")[0:DK, :], 1.0)])
            for i in (0, 2):
                evacuate(f"TM{i}", two_chunks(f"TM{i}", mT0, "mem0", i) + two_chunks(f"TM{i}", mT1, "mem1", i))

            def two_heads(name, dst, scale):
                src = bank(name)[:, :].rearrange("p (a s) -> p a s", a=2)
                return [(dst[0:64, j::2, :], src[64 * j:64 * j + 64], scale) for j in range(2)]

            evacuate("MQ", two_heads("MQ", mqT0, MD ** -0.5))
            evacuate("VM0", [(vm0[:, :, :].rearrange("p b n -> p (b n)"), bank("VM0")[:, :], 1.0)])

            def level_exp(n):
                act.wait_ge(sem("decay_diff"), n + 1)
                nc.scalar.activation(decay[0:DK, :], decay[0:DK, :], ACT.Exp).then_inc(sem("decay_exp"), 1)

            def softmax_mem(layer, name, i, first):
                b, j = divmod(i, 2)
                act.wait_ge(sem("mem_max"), first + i + 1)
                pmx, p_ = m_max[layer], (pm0, pm1)[layer]
                for h in range(2):
                    last = nc.scalar.activation(p_[:, b, 2 * j + h, :], bank(name)[:, 256 * h:256 * h + 256], ACT.Exp,
                                                bias=pmx[:, b, 2 * j + h:2 * j + h + 1],
                                                accum_out=m_sum[layer][:, 4 * b + 2 * j + h:4 * b + 2 * j + h + 1])
                last.then_inc(read_sem(name), 1)

            level_exp(0)
            evacuate("V00", [(val[:, 0, 0:384], bank("V00")[:, 0:384], 1.0)])
            level_exp(1)
            evacuate("V10", [(val[:, 1, 0:384], bank("V10")[:, 0:384], 1.0)])
            level_exp(2)
            level_exp(3)
            evacuate("VM1", [(vm1[:, :, :].rearrange("p b n -> p (b n)"), bank("VM1")[:, :], 1.0)])
            level_exp(4)
            softmax_mem(0, "SM0", 0, 0)
            softmax_mem(0, "SM1", 1, 0)
            level_exp(5)
            softmax_mem(0, "SM2", 2, 0)
            softmax_mem(0, "SM3", 3, 0)
            act.wait_ge(sem("decay_diff"), LEVELS + 1)
            nc.scalar.activation(decay[0:DK, :], bT[0:DK, :], ACT.Exp).then_inc(sem("decay_exp"), 1)
            act.wait_ge(sem("key_diff"), 1)
            nc.scalar.activation(bT[0:DK, :], bT[0:DK, :], ACT.Exp).then_inc(sem("key_exp"), 1)
            evacuate("KH0", [(khat[:, 0, :, :].rearrange("p h k -> p (h k)"), bank("KH0")[:, 0:384], 1.0)])
            evacuate("KH1", [(khat[:, 1, :, :].rearrange("p h k -> p (h k)"), bank("KH1")[:, 0:384], 1.0)])
            for b in range(TB):
                for i in range(2):
                    filled(act, f"R{b}{i}")
                    if b + i == 0:
                        read(act, "TM3")
                    nc.scalar.activation(mixed[:, b, 384 * i:384 * i + 384], bank(f"R{b}{i}")[:, 0:384],
                                         ACT.Silu).then_inc(read_sem(f"R{b}{i}"), 1)
            for i in (0, 2):
                evacuate(f"PM{i}", [(pmT0[:, i % 2, i // 2, :, :].rearrange("p h t -> p (h t)"), bank(f"PM{i}")[:, :], 1.0)])
            act.wait_ge(sem("key_prod"), 1)
            for b in range(TB):
                for i in range(2):
                    filled(act, f"O{b}{i}")
                    for h in range(2):
                        n = 4 * b + 2 * i + h
                        nc.scalar.activation(decay[:, 192 * (n % 4):192 * (n % 4) + 192], bank(f"O{b}{i}")[:, 192 * h:192 * h + 192],
                                             ACT.Square, accum_out=o_sq[:, n:n + 1]).then_inc(sem("o_squares"), 1)
                    if b == 0 and i == 1:
                        act.wait_ge(sem("o_squares"), 4)
            for i in (0, 2):
                evacuate(f"TO{i}", two_chunks(f"TO{i}", hT, "onorm", i))
            def x_squares(name, last):
                read(act, last)
                for b in range(TB):
                    nc.scalar.activation(xs[:, b, :], x[:, b, :], ACT.Square,
                                         accum_out=square[name][:, b:b + 1]).then_inc(sem(f"squares_{name}"), 1)
            x_squares("ffn0", "WB1")
            for i in (0, 2):
                evacuate(f"TF{i}", two_chunks(f"TF{i}", hT, "ffn0", i))
            for fc in range(NF):
                for b in range(TB):
                    filled(act, f"G{fc}_{b}")
                    if fc > 0:
                        read(act, f"G{fc - 1}_{b}")
                    nc.scalar.activation(d_sg[:, b, :], bank(f"G{fc}_{b}")[:, 0:FC], ACT.Silu).then_inc(sem("dense_silu"), 1)
                if fc >= 2:
                    act.wait_ge(sem("dense_chunks"), fc - 1)
                evacuate(f"T{fc}", [(d_hT[fc % 2][:, :, :].rearrange("p j t -> p (j t)"), bank(f"T{fc}")[:, :], 1.0)])
            x_squares("kv", "Y3")
            for i in (0, 2):
                evacuate(f"TK{i}", two_chunks(f"TK{i}", hT, "kv", i) + two_chunks(f"TK{i}", hT2, "mix1", i))
            act.wait_ge(sem("forget_abs"), 1)
            nc.scalar.activation(fe, fe, ACT.Exp).then_inc(sem("forget_exp"), 1)
            act.wait_ge(sem("forget_exp"), 1)
            nc.scalar.activation(fe, fe, ACT.Ln, bias=1.0).then_inc(sem("forget_log"), 1)
            for i in range(3):
                evacuate(f"FK{i}", [(fkT[0:64, 4 * i + j:4 * i + j + 3:2, :],
                                     bank(f"FK{i}")[64 * j:64 * j + 64, :].rearrange("p (a s) -> p a s", a=2), 1.0) for j in range(2)])
            filled(act, "CC")
            nc.scalar.activation(negcT[0:FH, :], bank("CC")[0:FH, 0:256], ACT.Copy, scale=-1.0)
            nc.scalar.activation(cT[0:FH, :], bank("CC")[0:FH, 0:256], ACT.Copy).then_inc(read_sem("CC"), 1)
            read(act, "CC")
            act.wait_ge(sem("aug_set"), 2)
            act.dma_start(fkT[64:65, :, :], negcT[0:FH, :]).then_inc(sem("aug_loaded"), 16)
            act.dma_start(fqT[65:66, :, :], cT[0:FH, :]).then_inc(sem("aug_loaded"), 16)
            for b in range(TB):
                evacuate(f"FV{b}0", [(val[:, b, 0:384], bank(f"FV{b}0")[:, 0:384], 1.0)])
            for i in range(3):
                evacuate(f"FQ{i}", [(fqT[0:64, 4 * i + j:4 * i + j + 3:2, :],
                                     bank(f"FQ{i}")[64 * j:64 * j + 64, :].rearrange("p (a s) -> p a s", a=2), FD ** -0.5) for j in range(2)])
            evacuate("MQ1", two_heads("MQ1", mqT1, MD ** -0.5))
            for i in range(4):
                softmax_mem(1, f"N{i}", i, 4)
            act.wait_ge(sem("fox_max"), 1)
            for h in range(FH):
                for b in range(TB):
                    lo, hi = (0, 128) if b == 0 else (128, 384)
                    if h % 4 == 0 and b == 0 and h > 0:
                        act.wait_ge(sem("fox_max"), h // 4 + 1)
                    nc.scalar.activation(logits[:, h, lo:hi], logits[:, h, lo:hi], ACT.Exp, bias=f_max[:, 2 * h + b:2 * h + b + 1],
                                         accum_out=f_sum[:, 2 * h + b:2 * h + b + 1]).then_inc(sem("fox_exp"), 1)
            for i in (0, 2):
                evacuate(f"PN{i}", [(pmT1[:, i % 2, i // 2, :, :].rearrange("p h t -> p (h t)"), bank(f"PN{i}")[:, :], 1.0)])
            for h in range(0, FH, 2):
                if h >= 4:
                    fox_head_done(act, h - 4)
                evacuate(f"PF{h}", [(probT[h % 4], bank(f"PF{h}")[:, 0:384], 1.0)])
            for i in (0, 2):
                evacuate(f"TP{i}", [(hT[:, 2 * i:2 * i + 2, :].rearrange("p c s -> p (c s)"), bank(f"TP{i}")[:, :], 1.0)])
            x_squares("ffn1", "XB1")
            for i in (0, 2):
                evacuate(f"TR{i}", two_chunks(f"TR{i}", hT, "ffn1", i))
            act.wait_ge(sem("logit_diff"), 1)
            nc.scalar.activation(ex[:, :, :], ex[:, :, :], ACT.Exp).then_inc(sem("logit_exp"), 1)

            def experts(k):
                with act.Fori(0, NE) as e:
                    n = e + k * NE
                    e_filled(act, n, "GA0")
                    e_filled_before(act, n, "G10")
                    for c in range(4):
                        last = nc.scalar.activation(hTe[:, c, :], e_bank("GA0")[:, c * CAP:(c + 1) * CAP], ACT.Copy,
                                                    scale=gains["ffn1"][:, c:c + 1])
                    last.then_inc(e_read_sem("GA0"), 1)
                    e_filled(act, n, "ST")
                    e_filled_before(act, n, "SC3")
                    nc.scalar.activation(scat[0:CAP, :, :].rearrange("p b t -> p (b t)"), e_bank("ST")[0:CAP, 0:S],
                                         ACT.Copy).then_inc(e_read_sem("ST"), 1)
                    for fc in range(NF):
                        e_filled(act, n, f"G{fc}")
                        if fc > 0:
                            e_read(act, n, f"G{fc - 1}")
                        else:
                            e_read_before(act, n, f"G{NF - 1}")
                        nc.scalar.activation(e_sg[0:CAP, :], e_bank(f"G{fc}")[0:CAP, 0:FC],
                                             ACT.Silu).then_inc(sem("expert_silu"), 1)
                        e_filled(act, n, f"T{fc}")
                        if fc > 0:
                            act.wait_ge(sem("expert_chunks"), n * (NF - 1) + fc)
                        else:
                            e_filled_before(act, n, "D1")
                        nc.scalar.activation(e_hT[:, :, :].rearrange("p j t -> p (j t)"), e_bank(f"T{fc}")[:, 0:2 * CAP],
                                             ACT.Copy).then_inc(e_read_sem(f"T{fc}"), 1)
                    e_filled(act, n, "D0")
                    e_filled_before(act, n, "SC3")
                    nc.scalar.activation(yE[0:CAP, 0:512], e_bank("D0")[0:CAP, :], ACT.Copy).then_inc(e_read_sem("D0"), 1)

            experts(0)
            overflow(act, lambda: experts(1))
            act.wait_ge(sem("y_done"), 1)
            for b in range(TB):
                nc.scalar.activation(xs[:, b, :], x[:, b, :], ACT.Square,
                                     accum_out=square["final"][:, b:b + 1]).then_inc(sem("squares_final"), 1)

        @block.gpsimd
        def _(pool):
            pool.dma_start(consts[:, :], table).then_inc(sem("table_loaded"), 16)
            per_channel = {"mix0": a["norm_mix"][0], "mix1": a["norm_mix"][1], "mem0": a["norm_mem"][0],
                           "mem1": a["norm_mem"][1], "ffn0": a["norm_ffn"][0], "ffn1": a["norm_ffn"][1], "kv": a["norm_kv"]}
            nc.gpsimd.memset(gains["onorm"], 1.0).then_inc(sem("onorm_set"), 1)
            pool.wait_ge(sem("onorm_set"), 1)
            loads = [(gains[n], row.rearrange("(p c) -> p c", c=KC)) for n, row in per_channel.items()]
            rows = DV // KC
            loads += [(gains["onorm"][rows * h:rows * (h + 1), :], a["gla_onorm"][0].rearrange("(p c) -> p c", c=KC))
                      for h in range(GH)]
            loads += [(w2[0:RANK, :], a["w_gla_gate2"][0]), (w2[RANK:RANK + 1, :], a["b_gla_gate2"]),
                      (wf, cols(a["w_kv"], 1536, 1548)), (wr, cols(a["w_router"][0], 0, NE)),
                      (bf, a["b_forget"].rearrange("(a n) -> a n", a=1).partition_broadcast(P)),
                      (final_row, a["norm_final"].rearrange("(a n) -> a n", a=1).partition_broadcast(P))]
            assert 16 * len(loads) == SMALL
            for dst, src in loads:
                pool.dma_start(dst, src).then_inc(sem("small_loaded"), 16)
            pool.wait_ge(sem("table_loaded"), 16)
            half = const("mhalf")
            for name in ("x", "mem", "gla", "ffn0", "kv", "ffn1", "final"):
                pool.wait_ge(sem(f"mean_{name}"), 1)
                dst, src = (o_rstd, o_mean) if name == "gla" else (rstd[name], mean[name])
                nc.gpsimd.tensor_tensor(dst, src, half[:, 0:dst.shape[1]], ALU.pow).then_inc(sem(f"rstd_{name}"), 1)

        @block.vector
        def _(dve):
            order = [0]

            def link(ins):
                order[0] += 1
                ins.then_inc(sem("dve_order"), 1)
                dve.wait_ge(sem("dve_order"), order[0])

            def evacuate(name, outs_ins):
                filled(dve, name)
                for o, i, sc in outs_ins:
                    last = nc.vector.tensor_copy(o, i) if sc is None else nc.vector.tensor_scalar(o, i, sc, None, ALU.mult)
                last.then_inc(read_sem(name), 1)

            def normed(name, src, dst, key):
                dve.wait_ge(sem(f"squares_{name}"), 2)
                nc.vector.tensor_scalar(mean[name], square[name], 1.0 / D, EPS, ALU.mult, ALU.add).then_inc(sem(f"mean_{name}"), 1)
                dve.wait_ge(sem(f"rstd_{name}"), 1)
                for b in range(TB):
                    nc.vector.tensor_scalar(dst[:, b, :], src[:, b, :], rstd[name][:, b:b + 1], None,
                                            ALU.mult).then_inc(sem(key), 1)

            nc.vector.memset(glrT[0:RANK + 1, :], 1.0)
            nc.vector.memset(pos[:, :, :], -1.0)
            nc.vector.memset(gate[:, :, :], 0.0)
            normed("x", x, xs, "xs_ready")
            dve.wait_ge(sem("small_loaded"), SMALL)

            def two_chunks(name, dst, gain, i):
                return [(dst[:, 2 * i + j, :], bank(name)[:, 256 * j:256 * j + 256], gains[gain][:, 2 * i + j:2 * i + j + 1])
                        for j in range(2)]

            def two_heads(name, dst):
                src = bank(name)[:, :].rearrange("p (a s) -> p a s", a=2)
                return [(dst[0:64, j::2, :], src[64 * j:64 * j + 64], None) for j in range(2)]

            for i in (1, 3):
                evacuate(f"TX{i}", two_chunks(f"TX{i}", hT, "mix0", i))
            normed("mem", mixed, mixed, "mem_ready")
            evacuate("GLR", [(glrT[0:RANK, :], bank("GLR")[0:RANK, 0:256], None)])
            for b in range(TB):
                evacuate(f"Z{b}", [(zz[:, 384 * b:384 * b + 384], bank(f"Z{b}")[:, 0:384], None)])
            read(dve, "Z1")
            nc.vector.scalar_tensor_tensor(ez, zz, -1.0, zz, ALU.mult, ALU.min).then_inc(sem("gate_abs"), 1)
            link(nc.vector.tensor_scalar(la, zz, 0.0, None, ALU.min))
            for i in (1, 3):
                evacuate(f"TM{i}", two_chunks(f"TM{i}", mT0, "mem0", i) + two_chunks(f"TM{i}", mT1, "mem1", i))
            dve.wait_ge(sem("gate_log"), 1)
            nc.vector.tensor_tensor(la, la, ez, ALU.subtract).then_inc(sem("log_gates"), 1)
            for i in range(2):
                evacuate(f"B{i}", [(bT[0:DK, 512 * i:512 * i + 512], bank(f"B{i}")[0:DK, :], None)])
            read(dve, "B1")

            def halves(tile, half):
                return tile[0:DK, :].rearrange("k (n two t) -> k n two t", two=2, t=half)

            def level_diff(n):
                half = CHUNK // 2 >> n
                bh, dh = halves(bT, half), halves(decay, half)
                mid = bh[:, :, 1, 0:1].to_broadcast([DK, S * GH // (2 * half), half])
                nc.vector.tensor_tensor(dh[:, :, 1, :], bh[:, :, 1, :], mid, ALU.subtract)
                nc.vector.tensor_tensor(dh[:, :, 0, :], mid, bh[:, :, 0, :], ALU.subtract).then_inc(sem("decay_diff"), 1)

            def level_prod(n):
                half = CHUNK // 2 >> n
                dh, ph = halves(decay, half), halves(prod[n % 2], half)
                dve.wait_ge(sem("decay_exp"), n + 1)
                if n == 0:
                    read(dve, "Q1"), read(dve, "K1")
                if n >= 2:
                    filled(dve, f"L{n - 2}_1")
                nc.vector.tensor_tensor(ph[:, :, 1, :], dh[:, :, 1, :], halves(qT, half)[:, :, 1, :], ALU.mult)
                nc.vector.tensor_tensor(ph[:, :, 0, :], dh[:, :, 0, :], halves(kT, half)[:, :, 0, :],
                                        ALU.mult).then_inc(sem("level_ready"), 1)
                dve.wait_ge(sem("level_ready"), n + 1)

            def level_mask(n):
                for b in range(TB):
                    filled(dve, f"L{n}_{b}")
                    src = bank(f"L{n}_{b}")[:, :].rearrange("s (h t) -> s h t", h=GH)
                    keep = ident if n == LEVELS else const("levels")[:, n * P:(n + 1) * P]
                    keep = keep.unsqueeze(1)
                    if n == 0:
                        ins = nc.vector.tensor_tensor(scoreT[:, b], src, keep.to_broadcast([P, GH, P]), ALU.mult)
                    else:
                        ins = nc.vector.copy_predicated(scoreT[:, b], keep.bitcast(U32).to_broadcast([P, GH, P]), src)
                    ins.then_inc(read_sem(f"L{n}_{b}"), 1)
                    read(dve, f"L{n}_{b}")

            def mem_max(layer, name, i):
                b, j = divmod(i, 2)
                filled(dve, name)
                part = m_max[layer][:, b, 2 * j:2 * j + 2]
                link(nc.vector.reduce_max(part, bank(name)[:, :].rearrange("p (h m) -> p h m", h=2), AX))
                nc.vector.tensor_scalar(part, part, -1.0, None, ALU.mult).then_inc(sem("mem_max"), 1)

            level_diff(0)
            evacuate("KM0", two_heads("KM0", kmT0))
            level_prod(0)
            level_diff(1)
            level_mask(0)
            evacuate("V01", [(val[:, 0, 384:768], bank("V01")[:, 0:384], None)])
            level_prod(1)
            level_diff(2)
            level_mask(1)
            evacuate("V11", [(val[:, 1, 384:768], bank("V11")[:, 0:384], None)])
            level_prod(2)
            level_diff(3)
            level_mask(2)
            level_prod(3)
            evacuate("KM1", two_heads("KM1", kmT1))
            level_diff(4)
            level_mask(3)
            level_prod(4)
            level_diff(5)
            level_mask(4)
            mem_max(0, "SM0", 0)
            mem_max(0, "SM1", 1)
            level_prod(5)
            nc.vector.tensor_copy(blast[0:DK, :], bT[0:DK, CHUNK - 1::CHUNK]).then_inc(sem("decay_diff"), 1)
            level_mask(5)
            mem_max(0, "SM2", 2)
            mem_max(0, "SM3", 3)
            level_mask(6)
            dve.wait_ge(sem("decay_exp"), LEVELS + 1)
            by_chunk = [P_.rearrange("k (n t) -> k n t", t=CHUNK) for P_ in (bT[0:DK, :],)][0]
            nc.vector.tensor_tensor(by_chunk, blast[0:DK, :].unsqueeze(2).to_broadcast([DK, S * GH // CHUNK, CHUNK]),
                                    by_chunk, ALU.subtract).then_inc(sem("key_diff"), 1)
            nc.vector.tensor_copy(alast[0:DK, :], decay[0:DK, CHUNK - 1::CHUNK])
            filled(dve, "L4_1")
            nc.vector.tensor_tensor(prod[0][0:DK, :], decay[0:DK, :], qT[0:DK, :], ALU.mult).then_inc(sem("query_prod"), 1)
            dve.wait_ge(sem("key_exp"), 1)
            filled(dve, "L5_1")
            nc.vector.tensor_tensor(prod[1][0:DK, :], bT[0:DK, :], kT[0:DK, :], ALU.mult).then_inc(sem("key_prod"), 1)
            for c in range(3):
                for i in range(2):
                    name = f"U{c}_{i}"
                    filled(dve, name)
                    if c == 0:
                        ins = nc.vector.tensor_copy(state[0:DK, 0, 2 * i:2 * i + 2, :].rearrange("k h v -> k (h v)"),
                                                    bank(name)[0:DK, 0:384])
                        if i == 0:
                            dve.wait_ge(sem("key_prod"), 1)
                    else:
                        for j in range(2):
                            h = 2 * i + j
                            ins = nc.vector.scalar_tensor_tensor(
                                state[0:DK, c, h, :], state[0:DK, c - 1, h, :], alast[0:DK, 4 * h + c:4 * h + c + 1],
                                bank(name)[0:DK, 192 * j:192 * j + 192], ALU.mult, ALU.add)
                    ins.then_inc(read_sem(name), 1)
                read(dve, f"U{c}_1")

            def memory_values(layer, name, scores):
                read(dve, scores)
                link(nc.vector.reciprocal(m_inv[layer], m_sum[layer]))
                filled(dve, name)
                inv = m_inv[layer].rearrange("p (b h) -> p b h", b=TB)
                for b in range(TB):
                    last = nc.vector.tensor_tensor(
                        mixed[:, b, MAIN:D].rearrange("p (h n) -> p h n", h=MH),
                        bank(name)[:, 256 * b:256 * b + 256].rearrange("p (h n) -> p h n", h=MH),
                        inv[:, b, :].unsqueeze(2).to_broadcast([P, MH, MD]), ALU.mult)
                last.then_inc(read_sem(name), 1)

            for i in (1, 3):
                evacuate(f"PM{i}", [(pmT0[:, i % 2, i // 2, :, :].rearrange("p h t -> p (h t)"), bank(f"PM{i}")[:, :], None)])
            memory_values(0, "MV", "SM3")
            dve.wait_ge(sem("o_squares"), 8)
            nc.vector.tensor_scalar(o_mean, o_sq, 1.0 / DV, EPS, ALU.mult, ALU.add).then_inc(sem("mean_gla"), 1)
            dve.wait_ge(sem("rstd_gla"), 1)
            read(dve, "R11")
            for b in range(TB):
                for i in range(2):
                    for h in (2 * i, 2 * i + 1):
                        part = mixed[:, b, DV * h:DV * (h + 1)]
                        last = nc.vector.scalar_tensor_tensor(part, bank(f"O{b}{i}")[:, DV * (h % 2):DV * (h % 2) + DV],
                                                              o_rstd[:, 4 * b + h:4 * b + h + 1], part, ALU.mult, ALU.mult)
                    last.then_inc(read_sem(f"O{b}{i}"), 1)
            for i in (1, 3):
                evacuate(f"TO{i}", two_chunks(f"TO{i}", hT, "onorm", i))

            def add_to_stream(name, b, half):
                filled(dve, name)
                part = x[:, b, 512 * half:512 * half + 512]
                nc.vector.tensor_tensor(part, part, bank(name)[:, :], ALU.add).then_inc(read_sem(name), 1)

            for n_, half in (("WA", 0), ("WB", 1)):
                for b in range(TB):
                    add_to_stream(f"{n_}{b}", b, half)
            read(dve, "WB1")
            normed("ffn0", x, xs, "ffn0_ready")
            for i in (1, 3):
                evacuate(f"TF{i}", two_chunks(f"TF{i}", hT, "ffn0", i))
            for fc in range(NF):
                if fc > 0:
                    filled(dve, f"T{fc - 1}")
                for b in range(TB):
                    dve.wait_ge(sem("dense_silu"), TB * fc + b + 1)
                    nc.vector.tensor_tensor(d_h[:, b, :], d_sg[:, b, :], bank(f"G{fc}_{b}")[:, FC:2 * FC],
                                            ALU.mult).then_inc(read_sem(f"G{fc}_{b}"), 1)
            for b in range(TB):
                for half in range(2):
                    add_to_stream(f"Y{2 * b + half}", b, half)
            read(dve, "Y3")
            normed("kv", x, xs, "kv_ready")
            for t_ in (fqT, fkT):
                nc.vector.memset(t_[64:66, :, :], 1.0).then_inc(sem("aug_set"), 1)
            for i in (1, 3):
                evacuate(f"TK{i}", two_chunks(f"TK{i}", hT, "kv", i) + two_chunks(f"TK{i}", hT2, "mix1", i))
            filled(dve, "FG")
            fzb = fz.rearrange("p (b h) -> p b h", b=TB)
            nc.vector.tensor_tensor(fzb, bank("FG")[:, 0:24].rearrange("p (b h) -> p b h", b=TB),
                                    bf.unsqueeze(1).to_broadcast([P, TB, FH]), ALU.add).then_inc(read_sem("FG"), 1)
            read(dve, "FG")
            nc.vector.scalar_tensor_tensor(fe, fz, -1.0, fz, ALU.mult, ALU.min).then_inc(sem("forget_abs"), 1)
            flat = fl.rearrange("p b h -> p (b h)")
            link(nc.vector.tensor_scalar(flat, fz, 0.0, None, ALU.min))
            dve.wait_ge(sem("forget_log"), 1)
            nc.vector.tensor_tensor(flat, flat, fe, ALU.subtract).then_inc(sem("log_forget"), 1)
            for b in range(TB):
                evacuate(f"FV{b}1", [(val[:, b, 384:768], bank(f"FV{b}1")[:, 0:384], None)])
            for i in range(4):
                mem_max(1, f"N{i}", i)
            fm = f_max.rearrange("p (h b) -> p h b", b=TB)
            for h in range(FH):
                filled(dve, f"S{h}")
                nc.vector.tensor_tensor(logits[:, h, :], bank(f"S{h}")[:, 0:384], const("causal"),
                                        ALU.add).then_inc(read_sem(f"S{h}"), 1)
                if h % 4 == 3:
                    read(dve, f"S{h}")
                    g_ = slice(h - 3, h + 1)
                    nc.vector.reduce_max(fm[:, g_, 0], logits[:, g_, 0:128], AX)
                    link(nc.vector.reduce_max(fm[:, g_, 1], logits[:, g_, 128:384], AX))
                    part = f_max[:, 2 * (h - 3):2 * (h + 1)]
                    nc.vector.tensor_scalar(part, part, -1.0, None, ALU.mult).then_inc(sem("fox_max"), 1)
            for i in (1, 3):
                evacuate(f"PN{i}", [(pmT1[:, i % 2, i // 2, :, :].rearrange("p h t -> p (h t)"), bank(f"PN{i}")[:, :], None)])
            memory_values(1, "MW", "N3")
            fi = f_inv.rearrange("p (h b) -> p b h", b=TB)

            def fox_values(g_):
                filled(dve, f"FO{g_}")
                for b in range(TB):
                    last = nc.vector.tensor_tensor(
                        mixed[:, b, 256 * g_:256 * g_ + 256].rearrange("p (h n) -> p h n", h=4),
                        bank(f"FO{g_}")[:, 256 * b:256 * b + 256].rearrange("p (h n) -> p h n", h=4),
                        fi[:, b, 4 * g_:4 * g_ + 4].unsqueeze(2).to_broadcast([P, 4, FD]), ALU.mult)
                last.then_inc(read_sem(f"FO{g_}"), 1)

            for h in range(1, FH, 2):
                if h >= 4:
                    fox_head_done(dve, h - 4)
                evacuate(f"PF{h}", [(probT[h % 4], bank(f"PF{h}")[:, 0:384], None)])
                if h == 5:
                    dve.wait_ge(sem("fox_exp"), 2 * FH)
                    link(nc.vector.reciprocal(f_inv, f_sum))
                if h >= 5 and (h - 5) % 4 == 0:
                    fox_values((h - 5) // 4)
            fox_values(2)
            for i in (1, 3):
                evacuate(f"TP{i}", [(hT[:, 2 * i:2 * i + 2, :].rearrange("p c s -> p (c s)"), bank(f"TP{i}")[:, :], None)])
            for n_, half in (("XA", 0), ("XB", 1)):
                for b in range(TB):
                    add_to_stream(f"{n_}{b}", b, half)
            read(dve, "XB1")
            normed("ffn1", x, xs, "ffn1_ready")
            for i in (1, 3):
                evacuate(f"TR{i}", two_chunks(f"TR{i}", hT, "ffn1", i))
            filled(dve, "RL")
            nc.vector.tensor_copy(lg[:, :, :].rearrange("p b e -> p (b e)"), bank("RL")[:, 0:16]).then_inc(read_sem("RL"), 1)
            read(dve, "RL")
            link(nc.vector.reduce_max(top, lg[:, :, :], AX))
            for b in range(TB):
                last = nc.vector.tensor_scalar(ex[:, b, :], lg[:, b, :], top[:, b:b + 1], None, ALU.subtract)
            last.then_inc(sem("logit_diff"), 1)
            for b in range(TB):
                mine = lg[:, b, :].unsqueeze(2).to_broadcast([P, NE, NE])
                other = lg[:, b, :].unsqueeze(1).to_broadcast([P, NE, NE])
                nc.vector.tensor_tensor(gt, other, mine, ALU.is_gt)
                link(nc.vector.tensor_tensor(eq, other, mine, ALU.is_equal))
                link(nc.vector.tensor_tensor(eq, eq, const("earlier").rearrange("p (e o) -> p e o", e=NE), ALU.mult))
                link(nc.vector.tensor_tensor(gt, gt, eq, ALU.add))
                link(nc.vector.reduce_sum(rank, gt, AX))
                ins = nc.vector.tensor_scalar(sel[:, b, :], rank, 1.5, None, ALU.is_lt)
                ins.then_inc(sem("chosen"), 1)
                dve.wait_ge(sem("chosen"), b + 1)
            dve.wait_ge(sem("logit_exp"), 1)
            link(nc.vector.tensor_tensor(ex[:, :, :], ex[:, :, :], sel[:, :, :], ALU.mult))
            link(nc.vector.reduce_sum(den, ex[:, :, :], AX))
            link(nc.vector.reciprocal(rden, den))
            nc.vector.tensor_tensor(gate[:, :, 0:NE], ex[:, :, :], rden.unsqueeze(2).to_broadcast([P, TB, NE]), ALU.mult)
            filled(dve, "POS")
            nc.vector.tensor_tensor(pos[:, :, 0:NE], bank("POS")[:, 0:16].rearrange("p (b e) -> p b e", b=TB), sel[:, :, :],
                                    ALU.mult).then_inc(read_sem("POS"), 1)
            read(dve, "POS")
            link(nc.vector.tensor_scalar(pos[:, :, 0:NE], pos[:, :, 0:NE], -1.0, None, ALU.add))
            filled(dve, "CNT")
            nc.vector.reduce_max(counts[0:1, 0:1], bank("CNT")[0:1, 0:8], AX).then_inc(read_sem("CNT"), 1)
            read(dve, "CNT")
            nc.vector.tensor_copy(over[0:1, 0:1], counts[0:1, 0:1]).then_inc(sem("overflow_known"), 1)

            def build(e, k):
                slots = const("slots")[:, CAP * k:CAP * (k + 1)]
                for b in range(TB):
                    at_e = pos[:, b, bass.ds(e, 1)]
                    nc.vector.tensor_scalar(perm[:, b, :], slots, at_e, None, ALU.is_equal)
                    last = nc.vector.tensor_scalar(wperm[:, b, :], slots, at_e, gate[:, b, bass.ds(e, 1)],
                                                   ALU.is_equal, ALU.mult)
                last.then_inc(sem("perm_built"), 1)

            def experts(k):
                build(0, k)
                with dve.Fori(0, NE) as e:
                    n = e + k * NE
                    e_filled(dve, n, "GA1")
                    for c in range(4, KC):
                        last = nc.vector.tensor_scalar(hTe[:, c, :], e_bank("GA1")[:, (c - 4) * CAP:(c - 3) * CAP],
                                                       gains["ffn1"][:, c:c + 1], None, ALU.mult)
                    last.then_inc(e_read_sem("GA1"), 1)
                    for fc in range(NF):
                        dve.wait_ge(sem("expert_silu"), n * NF + (fc + 1))
                        if fc > 0:
                            e_filled(dve, n, f"T{fc - 1}")
                        nc.vector.tensor_tensor(e_h[0:CAP, :], e_sg[0:CAP, :], e_bank(f"G{fc}")[0:CAP, FC:2 * FC],
                                                ALU.mult).then_inc(e_read_sem(f"G{fc}"), 1)
                        if fc == 1:
                            e_filled(dve, n, "ST")
                            build(e + 1, k)
                    e_filled(dve, n, "D1")
                    nc.vector.tensor_copy(yE[0:CAP, 512:1024], e_bank("D1")[0:CAP, :]).then_inc(e_read_sem("D1"), 1)
                    for q in range(4):
                        b, half = divmod(q, 2)
                        e_filled(dve, n, f"SC{q}")
                        part = x[:, b, 512 * half:512 * half + 512]
                        nc.vector.tensor_tensor(part, part, e_bank(f"SC{q}")[:, :], ALU.add).then_inc(e_read_sem(f"SC{q}"), 1)
                    e_read(dve, n, "SC3")

            experts(0)
            overflow(dve, lambda: experts(1))
            nc.vector.memset(counts[0:1, 8:16], 0.0).then_inc(sem("y_done"), 1)
            dve.wait_ge(sem("squares_final"), 2)
            nc.vector.tensor_scalar(mean["final"], square["final"], 1.0 / D, EPS, ALU.mult, ALU.add).then_inc(sem("mean_final"), 1)
            dve.wait_ge(sem("rstd_final"), 1)
            for b in range(TB):
                nc.vector.scalar_tensor_tensor(xs[:, b, :], x[:, b, :], rstd["final"][:, b:b + 1], final_row,
                                               ALU.mult, ALU.mult).then_inc(sem("out_ready"), 1)

        @block.tensor
        def _(pe):
            mm = nc.tensor.matmul

            def by_chunk(tile, b, c):
                return tile[:, b, :].rearrange("t (p c) -> t c p", c=KC)[:, c, :]

            def tok(b):
                return slice(b * P, (b + 1) * P)

            def transposes(prefix, src):
                for i in range(4):
                    name = f"{prefix}{i}"
                    free(pe, name)
                    for j in range(2):
                        for b in range(TB):
                            last = nc.tensor.transpose(bank(name)[:, (2 * j + b) * P:(2 * j + b + 1) * P],
                                                       by_chunk(src, b, 2 * i + j), ident)
                    last.then_inc(full_sem(name), 1)

            def project(name, groups):
                free(pe, name)
                for o, lhs, rhs in groups:
                    for c in range(KC):
                        last = mm(o, lhs(c), rhs(c), start=(c == 0), stop=(c == KC - 1))
                last.then_inc(full_sem(name), 1)

            def tokens_by(name, b, src, wt, lo, n, at_=0):
                project(name, [(bank(name)[:, at_:at_ + n], lambda c: src[:, c, tok(b)], lambda c: wt[:, c, lo:lo + n])])

            def columns_by(name, src, wt, los, n):
                project(name, [(bank(name)[0:n, 256 * j:256 * j + 256], lambda c, lo=lo: wt[:, c, lo:lo + n],
                                lambda c: src[:, c, :]) for j, lo in enumerate(los)])

            pe.wait_ge(sem("table_loaded"), 16)
            pe.wait_ge(sem("xs_ready"), 2)
            transposes("TX", xs)
            for i in range(4):
                read(pe, f"TX{i}")
            wgm = piece(weights(pe, 0), 0, KC, 272)
            columns_by("GLR", hT, wgm, [0], RANK)
            pe.wait_ge(sem("small_loaded"), SMALL)
            read(pe, "GLR")
            for b in range(TB):
                free(pe, f"Z{b}")
                mm(bank(f"Z{b}")[:, 0:384], glrT[0:RANK + 1, tok(b)], w2[0:RANK + 1, :], start=True,
                   stop=True).then_inc(full_sem(f"Z{b}"), 1)
            wqk = piece(weights(pe, 1), 0, KC, 768)
            for i in range(2):
                columns_by(f"Q{i}", hT, wqk, [DK * 2 * i, DK * (2 * i + 1)], DK)
            for i in range(2):
                columns_by(f"K{i}", hT, wqk, [384 + DK * 2 * i, 384 + DK * (2 * i + 1)], DK)
            pe.wait_ge(sem("mem_ready"), 2)
            transposes("TM", mixed)
            pe.wait_ge(sem("log_gates"), 1)
            for i in range(2):
                free(pe, f"B{i}")
                for j in range(2):
                    for b in range(TB):
                        lo = DK * (2 * i + j)
                        last = mm(bank(f"B{i}")[0:DK, 256 * j + P * b:256 * j + P * b + P], la_v[:, b, lo:lo + DK],
                                  const("tri16"), start=True, stop=True)
                last.then_inc(full_sem(f"B{i}"), 1)
            columns_by("MQ", hT, wgm, [16, 144], P)
            for i in range(4):
                read(pe, f"TM{i}")
            wkv = piece(weights(pe, 2), 0, KC, 512)
            columns_by("KM0", mT0, wkv, [0, P], P)

            def memory_values_of(name, src, wt):
                project(name, [(bank(name)[:, 256 * b:256 * b + 256], lambda c, b=b: src[:, c, tok(b)],
                                lambda c: wt[:, c, 256:512]) for b in range(TB)])

            memory_values_of("VM0", mT0, wkv)

            def level(n):
                if n < LEVELS:
                    pe.wait_ge(sem("level_ready"), n + 1)
                for b in range(TB):
                    free(pe, f"L{n}_{b}")
                    for h in range(GH):
                        at_ = slice(S * h + P * b, S * h + P * b + P)
                        lhs, rhs = (kT, qT) if n == LEVELS else (prod[n % 2], prod[n % 2])
                        last = mm(bank(f"L{n}_{b}")[:, P * h:P * h + P], lhs[0:DK, at_], rhs[0:DK, at_], start=True, stop=True)
                    last.then_inc(full_sem(f"L{n}_{b}"), 1)

            def memory_scores(name, i, q, k_):
                b, j = divmod(i, 2)
                free(pe, name)
                for h in range(2):
                    last = mm(bank(name)[:, 256 * h:256 * h + 256], q[0:64, 2 * j + h, tok(b)], k_[0:64, 2 * j + h, :],
                              start=True, stop=True)
                last.then_inc(full_sem(name), 1)

            level(0)
            wv = piece(weights(pe, 3), 0, KC, 768)
            for b in range(TB):
                for i in range(2):
                    tokens_by(f"V{b}{i}", b, hT, wv, 384 * i, 384)
                level(b + 1)
            wkv1 = piece(weights(pe, 4), 0, KC, 512)
            columns_by("KM1", mT1, wkv1, [0, P], P)
            level(3)
            memory_values_of("VM1", mT1, wkv1)
            level(4)
            read(pe, "MQ"), read(pe, "KM0")
            memory_scores("SM0", 0, mqT0, kmT0)
            memory_scores("SM1", 1, mqT0, kmT0)
            level(5)
            memory_scores("SM2", 2, mqT0, kmT0)
            memory_scores("SM3", 3, mqT0, kmT0)
            level(6)
            pe.wait_ge(sem("key_prod"), 1)
            for b in range(TB):
                free(pe, f"KH{b}")
                for h in range(GH):
                    last = nc.tensor.transpose(bank(f"KH{b}")[:, DK * h:DK * h + DK], prod[1][0:DK, S * h + P * b:S * h + P * b + P],
                                               ident[0:DK, 0:DK])
                last.then_inc(full_sem(f"KH{b}"), 1)
            wr_ = piece(weights(pe, 5), 0, KC, 768)
            for b in range(TB):
                for i in range(2):
                    tokens_by(f"R{b}{i}", b, hT, wr_, 384 * i, 384)
            read(pe, "KH0"), read(pe, "KH1")
            for b in range(TB):
                read(pe, f"V{b}0"), read(pe, f"V{b}1")
            for c in range(3):
                b, r = c // 2, slice(64 * (c % 2), 64 * (c % 2) + 64)
                for i in range(2):
                    free(pe, f"U{c}_{i}")
                    for j in range(2):
                        h = 2 * i + j
                        last = mm(bank(f"U{c}_{i}")[0:DK, DV * j:DV * j + DV], khat[r, b, h, :], val[r, b, DV * h:DV * (h + 1)],
                                  start=True, stop=True)
                    last.then_inc(full_sem(f"U{c}_{i}"), 1)

            def memory_transposes(prefix, probs):
                for i in range(4):
                    b, mc = divmod(i, 2)
                    name = f"{prefix}{i}"
                    free(pe, name)
                    for h in range(MH):
                        last = nc.tensor.transpose(bank(name)[:, P * h:P * h + P], probs[:, b, h, P * mc:P * mc + P], ident)
                    last.then_inc(full_sem(name), 1)

            def memory_outputs(name, prefix, probsT, vm):
                for i in range(4):
                    read(pe, f"{prefix}{i}")
                free(pe, name)
                for b in range(TB):
                    for h in range(MH):
                        for mc in range(2):
                            last = mm(bank(name)[:, 256 * b + MD * h:256 * b + MD * h + MD], probsT[:, mc, b, h, :],
                                      vm[:, mc, MD * h:MD * h + MD], start=(mc == 0), stop=(mc == 1))
                last.then_inc(full_sem(name), 1)

            for i in range(4):
                read(pe, f"SM{i}")
            memory_transposes("PM", pm0)
            memory_outputs("MV", "PM", pmT0, vm0)
            read(pe, "L6_1"), read(pe, "U2_1")
            for b in range(TB):
                for i in range(2):
                    free(pe, f"O{b}{i}")
                    for j in range(2):
                        h = 2 * i + j
                        for c in (2 * b, 2 * b + 1):
                            r = slice(64 * (c % 2), 64 * (c % 2) + 64)
                            o = bank(f"O{b}{i}")[r, DV * j:DV * j + DV]
                            last = mm(o, scoreT[:, b, h, r], val[:, b, DV * h:DV * (h + 1)], start=True, stop=(c == 0))
                            if c > 0:
                                last = mm(o, prod[0][0:DK, S * h + CHUNK * c:S * h + CHUNK * (c + 1)],
                                          state[0:DK, c - 1, h, :], start=False, stop=True)
                    last.then_inc(full_sem(f"O{b}{i}"), 1)

            def output_projection(prefix, load):
                for half, n_ in enumerate("AB"):
                    wt = piece(weights(pe, load + half), 0, KC, 512)
                    for b in range(TB):
                        tokens_by(f"{prefix}{n_}{b}", b, hT, wt, 0, 512)

            read(pe, "O11"), read(pe, "MV")
            transposes("TO", mixed)
            for i in range(4):
                read(pe, f"TO{i}")
            output_projection("W", 6)
            pe.wait_ge(sem("ffn0_ready"), 2)
            transposes("TF", xs)
            for i in range(4):
                read(pe, f"TF{i}")

            def dense_up(fc):
                wt = weights(pe, FIRST_FFN + fc)[:, 0:4096].rearrange("p (a c n) -> p c a n", a=2, c=KC)
                for b in range(TB):
                    name = f"G{fc}_{b}"
                    project(name, [(bank(name)[:, :].rearrange("p (a n) -> p a n", a=2), lambda c, b=b: hT[:, c, tok(b)],
                                    lambda c: wt[:, c])])

            dense_up(0)
            for fc in range(NF):
                if fc < NF - 1:
                    dense_up(fc + 1)
                read(pe, f"G{fc}_0"), read(pe, f"G{fc}_1")
                free(pe, f"T{fc}")
                for j in range(2):
                    for b in range(TB):
                        last = nc.tensor.transpose(bank(f"T{fc}")[:, (2 * j + b) * P:(2 * j + b + 1) * P], d_h[:, b, j::2], ident)
                last.then_inc(full_sem(f"T{fc}"), 1)
                read(pe, f"T{fc}")
                wd = piece(ring[:, arrived[FIRST_FFN + fc][0], :], 4096, 2, D)
                for b in range(TB):
                    for half in range(2):
                        if fc == 0:
                            free(pe, f"Y{2 * b + half}")
                        for j in range(2):
                            last = mm(bank(f"Y{2 * b + half}")[:, :], d_hT[fc % 2][:, j, tok(b)], wd[:, j, 512 * half:512 * half + 512],
                                      start=(fc == 0 and j == 0), stop=(fc == NF - 1 and j == 1))
                        if fc == NF - 1:
                            last.then_inc(full_sem(f"Y{2 * b + half}"), 1)
                if fc < NF - 1:
                    last.then_inc(sem("dense_chunks"), 1)

            pe.wait_ge(sem("kv_ready"), 2)
            transposes("TK", xs)
            for i in range(4):
                read(pe, f"TK{i}")
            project("FG", [(bank("FG")[:, FH * b:FH * b + FH], lambda c, b=b: hT[:, c, tok(b)], lambda c: wf[:, c, :])
                           for b in range(TB)])
            wt = piece(weights(pe, KV_K), 0, KC, 768)
            for i in range(3):
                columns_by(f"FK{i}", hT, wt, [P * 2 * i, P * (2 * i + 1)], P)
            pe.wait_ge(sem("log_forget"), 1)
            free(pe, "CC")
            mm(bank("CC")[0:FH, 0:P], fl[:, 0, :], const("tri"), start=True, stop=True)
            mm(bank("CC")[0:FH, P:2 * P], fl[:, 0, :], const("ones"), start=True, stop=False)
            mm(bank("CC")[0:FH, P:2 * P], fl[:, 1, :], const("tri"), start=False, stop=True).then_inc(full_sem("CC"), 1)
            wt = piece(weights(pe, KV_V), 0, KC, 768)
            for b in range(TB):
                for i in range(2):
                    tokens_by(f"FV{b}{i}", b, hT, wt, 384 * i, 384)
            wt = piece(weights(pe, INB_Q), 0, KC, 768)
            for i in range(3):
                columns_by(f"FQ{i}", hT2, wt, [P * 2 * i, P * (2 * i + 1)], P)
            columns_by("MQ1", hT2, piece(weights(pe, INB_M), 0, KC, 256), [0, P], P)
            read(pe, "MQ1"), read(pe, "KM1"), read(pe, "VM1")
            for i in range(4):
                memory_scores(f"N{i}", i, mqT1, kmT1)
            pe.wait_ge(sem("aug_loaded"), 32)
            read(pe, "FQ2"), read(pe, "FK2")
            for h in range(FH):
                name = f"S{h}"
                free(pe, name)
                mm(bank(name)[:, 0:P], fqT[0:66, h, 0:P], fkT[0:66, h, 0:P], start=True, stop=True)
                mm(bank(name)[:, P:3 * P], fqT[0:66, h, P:S], fkT[0:66, h, :], start=True, stop=True).then_inc(full_sem(name), 1)
            for i in range(4):
                read(pe, f"N{i}")
            memory_transposes("PN", pm1)
            memory_outputs("MW", "PN", pmT1, vm1)

            def fox_output(h):
                read(pe, f"PF{h}")
                g_, hh = divmod(h, 4)
                if hh == 0:
                    free(pe, f"FO{g_}")
                vh = [val[:, b, FD * h:FD * h + FD] for b in range(TB)]
                mm(bank(f"FO{g_}")[:, FD * hh:FD * hh + FD], probT[hh][:, 0:P], vh[0], start=True, stop=True)
                o = bank(f"FO{g_}")[:, 256 + FD * hh:256 + FD * hh + FD]
                mm(o, probT[hh][:, P:2 * P], vh[0], start=True, stop=False)
                mm(o, probT[hh][:, 2 * P:3 * P], vh[1], start=False,
                   stop=True).then_inc(full_sem(f"FO{g_}") if hh == 3 else sem("fox_heads"), 1)

            for b in range(TB):
                read(pe, f"FV{b}0"), read(pe, f"FV{b}1")
            for h in range(FH):
                free(pe, f"PF{h}")
                pe.wait_ge(sem("fox_exp"), 2 * h + 2)
                for i in range(3):
                    last = nc.tensor.transpose(bank(f"PF{h}")[:, P * i:P * i + P], logits[:, h, P * i:P * i + P], ident)
                last.then_inc(full_sem(f"PF{h}"), 1)
                if h >= 2:
                    fox_output(h - 2)
            fox_output(FH - 2)
            fox_output(FH - 1)
            read(pe, "FO2"), read(pe, "MW")
            transposes("TP", mixed)
            for i in range(4):
                read(pe, f"TP{i}")
            output_projection("X", OUT1A)
            pe.wait_ge(sem("ffn1_ready"), 2)
            transposes("TR", xs)
            for i in range(4):
                read(pe, f"TR{i}")
            project("RL", [(bank("RL")[:, NE * b:NE * b + NE], lambda c, b=b: hT[:, c, tok(b)], lambda c: wr[:, c, :])
                           for b in range(TB)])
            pe.wait_ge(sem("chosen"), 2)
            free(pe, "POS")
            mm(bank("POS")[:, 0:NE], const("tri"), sel[:, 0, :], start=True, stop=True)
            mm(bank("POS")[:, NE:2 * NE], const("ones"), sel[:, 0, :], start=True, stop=False)
            mm(bank("POS")[:, NE:2 * NE], const("tri"), sel[:, 1, :], start=False, stop=True).then_inc(full_sem("POS"), 1)
            free(pe, "CNT")
            for b in range(TB):
                last = mm(bank("CNT")[0:1, 0:NE], const("ones")[:, 0:1], sel[:, b, :], start=(b == 0), stop=(b == 1))
            last.then_inc(full_sem("CNT"), 1)

            def experts(k):
                with pe.Fori(0, NE) as e:
                    n = e + k * NE
                    pe.wait_ge(sem("perm_built"), n + (k + 1))
                    for i in range(2):
                        e_free(pe, n, f"GA{i}")
                        for c in range(4):
                            for b in range(TB):
                                last = mm(e_bank(f"GA{i}")[:, CAP * c:CAP * (c + 1)], by_chunk(xs, b, 4 * i + c), perm[:, b, :],
                                          start=(b == 0), stop=(b == 1))
                        last.then_inc(e_full_sem(f"GA{i}"), 1)
                    e_free(pe, n, "ST")
                    for b in range(TB):
                        last = nc.tensor.transpose(e_bank("ST")[0:CAP, P * b:P * b + P], wperm[:, b, :], ident)
                    last.then_inc(e_full_sem("ST"), 1)
                    e_read(pe, n, "GA0"), e_read(pe, n, "GA1")

                    def up(fc):
                        s_ = fc % RING_MOE
                        pe.wait_ge(sem(f"slot{s_}_loaded"), n * (48 * slot_fills[s_]) + (total[s_] + 48 * (fc // RING_MOE + 1)))
                        wt = ring[:, s_, 0:4096].rearrange("p (a c n) -> p c a n", a=2, c=KC)
                        e_free(pe, n, f"G{fc}")
                        for c in range(KC):
                            last = mm(e_bank(f"G{fc}")[0:CAP, :].rearrange("p (a n) -> p a n", a=2), hTe[:, c, :], wt[:, c],
                                      start=(c == 0), stop=(c == KC - 1))
                        last.then_inc(e_full_sem(f"G{fc}"), 1)

                    up(0)
                    for fc in range(NF):
                        if fc < NF - 1:
                            up(fc + 1)
                        e_read(pe, n, f"G{fc}")
                        e_free(pe, n, f"T{fc}")
                        for j in range(2):
                            last = nc.tensor.transpose(e_bank(f"T{fc}")[:, CAP * j:CAP * (j + 1)], e_h[0:CAP, j::2],
                                                       ident[0:CAP, 0:CAP])
                        last.then_inc(e_full_sem(f"T{fc}"), 1)
                        e_read(pe, n, f"T{fc}")
                        wd = piece(ring[:, fc % RING_MOE, :], 4096, 2, D)
                        for half in range(2):
                            if fc == 0:
                                e_free(pe, n, f"D{half}")
                            for j in range(2):
                                last = mm(e_bank(f"D{half}")[0:CAP, :], e_hT[:, j, :], wd[:, j, 512 * half:512 * half + 512],
                                          start=(fc == 0 and j == 0), stop=(fc == NF - 1 and j == 1))
                            if fc == NF - 1:
                                last.then_inc(e_full_sem(f"D{half}"), 1)
                        if fc < NF - 1:
                            last.then_inc(sem("expert_chunks"), 1)
                    e_read(pe, n, "ST"), e_read(pe, n, "D0"), e_read(pe, n, "D1")
                    for q in range(4):
                        b, half = divmod(q, 2)
                        e_free(pe, n, f"SC{q}")
                        mm(e_bank(f"SC{q}")[:, :], scat[0:CAP, b, :], yE[0:CAP, 512 * half:512 * half + 512], start=True,
                           stop=True).then_inc(e_full_sem(f"SC{q}"), 1)

            experts(0)
            overflow(pe, lambda: experts(1))


_INS = ["x", "mem", "norm_mix", "norm_mem", "norm_ffn", "norm_kv", "norm_final", "w_in_a", "w_gla_gate2", "b_gla_gate2",
        "gla_onorm", "w_in_b", "w_kv", "b_forget", "w_mem_kv", "w_out", "w_ff_gate", "w_ff_up", "w_ff_down", "w_router",
        "w_moe_gate", "w_moe_up", "w_moe_down"]


def kernel(**inputs):
    import concourse.bacc as _bacc
    from concourse.bass_utils import run_bass_kernel_spmd as _run

    nc = _bacc.Bacc("TRN2", target_bir_lowering=False, num_devices=1)
    arrays, args = {}, {}
    for name in _INS:
        arr = np.ascontiguousarray(inputs[name])
        arrays[f"in_{name}"] = arr
        args[name] = nc.dram_tensor(f"in_{name}", arr.shape, mybir.dt.from_np(arr.dtype), kind="ExternalInput").ap()
    arrays["in_table"] = constant_table()
    table = nc.dram_tensor("in_table", arrays["in_table"].shape, F32, kind="ExternalInput").ap()
    out = nc.dram_tensor("out", (1, S, D), F32, kind="ExternalOutput").ap()
    program(nc, args, table, out)
    return _run(nc, [arrays], core_ids=[0]).results[0]["out"]
```

```python
import concourse.bass as bass
from concourse import mybir
from contextlib import ExitStack
import numpy as np

F32 = mybir.dt.float32
F32R = mybir.dt.float32r
I32 = mybir.dt.int32
U32 = mybir.dt.uint32
ALU = mybir.AluOpType
ACT = mybir.ActivationFunctionType
AX = mybir.AxisListType.X

P = 128
D = 1024
KC = D // P
S = 256
TB = S // P
EPS = 1e-6
MAIN = 768
MEMW = 256
MH, MD = 4, 64
GH, DK, DV = 4, 96, 192
RANK = 16
CHUNK = 64
LEVELS = 6
FH, FD = 12, 64
DFF = 2816
FC = 256
NF = DFF // FC
NE = 8
CAP = 128
UNIT = 4096
DOWN = 2048
NBODY = 2 * NF
TURNS = NE // 2
GU_SLOTS = (0, 1, 2) * 6 + (0, 1, 0, 2)
GU_PARTS, D_PARTS = 4, 2
NEG = -1e30


def constant_columns():
    at, cols = {}, 0
    for name, n in (("ident", P), ("tri16", P), ("tri", P), ("ones", P), ("levels", LEVELS * P),
                    ("causal", 3 * P), ("slots", 2 * P), ("earlier", NE * NE), ("mhalf", 8)):
        at[name] = (cols, n)
        cols += n
    return at, cols


def constant_table():
    at, cols = constant_columns()
    c = np.zeros((P, cols), np.float32)
    i = np.arange(P)
    s, t = i[:, None], i[None, :]

    def put(name, value):
        c[:, at[name][0]:at[name][0] + at[name][1]] = value

    put("ident", s == t)
    put("tri16", ((s <= t) & (s // CHUNK == t // CHUNK)) / 16.0)
    put("tri", s <= t)
    put("ones", 1.0)
    put("levels", np.concatenate(
        [(s // (2 * h) == t // (2 * h)) & (s % (2 * h) < h) & (t % (2 * h) >= h)
         for h in (CHUNK // 2 >> n for n in range(LEVELS))], axis=1))
    later = np.where(t <= s, 0.0, NEG)
    put("causal", np.concatenate([later, 0.0 * later, later], axis=1))
    put("slots", np.arange(2 * P)[None, :])
    e = np.arange(NE)
    put("earlier", (e[None, :] < e[:, None]).reshape(1, -1))
    put("mhalf", -0.5)
    return c


def early_jobs():
    names = [f"TX{i}" for i in range(4)] + ["GLR", "Z0", "Z1", "Q0", "Q1", "K0", "K1"]
    names += [f"TM{i}" for i in range(4)] + ["B0", "B1", "MQ", "KM0", "VM0"]
    names += ["L0_0", "L0_1", "V00", "V10", "L1_0", "L1_1", "V01", "V11", "L2_0", "L2_1"]
    names += ["KM1", "L3_0", "L3_1", "VM1", "L4_0", "L4_1", "SM0", "SM1", "L5_0", "L5_1"]
    names += ["SM2", "SM3", "L6_0", "L6_1", "KH0", "KH1", "R00", "R10", "R01", "R11"]
    names += [f"U{c}_{hp}" for c in range(3) for hp in range(2)]
    names += [f"PM{i}" for i in range(4)] + ["MV"]
    names += ["O00", "O01", "O10", "O11"]
    names += [f"TO{i}" for i in range(4)] + ["WA0", "WA1", "WB0", "WB1"]
    names += [f"TF{i}" for i in range(4)]
    jobs = [(n, i % 8) for i, n in enumerate(names)]
    jobs += [(f"Y{i}", i) for i in range(4)]
    for f in range(NF):
        jobs += [(f"G{f}_{b}", 4 + b) for b in range(TB)] + [(f"T{f}", 6 + f % 2)]
    names = [f"TK{i}" for i in range(4)] + ["FG", "FK0", "FK1", "FK2", "CC"]
    names += ["FV00", "FV10", "FV01", "FV11", "FQ0", "FQ1", "FQ2", "MQ1"]
    names += [f"N{i}" for i in range(4)]
    names += [f"S{h}" for h in range(FH)] + [f"PN{i}" for i in range(4)] + ["MW"]
    for h in range(FH):
        names += [f"PF{h}"] + ([f"FO{(h - 2) // 4}"] if h >= 2 and (h - 2) % 4 == 0 else [])
    names += [f"TP{i}" for i in range(4)] + ["XA0", "XA1", "XB0", "XB1"]
    names += [f"TR{i}" for i in range(4)] + ["RL", "POS", "CNT"]
    jobs += [(n, i % 8) for i, n in enumerate(names)]
    return jobs


def expert_jobs():
    jobs = []
    for u in range(2):
        jobs += [((u, f"D{half}"), half) for half in range(2)]
        for fc in range(NF):
            jobs += [((u, f"T{fc}"), 4)]
            jobs += [((u + 1, "G0") if fc == NF - 1 else (u, f"G{fc + 1}"), g_bank(NF * u + fc + 1))]
        jobs += [((u, "SC0"), 5), ((u, "SC1"), 6), ((u, "SC2"), 7), ((u, "SC3"), 5), ((u, "ST"), 6)]
        jobs += [((u + 1, "GH0"), 7), ((u + 1, "GH1"), 5), ((u + 1, "GL0"), 6), ((u + 1, "GL1"), 7)]
    return jobs


def g_bank(j):
    return 2 + j % 2


def program(nc, a, table, out):
    at, ncols = constant_columns()
    ctx = ExitStack()
    with ctx:
        base = (nc.sbuf_base + 63) // 64 * 64

        def place(name, at_, n, dt=F32):
            return nc.alloc_sbuf_tensor_at(name, [P, n], dt, offset=base + 4 * at_)[:, :]

        sems = {}

        def sem(name):
            if name not in sems:
                sems[name] = ctx.enter_context(nc.semaphore(name))
            return sems[name]

        X, CONST, SMALLS, ROW = 0, 2048, 4096, 4736
        XS, MIXED, HT, EXTRA = 5760, 7808, 9856, 11904
        RAW, SPLIT = 16104, 16104 + 4 * UNIT
        assert ncols <= 2048 and base + 4 * (SPLIT + 4 * UNIT + 2 * DOWN) <= nc.sbuf_usable_end
        consts = place("consts", CONST, ncols)
        x = place("x", X, TB * D).rearrange("p (b d) -> p b d", b=TB)
        xs = place("xs", XS, TB * D).rearrange("p (b d) -> p b d", b=TB)
        hT = place("hT", HT, KC * S).rearrange("p (c s) -> p c s", c=KC)
        mixed = place("mixed", MIXED, TB * D).rearrange("p (b d) -> p b d", b=TB)
        extra = place("extra", EXTRA, 4200)
        small = place("small", SMALLS, 640)
        gain_row = place("gain_row", ROW, D)
        raw = place("raw", RAW, 4 * UNIT).rearrange("p (s n) -> p s n", s=4)
        raw_down = raw[:, 3, :].rearrange("p (s n) -> p s n", s=2)
        arena = place("arena", SPLIT, 4 * UNIT + 2 * DOWN)
        gu_hi, gu_lo = ([place(f"gu_{n_}{i}", SPLIT + (2 * i + j) * UNIT, UNIT, F32R) for i in range(2)]
                        for j, n_ in enumerate(("hi", "lo")))
        down_hi, down_lo = (place(f"down_{n_}", SPLIT + 4 * UNIT + j * DOWN, DOWN, F32R)
                            for j, n_ in enumerate(("hi", "lo")))
        psum = [ctx.enter_context(nc.psum_tensor(f"bank{i}", [P, 512], F32)) for i in range(8)]
        counts = place("counts", SMALLS + 600, 16)
        over = place("over", SMALLS + 616, 2, I32)

        class Carve:
            def __init__(self, base):
                self.base, self.n = base, 0

            def __call__(self, n, at=None):
                lo = self.n if at is None else at
                self.n = lo + n
                assert self.n <= self.base.shape[1], (self.n, self.base.shape)
                return self.base[:, lo:lo + n]

        def const(name):
            lo, n = at[name]
            return consts[:, lo:lo + n]

        ident = const("ident")
        g = Carve(arena)
        mT0 = g(2048).rearrange("p (c s) -> p c s", c=KC)
        mT1 = g(2048).rearrange("p (c s) -> p c s", c=KC)
        zbuf = g(2304)
        qT, kT, bT = (g(1024) for _ in range(3))
        decay = g(1024)
        prod = [g(1024), g(1024)]
        scoreT = g(1024).rearrange("p (b h t) -> p b h t", b=TB, h=GH)
        khat = g(768).rearrange("p (b h k) -> p b h k", b=TB, h=GH)
        kmT0 = g(1024).rearrange("p (h s) -> p h s", h=MH)
        mqT0 = g(1024).rearrange("p (h s) -> p h s", h=MH)
        vm0 = g(512).rearrange("p (b n) -> p b n", b=TB)
        alast, blast = g(16), g(16)
        zz, ez, la = (zbuf[:, 768 * i:768 * i + 768] for i in range(3))
        la_v = la.rearrange("p (b n) -> p b n", b=TB)
        state = zbuf.rearrange("p (c h v) -> p c h v", c=3, h=GH)
        pm0 = mT0.rearrange("p c s -> p (c s)").rearrange("p (b h m) -> p b h m", b=TB, h=MH)
        pmT0 = mT1.rearrange("p c s -> p (c s)").rearrange("p (m b h t) -> p m b h t", m=2, b=TB, h=MH)

        f = Carve(arena)
        fqT = f(FH * S).rearrange("p (h s) -> p h s", h=FH)
        fkT = f(FH * S).rearrange("p (h s) -> p h s", h=FH)
        logits = f(FH * 384).rearrange("p (h s) -> p h s", h=FH)
        probT = [f(384) for _ in range(4)]
        cT = f(256)
        negcT = f(256)
        hT2 = logits[:, 0:6, :].rearrange("p h s -> p (h s)")[:, 0:KC * S].rearrange("p (c s) -> p c s", c=KC)
        mqT1 = f(1024).rearrange("p (h s) -> p h s", h=MH)
        pm1 = f(2048).rearrange("p (b h m) -> p b h m", b=TB, h=MH)
        pmT1 = f(2048).rearrange("p (m b h t) -> p m b h t", m=2, b=TB, h=MH)

        def split_tile(name, hi_at, lo_at, n):
            return place(name + "_hi", hi_at, n, F32R), place(name + "_lo", lo_at, n, F32R)

        d_xT = [t_.rearrange("p (c s) -> p c s", c=KC) for t_ in split_tile("dense_xT", HT, MIXED, KC * S)]
        d_sg = place("dense_silu", XS, 512).rearrange("p (b n) -> p b n", b=TB)
        d_h = place("dense_h", XS + 512, 512).rearrange("p (b n) -> p b n", b=TB)
        d_hT = [t_.rearrange("p (j t) -> p j t", j=2) for t_ in split_tile("dense_hT", XS + 1024, XS + 1536, 512)]

        v = Carve(extra)
        kmT1 = v(1024).rearrange("p (h s) -> p h s", h=MH)
        vm1 = v(512).rearrange("p (b n) -> p b n", b=TB)
        val = v(1536).rearrange("p (b n) -> p b n", b=TB)
        glrT = v(256)
        w2 = v(384)
        v(3900 - v.n)
        wf = v(96).rearrange("p (c n) -> p c n", c=KC)
        wr = v(64).rearrange("p (c n) -> p c n", c=KC)
        bf = v(12)

        e_x = [t_.rearrange("p (b d) -> p b d", b=TB) for t_ in split_tile("expert_x", MIXED, EXTRA, TB * D)]
        e_xT = [[t_.rearrange("p (c s) -> p c s", c=KC) for t_ in split_tile(f"expert_xT{i}", hi_at, lo_at, KC * CAP)]
                for i, (hi_at, lo_at) in enumerate(((HT, HT + KC * CAP), (ROW, CONST + at["levels"][0])))]
        assert KC * CAP <= at["levels"][1] + at["causal"][1] and KC * CAP <= D
        final_gain = raw[:, 1, 0:D]
        e_y = list(split_tile("expert_y", XS, XS + D, D))
        at_ = EXTRA + TB * D
        e_sg, e_h = place("expert_silu", at_, FC), place("expert_h", at_ + FC, FC)
        e_hT = [t_.rearrange("p (j t) -> p j t", j=2) for t_ in split_tile("expert_hT", at_ + 512, at_ + 768, 2 * CAP)]
        perm = place("perm", at_ + 1024, TB * CAP).rearrange("p (b s) -> p b s", b=TB)
        perm_r = place("perm_r", at_ + 1280, TB * CAP, F32R).rearrange("p (b s) -> p b s", b=TB)
        scat = place("scat", at_ + 1536, S, F32R).rearrange("p (b t) -> p b t", b=TB)
        slot_gate = place("slot_gate", SMALLS + 624, 2)[:, 0:1]

        w = Carve(small)
        GAINS = ("mix0", "mem0", "mem1", "mix1", "ffn0", "kv", "onorm")
        gains = {n: w(KC) for n in GAINS}
        square = {n: w(2) for n in ("x", "mem", "ffn0", "kv", "ffn1", "final")}
        mean = {n: w(2) for n in square}
        rstd = {n: w(2) for n in square}
        o_sq, o_mean, o_rstd = (w(8) for _ in range(3))
        m_max = [w(8).rearrange("p (b h) -> p b h", b=TB) for _ in range(2)]
        m_sum = [w(8) for _ in range(2)]
        m_inv = [w(8) for _ in range(2)]
        f_max, f_sum, f_inv = (w(24) for _ in range(3))
        fz, fe = w(24), w(24)
        fl = w(24).rearrange("p (b h) -> p b h", b=TB)
        lg, ex, sel, gate_u = (w(16).rearrange("p (b e) -> p b e", b=TB) for _ in range(4))
        gt, eq = w(64).rearrange("p (e o) -> p e o", e=NE), w(64).rearrange("p (e o) -> p e o", e=NE)
        top, den, rden = w(2), w(2), w(2)
        r_mean = w(2)
        pos = w(18).rearrange("p (b e) -> p b e", b=TB)
        gate = w(18).rearrange("p (b e) -> p b e", b=TB)
        rank = w(8)

        fill, fills = {}, [0] * 8
        for name, bank in early_jobs():
            fills[bank] += 1
            fill[name] = (bank, fills[bank])
        per, e_fill = [0] * 8, {}
        for name, b in expert_jobs():
            per[b] += 1
            e_fill[name] = (b, per[b])
        start, around = [], []
        for k in range(2):
            once = {}
            for name, b in (("GH0", 7), ("GH1", 5), ("GL0", 6), ("GL1", 7), ("G0", g_bank(0)), ("D0", 0), ("D1", 1)):
                fills[b] += 1
                once[name] = (b, fills[b])
            start.append(list(fills))
            fills = [n + TURNS * m_ for n, m_ in zip(fills, per)]
            for (u, name), b in expert_jobs():
                fills[b] -= u == 2
            for name, b in (("SC0", 5), ("SC1", 6), ("SC2", 7), ("SC3", 5)):
                fills[b] += 1
                once[name] = (b, fills[b])
            around.append(once)

        def bank(name):
            return psum[fill[name][0]]

        def filled(eng, name):
            b, n = fill[name]
            eng.wait_ge(sem(f"bank{b}_full"), n)

        def read(eng, name):
            b, n = fill[name]
            eng.wait_ge(sem(f"bank{b}_read"), n)

        def free(eng, name):
            b, n = fill[name]
            if n > 1:
                eng.wait_ge(sem(f"bank{b}_read"), n - 1)

        def full_sem(name):
            return sem(f"bank{fill[name][0]}_full")

        def read_sem(name):
            return sem(f"bank{fill[name][0]}_read")

        def e_count(T, u, name, less=0):
            (k, t_), turns = T, 0
            while (u, name) not in e_fill or u < 0:
                u, turns = u + 2, turns + 1
            b, i = e_fill[u, name]
            i += start[k][b] - turns * per[b] - less
            assert i > 0
            return b, t_ * per[b] + i

        def count_filled(eng, count):
            eng.wait_ge(sem(f"bank{count[0]}_full"), count[1])

        def count_read(eng, count):
            eng.wait_ge(sem(f"bank{count[0]}_read"), count[1])

        def e_filled(eng, T, u, name):
            count_filled(eng, e_count(T, u, name))

        def e_read(eng, T, u, name):
            count_read(eng, e_count(T, u, name))

        def e_free(eng, T, u, name):
            count_read(eng, e_count(T, u, name, less=1))

        def e_place(u, name):
            return next(b for (v_, n_), (b, _) in e_fill.items() if n_ == name and (v_ - u) % 2 == 0)

        def e_bank(name, u=0):
            return psum[e_place(u, name)]

        def e_full_sem(name, u=0):
            return sem(f"bank{e_place(u, name)}_full")

        def e_read_sem(name, u=0):
            return sem(f"bank{e_place(u, name)}_read")

        def chunk_done(eng, T, j):
            u, fc = divmod(j, NF)
            if fc == NF - 1:
                e_filled(eng, T, u, "D1")
            else:
                n = T[1] + TURNS * T[0]
                eng.wait_ge(sem("expert_chunks"), n * (2 * (NF - 1)) + ((NF - 1) * u + fc + 1))

        def chunk_no(n, j):
            return n * NBODY + (NF + j)

        def cols(wt, lo, hi):
            return wt.rearrange("(p c) n -> p c n", c=KC)[:, :, lo:hi]

        w_in_a, w_in_b = a["w_in_a"][0], a["w_in_b"][0]
        GLA_UNITS = [
            ("gates", 0, cols(w_in_a, 2304, 2576), "MQ"),
            ("q", 1, cols(w_in_a, 0, 384), "Q1"),
            ("k", 2, cols(w_in_a, 384, 768), "K1"),
            ("mem0", 3, cols(a["w_mem_kv"][0], 0, 512), "VM0"),
            ("v0", 1, cols(w_in_a, 768, 1152), "V10"),
            ("v1", 2, cols(w_in_a, 1152, 1536), "V11"),
            ("mem1", 0, cols(a["w_mem_kv"][1], 0, 512), "VM1"),
            ("r0", 3, cols(w_in_a, 1536, 1920), "R10"),
            ("r1", 1, cols(w_in_a, 1920, 2304), "R11"),
            ("out0a", 2, cols(a["w_out"][0], 0, 512), "WA1"),
            ("out0b", 0, cols(a["w_out"][0], 512, 1024), "WB1"),
        ]
        FOX_UNITS = [
            ("fk0", 0, cols(a["w_kv"], 0, 384), "FK1"),
            ("fk1", 1, cols(a["w_kv"], 384, 768), "FK2"),
            ("fv0", 2, cols(a["w_kv"], 768, 1152), "FV10"),
            ("fv1", 3, cols(a["w_kv"], 1152, 1536), "FV11"),
            ("fq0", 0, cols(w_in_b, 0, 384), "FQ1"),
            ("fq1", 1, cols(w_in_b, 384, 768), "FQ2"),
            ("fmq", 2, cols(w_in_b, 768, 1024), "MQ1"),
            ("out1a", 3, cols(a["w_out"][1], 0, 512), "XA1"),
            ("out1b", 2, cols(a["w_out"][1], 512, 1024), "XB1"),
        ]
        DENSE_GU = [(1 + f_) % 3 for f_ in range(NF)]
        arrived, unit_slot, loaded = {}, {}, [0] * 4
        for name, s_, _, _ in GLA_UNITS:
            loaded[s_] += 16
            arrived[name], unit_slot[name] = loaded[s_], s_
        for f_ in range(NF):
            loaded[DENSE_GU[f_]] += 32
            arrived[f"gu{f_}"] = loaded[DENSE_GU[f_]]
        for name, s_, _, _ in FOX_UNITS:
            loaded[s_] += 16
            arrived[name], unit_slot[name] = loaded[s_], s_
        DENSE_DOWN = [16 * (f_ // 2 + 1) for f_ in range(NF)]
        down_loaded = [16 * len(range(s_, NF, 2)) for s_ in range(2)]

        def weights(eng, name):
            s_ = unit_slot[name]
            eng.wait_ge(sem(f"raw{s_}_loaded"), arrived[name])
            src = next(u[2] for u in GLA_UNITS + FOX_UNITS if u[0] == name)
            return piece(raw[:, s_, :], 0, KC, src.shape[2])

        def piece(slot, lo, nc_, n):
            return slot[:, lo:lo + nc_ * n].rearrange("p (c n) -> p c n", c=nc_)

        def gu_arrived(eng, n, j):
            s_ = GU_SLOTS[j]
            eng.wait_ge(sem(f"raw{s_}_loaded"), n * (32 * GU_SLOTS.count(s_)) + (loaded[s_] + 32 * GU_SLOTS[:j + 1].count(s_)))
            return raw[:, s_, :]

        def dense_gu_arrived(eng, fc):
            eng.wait_ge(sem(f"raw{DENSE_GU[fc]}_loaded"), arrived[f"gu{fc}"])

        def down_arrived(eng, n, j):
            s_ = j % 2
            eng.wait_ge(sem(f"down{s_}_loaded"), n * (16 * NF) + (down_loaded[s_] + 16 * (j // 2 + 1)))
            return raw_down[:, s_, :]

        def fox_head_done(eng, h):
            if h % 4 == 3:
                filled(eng, f"FO{h // 4}")
            else:
                eng.wait_ge(sem("fox_heads"), 3 * (h // 4) + h % 4 + 1)

        SMALL = 16 * 16
        def overflow(eng, second_pass):
            eng.wait_ge(sem("overflow_known"), 1)
            most = eng.value_load(over[0:1, 0:1], min_val=0, max_val=S)
            with eng.If(most > CAP):
                second_pass()

        block = ctx.enter_context(nc.Block())

        @block.sync
        def _(sp):
            def unit(name, s_, src):
                n = src.shape[2]
                sp.dma_start(piece(raw[:, s_, :], 0, KC, n), src).then_inc(sem(f"raw{s_}_loaded"), 16)

            def gate_up(s_, wg, wu):
                for i, src in enumerate((wg, wu)):
                    sp.dma_start(piece(raw[:, s_, :], 2048 * i, KC, FC), src).then_inc(sem(f"raw{s_}_loaded"), 16)

            def down(s_, wd):
                sp.dma_start(raw_down[:, s_, :].rearrange("p (j n) -> p j n", j=2), wd).then_inc(sem(f"down{s_}_loaded"), 16)

            LAG = 2

            def dense_downs(f_):
                return {0: [0], 1: [], 2: [], NF - 1: [NF - 3, NF - 2, NF - 1]}.get(f_, [f_ - LAG])

            last = {}
            for name, s_, src, job in GLA_UNITS:
                if s_ in last:
                    filled(sp, last[s_])
                unit(name, s_, src)
                last[s_] = job
            wg, wu, wd = a["w_ff_gate"][0], a["w_ff_up"][0], a["w_ff_down"][0]
            for f_ in range(NF):
                s_ = DENSE_GU[f_]
                if f_ < 3:
                    filled(sp, last[s_])
                else:
                    sp.wait_ge(sem("gu_split"), GU_PARTS * (f_ - 2))
                gate_up(s_, cols(wg, f_ * FC, (f_ + 1) * FC), cols(wu, f_ * FC, (f_ + 1) * FC))
                for i in dense_downs(f_):
                    if i == 0:
                        filled(sp, last[3])
                    elif i >= 2:
                        sp.wait_ge(sem("down_split"), D_PARTS * (i - 1))
                    down(i % 2, wd[i * FC:(i + 1) * FC, :].rearrange("(p j) n -> p j n", j=2))
            last = {}
            for name, s_, src, job in FOX_UNITS:
                if s_ in last:
                    filled(sp, last[s_])
                elif s_ == 3:
                    sp.wait_ge(sem("down_split"), D_PARTS * NF)
                else:
                    was = max(f_ for f_ in range(NF) if DENSE_GU[f_] == s_)
                    sp.wait_ge(sem("gu_split"), GU_PARTS * (was + 1))
                unit(name, s_, src)
                last[s_] = job

            def expert_gate_up(e, j):
                lo = (j % NF) * FC
                gate_up(GU_SLOTS[j], *(a[wt][0, bass.ds(e, 1), :, lo:lo + FC].rearrange("a (p c) n -> (a p) c n", c=KC)
                                       for wt in ("w_moe_gate", "w_moe_up")))

            def expert_down(e, j):
                lo = (j % NF) * FC
                down(j % 2, a["w_moe_down"][0, bass.ds(e, 1), lo:lo + FC, :].rearrange("a (p j) n -> (a p) j n", j=2))

            AHEAD = 3

            def load_gate_up(n, t_, j, first):
                s_ = GU_SLOTS[j]
                if not first:
                    was = max(i for i in range(j - NBODY, j) if GU_SLOTS[i] == s_)
                    sp.wait_ge(sem("gu_split"), (chunk_no(n, was) + 1) * GU_PARTS)
                else:
                    filled(sp, last[s_])
                expert_gate_up(t_ * 2 + j // NF, j)

            def load_down(n, t_, j, first=False):
                if not first or j >= 2:
                    sp.wait_ge(sem("down_split"), (chunk_no(n, j - 2) + 1) * D_PARTS)
                elif j == 0:
                    filled(sp, last[3])
                expert_down(t_ * 2 + j // NF, j)

            def experts(k):
                n = TURNS * k
                if k > 0:
                    sp.wait_ge(sem("final_gain_loaded"), 16)
                load_gate_up(n, 0, 0, k == 0)
                load_down(n, 0, 0, k == 0)
                load_gate_up(n, 0, 1, k == 0)
                load_gate_up(n, 0, 2, k == 0)

                def turn(t_, final):
                    n = t_ + TURNS * k
                    for j in range(AHEAD, NBODY):
                        load_down(n, t_, j - LAG)
                        load_gate_up(n, t_, j, False)
                    if final:
                        for j in range(NBODY - LAG, NBODY):
                            load_down(n, t_, j)
                    else:
                        following = t_ + (TURNS * k + 1), t_ + 1
                        for j in range(AHEAD):
                            if j < LAG:
                                load_down(n, t_, NBODY - LAG + j)
                            else:
                                load_down(*following, j - LAG)
                            load_gate_up(*following, j, False)

                with sp.Fori(0, TURNS - 1) as t_:
                    turn(t_, False)
                turn(TURNS - 1, True)
                was = max(j for j in range(NBODY) if GU_SLOTS[j] == 1)
                sp.wait_ge(sem("gu_split"), (chunk_no(TURNS * k + TURNS - 1, was) + 1) * GU_PARTS)
                sp.dma_start(final_gain, a["norm_final"].rearrange("(a n) -> a n", a=1).partition_broadcast(P)).then_inc(
                    sem("final_gain_loaded"), 16)

            experts(0)
            overflow(sp, lambda: experts(1))
            for b in range(TB):
                sp.wait_ge(sem("out_ready"), b + 1)
                sp.dma_start(out[0, b * P:(b + 1) * P, :], xs[:, b, :]).then_inc(sem("stored"), 16)
            sp.wait_ge(sem("stored"), 32)

        @block.scalar
        def _(act):
            act.dma_start(x[:, :, :], a["x"].rearrange("a (b p) d -> p (a b) d", p=P)).then_inc(sem("x_loaded"), 16)
            act.dma_start(mixed[:, :, :], a["mem"].rearrange("a (b p) d -> p (a b) d", p=P)).then_inc(sem("mem_loaded"), 16)

            def evacuate(name, outs_ins):
                filled(act, name)
                for o, i, sc in outs_ins:
                    last = nc.scalar.activation(o, i, ACT.Copy, scale=sc)
                last.then_inc(read_sem(name), 1)

            def split_high(src, dst, parts, done, which=None):
                n = src.shape[1] // parts
                for i in range(parts) if which is None else which:
                    nc.scalar.activation(dst[:, n * i:n * i + n], src[:, n * i:n * i + n], ACT.Copy).then_inc(sem(done), 1)

            for name, src in (("x", x), ("mem", mixed)):
                act.wait_ge(sem(f"{name}_loaded"), 16)
                for b in range(TB):
                    if name == "mem":
                        act.wait_ge(sem("squares_x"), b + 1)
                    nc.scalar.activation(prod[b], src[:, b, :], ACT.Square,
                                         accum_out=square[name][:, b:b + 1]).then_inc(sem(f"squares_{name}"), 1)

            act.wait_ge(sem("small_loaded"), SMALL)
            def two_chunks(name, dst, gain, i):
                return [(dst[:, 2 * i + j, :], bank(name)[:, 256 * j:256 * j + 256], gains[gain][:, 2 * i + j:2 * i + j + 1])
                        for j in range(2)]
            for i in (0, 2):
                evacuate(f"TX{i}", two_chunks(f"TX{i}", hT, "mix0", i))
            act.wait_ge(sem("gate_abs"), 1)
            nc.scalar.activation(ez, ez, ACT.Exp).then_inc(sem("gate_exp"), 1)
            act.wait_ge(sem("gate_exp"), 1)
            nc.scalar.activation(ez, ez, ACT.Ln, bias=1.0).then_inc(sem("gate_log"), 1)
            for i in range(2):
                evacuate(f"Q{i}", [(qT[0:DK, 512 * i:512 * i + 512], bank(f"Q{i}")[0:DK, :], DK ** -0.5)])
            for i in range(2):
                evacuate(f"K{i}", [(kT[0:DK, 512 * i:512 * i + 512], bank(f"K{i}")[0:DK, :], 1.0)])
            for i in (0, 2):
                evacuate(f"TM{i}", two_chunks(f"TM{i}", mT0, "mem0", i) + two_chunks(f"TM{i}", mT1, "mem1", i))

            def two_heads(name, dst, scale):
                src = bank(name)[:, :].rearrange("p (a s) -> p a s", a=2)
                return [(dst[0:64, j::2, :], src[64 * j:64 * j + 64], scale) for j in range(2)]

            evacuate("MQ", two_heads("MQ", mqT0, MD ** -0.5))
            evacuate("VM0", [(vm0[:, :, :].rearrange("p b n -> p (b n)"), bank("VM0")[:, :], 1.0)])

            def level_exp(n):
                act.wait_ge(sem("decay_diff"), n + 1)
                nc.scalar.activation(decay[0:DK, :], decay[0:DK, :], ACT.Exp).then_inc(sem("decay_exp"), 1)

            def softmax_mem(layer, name, i, first):
                b, j = divmod(i, 2)
                act.wait_ge(sem("mem_max"), first + i + 1)
                pmx, p_ = m_max[layer], (pm0, pm1)[layer]
                for h in range(2):
                    last = nc.scalar.activation(p_[:, b, 2 * j + h, :], bank(name)[:, 256 * h:256 * h + 256], ACT.Exp,
                                                bias=pmx[:, b, 2 * j + h:2 * j + h + 1],
                                                accum_out=m_sum[layer][:, 4 * b + 2 * j + h:4 * b + 2 * j + h + 1])
                last.then_inc(read_sem(name), 1)

            level_exp(0)
            evacuate("V00", [(val[:, 0, 0:384], bank("V00")[:, 0:384], 1.0)])
            level_exp(1)
            evacuate("V10", [(val[:, 1, 0:384], bank("V10")[:, 0:384], 1.0)])
            level_exp(2)
            level_exp(3)
            evacuate("VM1", [(vm1[:, :, :].rearrange("p b n -> p (b n)"), bank("VM1")[:, :], 1.0)])
            level_exp(4)
            softmax_mem(0, "SM0", 0, 0)
            softmax_mem(0, "SM1", 1, 0)
            level_exp(5)
            softmax_mem(0, "SM2", 2, 0)
            softmax_mem(0, "SM3", 3, 0)
            act.wait_ge(sem("decay_diff"), LEVELS + 1)
            nc.scalar.activation(decay[0:DK, :], bT[0:DK, :], ACT.Exp).then_inc(sem("decay_exp"), 1)
            act.wait_ge(sem("key_diff"), 1)
            nc.scalar.activation(bT[0:DK, :], bT[0:DK, :], ACT.Exp).then_inc(sem("key_exp"), 1)
            evacuate("KH0", [(khat[:, 0, :, :].rearrange("p h k -> p (h k)"), bank("KH0")[:, 0:384], 1.0)])
            evacuate("KH1", [(khat[:, 1, :, :].rearrange("p h k -> p (h k)"), bank("KH1")[:, 0:384], 1.0)])
            for i in range(2):
                for b in range(TB):
                    filled(act, f"R{b}{i}")
                    if b + i == 0:
                        read(act, "TM3")
                    nc.scalar.activation(mixed[:, b, 384 * i:384 * i + 384], bank(f"R{b}{i}")[:, 0:384],
                                         ACT.Silu).then_inc(read_sem(f"R{b}{i}"), 1)
            for i in (0, 2):
                evacuate(f"PM{i}", [(pmT0[:, i % 2, i // 2, :, :].rearrange("p h t -> p (h t)"), bank(f"PM{i}")[:, :], 1.0)])
            act.wait_ge(sem("key_prod"), 1)
            for b in range(TB):
                for i in range(2):
                    filled(act, f"O{b}{i}")
                    for h in range(2):
                        n = 4 * b + 2 * i + h
                        nc.scalar.activation(decay[:, 192 * (n % 4):192 * (n % 4) + 192], bank(f"O{b}{i}")[:, 192 * h:192 * h + 192],
                                             ACT.Square, accum_out=o_sq[:, n:n + 1]).then_inc(sem("o_squares"), 1)
                    if b == 0 and i == 1:
                        act.wait_ge(sem("o_squares"), 4)
            for i in (0, 2):
                evacuate(f"TO{i}", two_chunks(f"TO{i}", hT, "onorm", i))
            act.wait_ge(sem("o_squares"), 8)
            read(act, "O11"), read(act, "MV")
            dense_gu_arrived(act, 0)
            split_high(raw[:, DENSE_GU[0], :], gu_hi[0], GU_PARTS, "gu_high")
            act.wait_ge(sem("down0_loaded"), DENSE_DOWN[0])
            split_high(raw_down[:, 0, :], down_hi, D_PARTS, "down_high")

            def x_squares(name, last):
                read(act, last)
                for b in range(TB):
                    nc.scalar.activation(xs[:, b, :], x[:, b, :], ACT.Square,
                                         accum_out=square[name][:, b:b + 1]).then_inc(sem(f"squares_{name}"), 1)
            x_squares("ffn0", "WB1")
            for i in range(4):
                filled(act, f"TF{i}")
                for o, src, gain in two_chunks(f"TF{i}", d_xT[0], "ffn0", i):
                    last = nc.scalar.activation(o, src, ACT.Copy, scale=gain)
                last.then_inc(sem("dense_x_high"), 1)

            def dense_gu_high(fc, which):
                if fc >= NF:
                    return
                if 0 in which:
                    dense_gu_arrived(act, fc)
                    if fc >= 2:
                        filled(act, f"G{fc - 2}_1")
                split_high(raw[:, DENSE_GU[fc], :], gu_hi[fc % 2], GU_PARTS, "gu_high", which)

            def dense_down_high(fc):
                if fc >= NF:
                    return
                act.wait_ge(sem(f"down{fc % 2}_loaded"), DENSE_DOWN[fc])
                if fc > 0:
                    act.wait_ge(sem("dense_chunks"), fc)
                split_high(raw_down[:, fc % 2, :], down_hi, D_PARTS, "down_high")

            def dense_silu(fc, b):
                filled(act, f"G{fc}_{b}")
                if fc > 0:
                    read(act, f"G{fc - 1}_{b}")
                nc.scalar.activation(d_sg[:, b, :], bank(f"G{fc}_{b}")[:, 0:FC], ACT.Silu).then_inc(sem("dense_silu"), 1)

            dense_gu_high(1, range(GU_PARTS))
            for b in range(TB):
                dense_silu(0, b)
            for fc in range(NF):
                if fc > 0:
                    dense_down_high(fc)
                dense_gu_high(fc + 2, (0, 1))
                filled(act, f"T{fc}")
                if fc > 0:
                    act.wait_ge(sem("dense_chunks"), fc)
                nc.scalar.activation(d_hT[0][:, :, :].rearrange("p j t -> p (j t)"), bank(f"T{fc}")[:, :],
                                     ACT.Copy).then_inc(sem("dense_hT_high"), 1)
                if fc + 1 < NF:
                    dense_silu(fc + 1, 0)
                dense_gu_high(fc + 2, (2, 3))
                if fc + 1 < NF:
                    dense_silu(fc + 1, 1)
            x_squares("kv", "Y3")
            for i in (0, 2):
                evacuate(f"TK{i}", two_chunks(f"TK{i}", hT, "kv", i) + two_chunks(f"TK{i}", hT2, "mix1", i))
            act.wait_ge(sem("forget_abs"), 1)
            nc.scalar.activation(fe, fe, ACT.Exp).then_inc(sem("forget_exp"), 1)
            act.wait_ge(sem("forget_exp"), 1)
            nc.scalar.activation(fe, fe, ACT.Ln, bias=1.0).then_inc(sem("forget_log"), 1)
            for i in range(3):
                evacuate(f"FK{i}", [(fkT[0:64, 4 * i + j:4 * i + j + 3:2, :],
                                     bank(f"FK{i}")[64 * j:64 * j + 64, :].rearrange("p (a s) -> p a s", a=2), 1.0) for j in range(2)])
            filled(act, "CC")
            nc.scalar.activation(negcT[0:FH, :], bank("CC")[0:FH, 0:256], ACT.Copy, scale=-1.0)
            nc.scalar.activation(cT[0:FH, :], bank("CC")[0:FH, 0:256], ACT.Copy).then_inc(read_sem("CC"), 1)
            read(act, "CC")
            act.wait_ge(sem("aug_set"), 2)
            act.dma_start(fkT[64:65, :, :], negcT[0:FH, :]).then_inc(sem("aug_loaded"), 16)
            act.dma_start(fqT[65:66, :, :], cT[0:FH, :]).then_inc(sem("aug_loaded"), 16)
            for b in range(TB):
                evacuate(f"FV{b}0", [(val[:, b, 0:384], bank(f"FV{b}0")[:, 0:384], 1.0)])
            for i in range(3):
                evacuate(f"FQ{i}", [(fqT[0:64, 4 * i + j:4 * i + j + 3:2, :],
                                     bank(f"FQ{i}")[64 * j:64 * j + 64, :].rearrange("p (a s) -> p a s", a=2), FD ** -0.5) for j in range(2)])
            evacuate("MQ1", two_heads("MQ1", mqT1, MD ** -0.5))
            for i in range(4):
                softmax_mem(1, f"N{i}", i, 4)
            act.wait_ge(sem("fox_max"), 1)
            for h in range(FH):
                for b in range(TB):
                    lo, hi = (0, 128) if b == 0 else (128, 384)
                    if h % 4 == 0 and b == 0 and h > 0:
                        act.wait_ge(sem("fox_max"), h // 4 + 1)
                    nc.scalar.activation(logits[:, h, lo:hi], logits[:, h, lo:hi], ACT.Exp, bias=f_max[:, 2 * h + b:2 * h + b + 1],
                                         accum_out=f_sum[:, 2 * h + b:2 * h + b + 1]).then_inc(sem("fox_exp"), 1)
            for i in (0, 2):
                evacuate(f"PN{i}", [(pmT1[:, i % 2, i // 2, :, :].rearrange("p h t -> p (h t)"), bank(f"PN{i}")[:, :], 1.0)])
            for h in range(0, FH, 2):
                if h >= 4:
                    fox_head_done(act, h - 4)
                evacuate(f"PF{h}", [(probT[h % 4], bank(f"PF{h}")[:, 0:384], 1.0)])
            for i in (0, 2):
                evacuate(f"TP{i}", [(hT[:, 2 * i:2 * i + 2, :].rearrange("p c s -> p (c s)"), bank(f"TP{i}")[:, :], 1.0)])
            read(act, "FO2"), read(act, "MW")
            for j in range(2):
                split_high(gu_arrived(act, 0, j), gu_hi[j], GU_PARTS, "gu_high")
            x_squares("ffn1", "XB1")
            for b in range(TB):
                act.wait_ge(sem("ffn1_ready"), b + 1)
                nc.scalar.activation(e_x[0][:, b, :], xs[:, b, :], ACT.Copy).then_inc(sem("x_high"), 1)
            for i in (0, 2):
                evacuate(f"TR{i}", [(hT[:, 2 * i:2 * i + 2, :].rearrange("p c s -> p (c s)"), bank(f"TR{i}")[:, :], 1.0)])
            act.wait_ge(sem("logit_diff"), 1)
            nc.scalar.activation(ex[:, :, :], ex[:, :, :], ACT.Exp).then_inc(sem("logit_exp"), 1)

            def gu_high(n, T, j, which):
                if 0 in which:
                    gu_arrived(act, n, j)
                    e_filled(act, T, (j - 2) // NF, f"G{(j - 2) % NF}")
                split_high(raw[:, GU_SLOTS[j], :], gu_hi[j % 2], GU_PARTS, "gu_high", which)

            def tokens(dst, *counts_):
                for i, count in enumerate(counts_):
                    count_filled(act, count)
                    nc.scalar.activation(dst[:, 4 * i:4 * i + 4, :].rearrange("p c s -> p (c s)"), psum[count[0]][:, 0:4 * CAP],
                                         ACT.Copy).then_inc(sem(f"bank{count[0]}_read"), 1)

            def silu(count):
                count_filled(act, count)
                nc.scalar.activation(e_sg[0:CAP, :], psum[count[0]][0:CAP, 0:FC], ACT.Silu).then_inc(sem("expert_silu"), 1)

            def outputs(*counts_):
                for half, count in enumerate(counts_):
                    count_filled(act, count)
                    nc.scalar.activation(e_y[0][0:CAP, 512 * half:512 * half + 512], psum[half][0:CAP, :], ACT.Copy,
                                         scale=slot_gate[0:CAP, :]).then_inc(sem("y_high"), 1)

            def experts(k):
                def turn(t_, final):
                    T, n = (k, t_), t_ + TURNS * k
                    for j in range(NBODY):
                        u, fc = divmod(j, NF)
                        ahead2 = None if final and j + 2 >= NBODY else ((n, T, j + 2) if j + 2 < NBODY else (n + 1, (k, t_ + 1), j + 2 - NBODY))
                        if fc == 0:
                            outputs(*(e_count(T, u - 1, f"D{half}") for half in range(2)))
                        down_arrived(act, n, j)
                        chunk_done(act, T, j - 1)
                        split_high(raw_down[:, j % 2, :], down_hi, D_PARTS, "down_high")
                        e_filled(act, T, u, f"T{fc}")
                        nc.scalar.activation(e_hT[0][:, :, :].rearrange("p j t -> p (j t)"), e_bank(f"T{fc}")[:, 0:2 * CAP],
                                             ACT.Copy).then_inc(sem("hT_high"), 1)
                        if fc == 4:
                            e_filled(act, T, u, "ST")
                            nc.scalar.activation(scat[0:CAP, :, :].rearrange("p b t -> p (b t)"), e_bank("ST")[0:CAP, 0:S], ACT.Copy)
                            nc.scalar.activation(slot_gate[0:CAP, :], e_bank("ST")[0:CAP, S:S + 1], ACT.Copy).then_inc(e_read_sem("ST"), 1)
                        if ahead2:
                            gu_high(*ahead2, (0, 1))
                        if fc == 6 and not (final and u == 1):
                            tokens(e_xT[(u + 1) % 2][0], e_count(T, u + 1, "GH0"), e_count(T, u + 1, "GH1"))
                        if ahead2:
                            gu_high(*ahead2, (2, 3))
                        if not (final and j == NBODY - 1):
                            e_read(act, T, u, f"G{fc}")
                            silu(e_count(T, (j + 1) // NF, f"G{(j + 1) % NF}"))

                if k > 0:
                    for j in range(2):
                        gu_high(TURNS * k, (k, 0), j, range(GU_PARTS))
                tokens(e_xT[0][0], around[k]["GH0"], around[k]["GH1"])
                silu(around[k]["G0"])
                with act.Fori(0, TURNS - 1) as t_:
                    turn(t_, False)
                turn(TURNS - 1, True)
                outputs(*(e_count((k, TURNS - 1), 1, f"D{half}") for half in range(2)))

            experts(0)
            overflow(act, lambda: experts(1))
            act.wait_ge(sem("y_done"), 1)
            for b in range(TB):
                nc.scalar.activation(xs[:, b, :], x[:, b, :], ACT.Square,
                                     accum_out=square["final"][:, b:b + 1]).then_inc(sem("squares_final"), 1)

        @block.gpsimd
        def _(pool):
            pool.dma_start(consts[:, :], table).then_inc(sem("table_loaded"), 16)
            per_channel = {"mix0": a["norm_mix"][0], "mix1": a["norm_mix"][1], "mem0": a["norm_mem"][0],
                           "mem1": a["norm_mem"][1], "ffn0": a["norm_ffn"][0], "kv": a["norm_kv"]}
            nc.gpsimd.memset(gains["onorm"], 1.0).then_inc(sem("onorm_set"), 1)
            pool.wait_ge(sem("onorm_set"), 1)
            loads = [(gains[n], row.rearrange("(p c) -> p c", c=KC)) for n, row in per_channel.items()]
            rows = DV // KC
            loads += [(gains["onorm"][rows * h:rows * (h + 1), :], a["gla_onorm"][0].rearrange("(p c) -> p c", c=KC))
                      for h in range(GH)]
            loads += [(w2[0:RANK, :], a["w_gla_gate2"][0]), (w2[RANK:RANK + 1, :], a["b_gla_gate2"]),
                      (wf, cols(a["w_kv"], 1536, 1548)), (wr, cols(a["w_router"][0], 0, NE)),
                      (bf, a["b_forget"].rearrange("(a n) -> a n", a=1).partition_broadcast(P)),
                      (gain_row, a["norm_ffn"][1:2, :].partition_broadcast(P))]
            assert 16 * len(loads) == SMALL
            for dst, src in loads:
                pool.dma_start(dst, src).then_inc(sem("small_loaded"), 16)
            pool.wait_ge(sem("table_loaded"), 16)
            half = const("mhalf")
            for name in ("x", "mem", "gla", "ffn0", "kv", "ffn1", "final"):
                pool.wait_ge(sem(f"mean_{name}"), 1)
                dst, src = (o_rstd, o_mean) if name == "gla" else (rstd[name], mean[name])
                nc.gpsimd.tensor_tensor(dst, src, half[:, 0:dst.shape[1]], ALU.pow).then_inc(sem(f"rstd_{name}"), 1)

        @block.vector
        def _(dve):
            order = [0]

            def link(ins):
                order[0] += 1
                ins.then_inc(sem("dve_order"), 1)
                dve.wait_ge(sem("dve_order"), order[0])

            def evacuate(name, outs_ins):
                filled(dve, name)
                for o, i, sc in outs_ins:
                    last = nc.vector.tensor_copy(o, i) if sc is None else nc.vector.tensor_scalar(o, i, sc, None, ALU.mult)
                last.then_inc(read_sem(name), 1)

            def normed(name, src, dst, key):
                dve.wait_ge(sem(f"squares_{name}"), 2)
                nc.vector.tensor_scalar(mean[name], square[name], 1.0 / D, EPS, ALU.mult, ALU.add).then_inc(sem(f"mean_{name}"), 1)
                dve.wait_ge(sem(f"rstd_{name}"), 1)
                for b in range(TB):
                    nc.vector.tensor_scalar(dst[:, b, :], src[:, b, :], rstd[name][:, b:b + 1], None,
                                            ALU.mult).then_inc(sem(key), 1)

            nc.vector.memset(glrT[0:RANK + 1, :], 1.0)
            nc.vector.memset(pos[:, :, :], -1.0)
            nc.vector.memset(gate[:, :, :], 0.0)
            normed("x", x, xs, "xs_ready")
            dve.wait_ge(sem("small_loaded"), SMALL)

            def two_chunks(name, dst, gain, i):
                return [(dst[:, 2 * i + j, :], bank(name)[:, 256 * j:256 * j + 256], gains[gain][:, 2 * i + j:2 * i + j + 1])
                        for j in range(2)]

            def two_heads(name, dst):
                src = bank(name)[:, :].rearrange("p (a s) -> p a s", a=2)
                return [(dst[0:64, j::2, :], src[64 * j:64 * j + 64], None) for j in range(2)]

            for i in (1, 3):
                evacuate(f"TX{i}", two_chunks(f"TX{i}", hT, "mix0", i))
            normed("mem", mixed, mixed, "mem_ready")
            evacuate("GLR", [(glrT[0:RANK, :], bank("GLR")[0:RANK, 0:256], None)])
            for b in range(TB):
                evacuate(f"Z{b}", [(zz[:, 384 * b:384 * b + 384], bank(f"Z{b}")[:, 0:384], None)])
            read(dve, "Z1")
            nc.vector.scalar_tensor_tensor(ez, zz, -1.0, zz, ALU.mult, ALU.min).then_inc(sem("gate_abs"), 1)
            link(nc.vector.tensor_scalar(la, zz, 0.0, None, ALU.min))
            for i in (1, 3):
                evacuate(f"TM{i}", two_chunks(f"TM{i}", mT0, "mem0", i) + two_chunks(f"TM{i}", mT1, "mem1", i))
            dve.wait_ge(sem("gate_log"), 1)
            nc.vector.tensor_tensor(la, la, ez, ALU.subtract).then_inc(sem("log_gates"), 1)
            for i in range(2):
                evacuate(f"B{i}", [(bT[0:DK, 512 * i:512 * i + 512], bank(f"B{i}")[0:DK, :], None)])
            read(dve, "B1")

            def halves(tile, half):
                return tile[0:DK, :].rearrange("k (n two t) -> k n two t", two=2, t=half)

            def level_diff(n):
                half = CHUNK // 2 >> n
                bh, dh = halves(bT, half), halves(decay, half)
                mid = bh[:, :, 1, 0:1].to_broadcast([DK, S * GH // (2 * half), half])
                nc.vector.tensor_tensor(dh[:, :, 1, :], bh[:, :, 1, :], mid, ALU.subtract)
                nc.vector.tensor_tensor(dh[:, :, 0, :], mid, bh[:, :, 0, :], ALU.subtract).then_inc(sem("decay_diff"), 1)

            def level_prod(n):
                half = CHUNK // 2 >> n
                dh, ph = halves(decay, half), halves(prod[n % 2], half)
                dve.wait_ge(sem("decay_exp"), n + 1)
                if n == 0:
                    read(dve, "Q1"), read(dve, "K1")
                if n >= 2:
                    filled(dve, f"L{n - 2}_1")
                nc.vector.tensor_tensor(ph[:, :, 1, :], dh[:, :, 1, :], halves(qT, half)[:, :, 1, :], ALU.mult)
                nc.vector.tensor_tensor(ph[:, :, 0, :], dh[:, :, 0, :], halves(kT, half)[:, :, 0, :],
                                        ALU.mult).then_inc(sem("level_ready"), 1)
                dve.wait_ge(sem("level_ready"), n + 1)

            def level_mask(n):
                for b in range(TB):
                    filled(dve, f"L{n}_{b}")
                    src = bank(f"L{n}_{b}")[:, :].rearrange("s (h t) -> s h t", h=GH)
                    keep = ident if n == LEVELS else const("levels")[:, n * P:(n + 1) * P]
                    keep = keep.unsqueeze(1)
                    if n == 0:
                        ins = nc.vector.tensor_tensor(scoreT[:, b], src, keep.to_broadcast([P, GH, P]), ALU.mult)
                    else:
                        ins = nc.vector.copy_predicated(scoreT[:, b], keep.bitcast(U32).to_broadcast([P, GH, P]), src)
                    ins.then_inc(read_sem(f"L{n}_{b}"), 1)
                    read(dve, f"L{n}_{b}")

            def mem_max(layer, name, i):
                b, j = divmod(i, 2)
                filled(dve, name)
                part = m_max[layer][:, b, 2 * j:2 * j + 2]
                link(nc.vector.reduce_max(part, bank(name)[:, :].rearrange("p (h m) -> p h m", h=2), AX))
                nc.vector.tensor_scalar(part, part, -1.0, None, ALU.mult).then_inc(sem("mem_max"), 1)

            level_diff(0)
            evacuate("KM0", two_heads("KM0", kmT0))
            level_prod(0)
            level_diff(1)
            level_mask(0)
            level_prod(1)
            level_diff(2)
            level_mask(1)
            level_prod(2)
            level_diff(3)
            evacuate("V01", [(val[:, 0, 384:768], bank("V01")[:, 0:384], None)])
            evacuate("V11", [(val[:, 1, 384:768], bank("V11")[:, 0:384], None)])
            level_mask(2)
            level_prod(3)
            evacuate("KM1", two_heads("KM1", kmT1))
            level_diff(4)
            level_mask(3)
            level_prod(4)
            level_diff(5)
            level_mask(4)
            mem_max(0, "SM0", 0)
            mem_max(0, "SM1", 1)
            level_prod(5)
            nc.vector.tensor_copy(blast[0:DK, :], bT[0:DK, CHUNK - 1::CHUNK]).then_inc(sem("decay_diff"), 1)
            level_mask(5)
            mem_max(0, "SM2", 2)
            mem_max(0, "SM3", 3)
            level_mask(6)
            dve.wait_ge(sem("decay_exp"), LEVELS + 1)
            by_chunk = [P_.rearrange("k (n t) -> k n t", t=CHUNK) for P_ in (bT[0:DK, :],)][0]
            nc.vector.tensor_tensor(by_chunk, blast[0:DK, :].unsqueeze(2).to_broadcast([DK, S * GH // CHUNK, CHUNK]),
                                    by_chunk, ALU.subtract).then_inc(sem("key_diff"), 1)
            nc.vector.tensor_copy(alast[0:DK, :], decay[0:DK, CHUNK - 1::CHUNK])
            filled(dve, "L4_1")
            nc.vector.tensor_tensor(prod[0][0:DK, :], decay[0:DK, :], qT[0:DK, :], ALU.mult).then_inc(sem("query_prod"), 1)
            dve.wait_ge(sem("key_exp"), 1)
            filled(dve, "L5_1")
            nc.vector.tensor_tensor(prod[1][0:DK, :], bT[0:DK, :], kT[0:DK, :], ALU.mult).then_inc(sem("key_prod"), 1)
            for c in range(3):
                for i in range(2):
                    name = f"U{c}_{i}"
                    filled(dve, name)
                    if c == 0:
                        ins = nc.vector.tensor_copy(state[0:DK, 0, 2 * i:2 * i + 2, :].rearrange("k h v -> k (h v)"),
                                                    bank(name)[0:DK, 0:384])
                        if i == 0:
                            dve.wait_ge(sem("key_prod"), 1)
                    else:
                        for j in range(2):
                            h = 2 * i + j
                            ins = nc.vector.scalar_tensor_tensor(
                                state[0:DK, c, h, :], state[0:DK, c - 1, h, :], alast[0:DK, 4 * h + c:4 * h + c + 1],
                                bank(name)[0:DK, 192 * j:192 * j + 192], ALU.mult, ALU.add)
                    ins.then_inc(read_sem(name), 1)
                read(dve, f"U{c}_1")

            def memory_values(layer, name, scores):
                read(dve, scores)
                link(nc.vector.reciprocal(m_inv[layer], m_sum[layer]))
                filled(dve, name)
                inv = m_inv[layer].rearrange("p (b h) -> p b h", b=TB)
                for b in range(TB):
                    last = nc.vector.tensor_tensor(
                        mixed[:, b, MAIN:D].rearrange("p (h n) -> p h n", h=MH),
                        bank(name)[:, 256 * b:256 * b + 256].rearrange("p (h n) -> p h n", h=MH),
                        inv[:, b, :].unsqueeze(2).to_broadcast([P, MH, MD]), ALU.mult)
                last.then_inc(read_sem(name), 1)

            for i in (1, 3):
                evacuate(f"PM{i}", [(pmT0[:, i % 2, i // 2, :, :].rearrange("p h t -> p (h t)"), bank(f"PM{i}")[:, :], None)])
            memory_values(0, "MV", "SM3")
            dve.wait_ge(sem("o_squares"), 8)
            nc.vector.tensor_scalar(o_mean, o_sq, 1.0 / DV, EPS, ALU.mult, ALU.add).then_inc(sem("mean_gla"), 1)
            dve.wait_ge(sem("rstd_gla"), 1)
            read(dve, "R11")
            for b in range(TB):
                for i in range(2):
                    for h in (2 * i, 2 * i + 1):
                        part = mixed[:, b, DV * h:DV * (h + 1)]
                        last = nc.vector.scalar_tensor_tensor(part, bank(f"O{b}{i}")[:, DV * (h % 2):DV * (h % 2) + DV],
                                                              o_rstd[:, 4 * b + h:4 * b + h + 1], part, ALU.mult, ALU.mult)
                    last.then_inc(read_sem(f"O{b}{i}"), 1)
            for i in (1, 3):
                evacuate(f"TO{i}", two_chunks(f"TO{i}", hT, "onorm", i))

            def split_low(src, hi_, lo_, parts, what, count, which=None):
                n = src.shape[1] // parts
                for i in range(parts) if which is None else which:
                    at_ = slice(n * i, n * i + n)
                    dve.wait_ge(sem(f"{what}_high"), count + (i + 1))
                    nc.vector.tensor_tensor(lo_[:, at_], src[:, at_], hi_[:, at_].bitcast(F32),
                                            ALU.subtract).then_inc(sem(f"{what}_split"), 1)

            read(dve, "O11"), read(dve, "MV")
            split_low(raw[:, DENSE_GU[0], :], gu_hi[0], gu_lo[0], GU_PARTS, "gu", 0)
            split_low(raw_down[:, 0, :], down_hi, down_lo, D_PARTS, "down", 0)

            def add_to_stream(name, b, half):
                filled(dve, name)
                part = x[:, b, 512 * half:512 * half + 512]
                nc.vector.tensor_tensor(part, part, bank(name)[:, :], ALU.add).then_inc(read_sem(name), 1)

            for n_, half in (("WA", 0), ("WB", 1)):
                for b in range(TB):
                    add_to_stream(f"{n_}{b}", b, half)
            read(dve, "WB1")
            normed("ffn0", x, xs, "ffn0_ready")
            for i in range(4):
                filled(dve, f"TF{i}")
                dve.wait_ge(sem("dense_x_high"), i + 1)
                for (lo_, src, gain), (hi_, _, _) in zip(two_chunks(f"TF{i}", d_xT[1], "ffn0", i), two_chunks(f"TF{i}", d_xT[0], "ffn0", i)):
                    last = nc.vector.scalar_tensor_tensor(lo_, src, gain, hi_.bitcast(F32), ALU.mult, ALU.subtract)
                last.then_inc(read_sem(f"TF{i}"), 1)

            def dense_gu_low(fc, which):
                if fc < NF:
                    split_low(raw[:, DENSE_GU[fc], :], gu_hi[fc % 2], gu_lo[fc % 2], GU_PARTS, "gu", GU_PARTS * fc, which)

            def dense_product(fc, b):
                if fc > 0:
                    filled(dve, f"T{fc - 1}")
                dve.wait_ge(sem("dense_silu"), TB * fc + b + 1)
                nc.vector.tensor_tensor(d_h[:, b, :], d_sg[:, b, :], bank(f"G{fc}_{b}")[:, FC:2 * FC],
                                        ALU.mult).then_inc(read_sem(f"G{fc}_{b}"), 1)

            dense_gu_low(1, range(GU_PARTS))
            for b in range(TB):
                dense_product(0, b)
            for fc in range(NF):
                if fc > 0:
                    split_low(raw_down[:, fc % 2, :], down_hi, down_lo, D_PARTS, "down", D_PARTS * fc)
                dense_gu_low(fc + 2, (0, 1))
                dve.wait_ge(sem("dense_hT_high"), fc + 1)
                nc.vector.tensor_tensor(d_hT[1][:, :, :].rearrange("p j t -> p (j t)"), bank(f"T{fc}")[:, :],
                                        d_hT[0][:, :, :].rearrange("p j t -> p (j t)").bitcast(F32),
                                        ALU.subtract).then_inc(read_sem(f"T{fc}"), 1)
                if fc + 1 < NF:
                    dense_product(fc + 1, 0)
                dense_gu_low(fc + 2, (2, 3))
                if fc + 1 < NF:
                    dense_product(fc + 1, 1)
            for b in range(TB):
                for half in range(2):
                    add_to_stream(f"Y{2 * b + half}", b, half)
            read(dve, "Y3")
            normed("kv", x, xs, "kv_ready")
            for t_ in (fqT, fkT):
                nc.vector.memset(t_[64:66, :, :], 1.0).then_inc(sem("aug_set"), 1)
            for i in (1, 3):
                evacuate(f"TK{i}", two_chunks(f"TK{i}", hT, "kv", i) + two_chunks(f"TK{i}", hT2, "mix1", i))
            filled(dve, "FG")
            fzb = fz.rearrange("p (b h) -> p b h", b=TB)
            nc.vector.tensor_tensor(fzb, bank("FG")[:, 0:24].rearrange("p (b h) -> p b h", b=TB),
                                    bf.unsqueeze(1).to_broadcast([P, TB, FH]), ALU.add).then_inc(read_sem("FG"), 1)
            read(dve, "FG")
            nc.vector.scalar_tensor_tensor(fe, fz, -1.0, fz, ALU.mult, ALU.min).then_inc(sem("forget_abs"), 1)
            flat = fl.rearrange("p b h -> p (b h)")
            link(nc.vector.tensor_scalar(flat, fz, 0.0, None, ALU.min))
            dve.wait_ge(sem("forget_log"), 1)
            nc.vector.tensor_tensor(flat, flat, fe, ALU.subtract).then_inc(sem("log_forget"), 1)
            for b in range(TB):
                evacuate(f"FV{b}1", [(val[:, b, 384:768], bank(f"FV{b}1")[:, 0:384], None)])
            for i in range(4):
                mem_max(1, f"N{i}", i)
            fm = f_max.rearrange("p (h b) -> p h b", b=TB)
            for h in range(FH):
                filled(dve, f"S{h}")
                nc.vector.tensor_tensor(logits[:, h, :], bank(f"S{h}")[:, 0:384], const("causal"),
                                        ALU.add).then_inc(read_sem(f"S{h}"), 1)
                if h % 4 == 3:
                    read(dve, f"S{h}")
                    g_ = slice(h - 3, h + 1)
                    nc.vector.reduce_max(fm[:, g_, 0], logits[:, g_, 0:128], AX)
                    link(nc.vector.reduce_max(fm[:, g_, 1], logits[:, g_, 128:384], AX))
                    part = f_max[:, 2 * (h - 3):2 * (h + 1)]
                    nc.vector.tensor_scalar(part, part, -1.0, None, ALU.mult).then_inc(sem("fox_max"), 1)
            for i in (1, 3):
                evacuate(f"PN{i}", [(pmT1[:, i % 2, i // 2, :, :].rearrange("p h t -> p (h t)"), bank(f"PN{i}")[:, :], None)])
            memory_values(1, "MW", "N3")
            fi = f_inv.rearrange("p (h b) -> p b h", b=TB)

            def fox_values(g_):
                filled(dve, f"FO{g_}")
                for b in range(TB):
                    last = nc.vector.tensor_tensor(
                        mixed[:, b, 256 * g_:256 * g_ + 256].rearrange("p (h n) -> p h n", h=4),
                        bank(f"FO{g_}")[:, 256 * b:256 * b + 256].rearrange("p (h n) -> p h n", h=4),
                        fi[:, b, 4 * g_:4 * g_ + 4].unsqueeze(2).to_broadcast([P, 4, FD]), ALU.mult)
                last.then_inc(read_sem(f"FO{g_}"), 1)

            for h in range(1, FH, 2):
                if h >= 4:
                    fox_head_done(dve, h - 4)
                evacuate(f"PF{h}", [(probT[h % 4], bank(f"PF{h}")[:, 0:384], None)])
                if h == 5:
                    dve.wait_ge(sem("fox_exp"), 2 * FH)
                    link(nc.vector.reciprocal(f_inv, f_sum))
                if h >= 5 and (h - 5) % 4 == 0:
                    fox_values((h - 5) // 4)
            fox_values(2)
            for i in (1, 3):
                evacuate(f"TP{i}", [(hT[:, 2 * i:2 * i + 2, :].rearrange("p c s -> p (c s)"), bank(f"TP{i}")[:, :], None)])
            read(dve, "FO2"), read(dve, "MW")
            for j in range(2):
                split_low(raw[:, GU_SLOTS[j], :], gu_hi[j], gu_lo[j], GU_PARTS, "gu", GU_PARTS * (NF + j))
            for n_, half in (("XA", 0), ("XB", 1)):
                for b in range(TB):
                    add_to_stream(f"{n_}{b}", b, half)
            read(dve, "XB1")
            dve.wait_ge(sem("squares_ffn1"), 2)
            nc.vector.tensor_scalar(mean["ffn1"], square["ffn1"], 1.0 / D, EPS, ALU.mult, ALU.add).then_inc(sem("mean_ffn1"), 1)
            dve.wait_ge(sem("rstd_ffn1"), 1)
            for b in range(TB):
                nc.vector.scalar_tensor_tensor(xs[:, b, :], x[:, b, :], rstd["ffn1"][:, b:b + 1], gain_row,
                                               ALU.mult, ALU.mult).then_inc(sem("ffn1_ready"), 1)
            for b in range(TB):
                dve.wait_ge(sem("x_high"), b + 1)
                nc.vector.tensor_tensor(e_x[1][:, b, :], xs[:, b, :], e_x[0][:, b, :].bitcast(F32),
                                        ALU.subtract).then_inc(sem("x_split"), 1)
            for i in (1, 3):
                evacuate(f"TR{i}", [(hT[:, 2 * i:2 * i + 2, :].rearrange("p c s -> p (c s)"), bank(f"TR{i}")[:, :], None)])
            filled(dve, "RL")
            nc.vector.tensor_copy(lg[:, :, :].rearrange("p b e -> p (b e)"), bank("RL")[:, 0:16]).then_inc(read_sem("RL"), 1)
            read(dve, "RL")
            link(nc.vector.reduce_max(top, lg[:, :, :], AX))
            for b in range(TB):
                last = nc.vector.tensor_scalar(ex[:, b, :], lg[:, b, :], top[:, b:b + 1], None, ALU.subtract)
            last.then_inc(sem("logit_diff"), 1)
            for b in range(TB):
                mine = lg[:, b, :].unsqueeze(2).to_broadcast([P, NE, NE])
                other = lg[:, b, :].unsqueeze(1).to_broadcast([P, NE, NE])
                nc.vector.tensor_tensor(gt, other, mine, ALU.is_gt)
                link(nc.vector.tensor_tensor(eq, other, mine, ALU.is_equal))
                link(nc.vector.tensor_tensor(eq, eq, const("earlier").rearrange("p (e o) -> p e o", e=NE), ALU.mult))
                link(nc.vector.tensor_tensor(gt, gt, eq, ALU.add))
                link(nc.vector.reduce_sum(rank, gt, AX))
                ins = nc.vector.tensor_scalar(sel[:, b, :], rank, 1.5, None, ALU.is_lt)
                ins.then_inc(sem("chosen"), 1)
                dve.wait_ge(sem("chosen"), b + 1)
            dve.wait_ge(sem("logit_exp"), 1)
            link(nc.vector.tensor_tensor(ex[:, :, :], ex[:, :, :], sel[:, :, :], ALU.mult))
            link(nc.vector.reduce_sum(den, ex[:, :, :], AX))
            link(nc.vector.reciprocal(rden, den))
            nc.vector.tensor_tensor(gate[:, :, 0:NE], ex[:, :, :], rden.unsqueeze(2).to_broadcast([P, TB, NE]), ALU.mult)
            filled(dve, "POS")
            nc.vector.tensor_tensor(pos[:, :, 0:NE], bank("POS")[:, 0:16].rearrange("p (b e) -> p b e", b=TB), sel[:, :, :],
                                    ALU.mult).then_inc(read_sem("POS"), 1)
            read(dve, "POS")
            link(nc.vector.tensor_scalar(pos[:, :, 0:NE], pos[:, :, 0:NE], -1.0, None, ALU.add))
            filled(dve, "CNT")
            nc.vector.reduce_max(counts[0:1, 0:1], bank("CNT")[0:1, 0:8], AX).then_inc(read_sem("CNT"), 1)
            read(dve, "CNT")
            nc.vector.tensor_copy(over[0:1, 0:1], counts[0:1, 0:1]).then_inc(sem("overflow_known"), 1)

            def build(e, k):
                slots = const("slots")[:, CAP * k:CAP * (k + 1)]
                for dst in (perm, perm_r):
                    for b in range(TB):
                        last = nc.vector.tensor_scalar(dst[:, b, :], slots, pos[:, b, bass.ds(e, 1)], None, ALU.is_equal)
                last.then_inc(sem("perm_built"), 1)

            def tokens(dst, *counts_):
                for i, count in enumerate(counts_):
                    count_filled(dve, count)
                    nc.vector.tensor_copy(dst[:, 4 * i:4 * i + 4, :].rearrange("p c s -> p (c s)"),
                                          psum[count[0]][:, 0:4 * CAP]).then_inc(sem(f"bank{count[0]}_read"), 1)

            def product(n_silu, count):
                dve.wait_ge(sem("expert_silu"), n_silu)
                nc.vector.tensor_tensor(e_h[0:CAP, :], e_sg[0:CAP, :], psum[count[0]][0:CAP, FC:2 * FC],
                                        ALU.mult).then_inc(sem(f"bank{count[0]}_read"), 1)

            def outputs(n_high):
                for half in range(2):
                    dve.wait_ge(sem("y_high"), n_high + (half + 1))
                    at_ = slice(512 * half, 512 * half + 512)
                    nc.vector.scalar_tensor_tensor(e_y[1][0:CAP, at_], psum[half][0:CAP, :], slot_gate[0:CAP, :],
                                                   e_y[0][0:CAP, at_].bitcast(F32), ALU.mult,
                                                   ALU.subtract).then_inc(sem(f"bank{half}_read"), 1)

            def scattered(counts_, parts=(0, 1, 2, 3)):
                for q, count in zip(parts, counts_):
                    b, half = divmod(q, 2)
                    count_filled(dve, count)
                    part = x[:, b, 512 * half:512 * half + 512]
                    nc.vector.tensor_tensor(part, part, e_bank(f"SC{q}")[:, :], ALU.add).then_inc(e_read_sem(f"SC{q}"), 1)

            def experts(k):
                def turn(t_, final):
                    T, n = (k, t_), t_ + TURNS * k
                    for j in range(NBODY):
                        u, fc = divmod(j, NF)
                        ahead2 = None if final and j + 2 >= NBODY else ((n, j + 2) if j + 2 < NBODY else (n + 1, j + 2 - NBODY))

                        def gu_low(which):
                            if ahead2:
                                m_, i = ahead2
                                split_low(raw[:, GU_SLOTS[i], :], gu_hi[i % 2], gu_lo[i % 2], GU_PARTS, "gu",
                                          chunk_no(m_, i) * GU_PARTS, which)

                        if fc == 0:
                            outputs(n * 4 + (2 * k + 2 * u))
                        split_low(raw_down[:, j % 2, :], down_hi, down_lo, D_PARTS, "down", chunk_no(n, j) * D_PARTS)
                        dve.wait_ge(sem("hT_high"), n * NBODY + (j + 1))
                        nc.vector.tensor_tensor(e_hT[1][:, :, :].rearrange("p j t -> p (j t)"), e_bank(f"T{fc}")[:, 0:2 * CAP],
                                                e_hT[0][:, :, :].rearrange("p j t -> p (j t)").bitcast(F32),
                                                ALU.subtract).then_inc(e_read_sem(f"T{fc}"), 1)
                        gu_low((0, 1))
                        if fc in (2, 3):
                            parts = (2 * fc - 4, 2 * fc - 3)
                            scattered([e_count(T, u, f"SC{q}") for q in parts], parts)
                        if not (final and u == 1):
                            if fc == 4:
                                e_filled(dve, T, u, "ST")
                                build(t_ * 2 + (u + 1), k)
                            if fc == 7:
                                tokens(e_xT[(u + 1) % 2][1], e_count(T, u + 1, "GL0"), e_count(T, u + 1, "GL1"))
                        gu_low((2, 3))
                        if not (final and j == NBODY - 1):
                            e_filled(dve, T, u, f"T{fc}")
                            product(n * NBODY + (j + 2), e_count(T, (j + 1) // NF, f"G{(j + 1) % NF}"))

                if k == 0:
                    filled(dve, "TR3")
                    dve.wait_ge(sem("x_split"), 2)
                else:
                    count_filled(dve, around[0]["SC3"])
                    count_read(dve, around[0]["SC3"])
                for t_ in (*e_y, scat[:, :, :].rearrange("p b t -> p (b t)")):
                    n_ = t_.shape[1] // P
                    nc.vector.tensor_scalar(t_.rearrange("p (a n) -> p a n", a=n_), const("ones").unsqueeze(1).to_broadcast([P, n_, P]),
                                            0.0, None, ALU.mult)
                nc.vector.memset(slot_gate, 0.0).then_inc(sem("scatter_cleared"), 1)
                build(0, k)
                if k > 0:
                    for j in range(2):
                        split_low(raw[:, GU_SLOTS[j], :], gu_hi[j], gu_lo[j], GU_PARTS, "gu", chunk_no(TURNS * k, j) * GU_PARTS)
                tokens(e_xT[0][1], around[k]["GL0"], around[k]["GL1"])
                product(TURNS * k * NBODY + 1, around[k]["G0"])
                with dve.Fori(0, TURNS - 1) as t_:
                    turn(t_, False)
                turn(TURNS - 1, True)
                outputs((TURNS * (k + 1)) * 4 + 2 * k)
                scattered([around[k][f"SC{q}"] for q in range(4)])
                dve.wait_ge(sem("final_gain_loaded"), 16 * (k + 1))

            experts(0)
            overflow(dve, lambda: experts(1))
            nc.vector.memset(counts[0:1, 8:16], 0.0).then_inc(sem("y_done"), 1)
            dve.wait_ge(sem("squares_final"), 2)
            nc.vector.tensor_scalar(mean["final"], square["final"], 1.0 / D, EPS, ALU.mult, ALU.add).then_inc(sem("mean_final"), 1)
            dve.wait_ge(sem("rstd_final"), 1)
            for b in range(TB):
                nc.vector.scalar_tensor_tensor(xs[:, b, :], x[:, b, :], rstd["final"][:, b:b + 1], final_gain,
                                               ALU.mult, ALU.mult).then_inc(sem("out_ready"), 1)

        @block.tensor
        def _(pe):
            mm = nc.tensor.matmul

            def by_chunk(tile, b, c):
                return tile[:, b, :].rearrange("t (p c) -> t c p", c=KC)[:, c, :]

            def tok(b):
                return slice(b * P, (b + 1) * P)

            def transposes(prefix, src):
                for i in range(4):
                    name = f"{prefix}{i}"
                    free(pe, name)
                    for j in range(2):
                        for b in range(TB):
                            last = nc.tensor.transpose(bank(name)[:, (2 * j + b) * P:(2 * j + b + 1) * P],
                                                       by_chunk(src, b, 2 * i + j), ident)
                    last.then_inc(full_sem(name), 1)

            def project(name, groups):
                free(pe, name)
                for o, lhs, rhs in groups:
                    for c in range(KC):
                        last = mm(o, lhs(c), rhs(c), start=(c == 0), stop=(c == KC - 1))
                last.then_inc(full_sem(name), 1)

            def tokens_by(name, b, src, wt, lo, n, at_=0):
                project(name, [(bank(name)[:, at_:at_ + n], lambda c: src[:, c, tok(b)], lambda c: wt[:, c, lo:lo + n])])

            def columns_by(name, src, wt, los, n):
                project(name, [(bank(name)[0:n, 256 * j:256 * j + 256], lambda c, lo=lo: wt[:, c, lo:lo + n],
                                lambda c: src[:, c, :]) for j, lo in enumerate(los)])

            pe.wait_ge(sem("table_loaded"), 16)
            pe.wait_ge(sem("xs_ready"), 2)
            transposes("TX", xs)
            for i in range(4):
                read(pe, f"TX{i}")
            wgm = weights(pe, "gates")
            columns_by("GLR", hT, wgm, [0], RANK)
            pe.wait_ge(sem("small_loaded"), SMALL)
            read(pe, "GLR")
            for b in range(TB):
                free(pe, f"Z{b}")
                mm(bank(f"Z{b}")[:, 0:384], glrT[0:RANK + 1, tok(b)], w2[0:RANK + 1, :], start=True,
                   stop=True).then_inc(full_sem(f"Z{b}"), 1)
            for n_ in ("q", "k"):
                wt = weights(pe, n_)
                for i in range(2):
                    columns_by(f"{n_.upper()}{i}", hT, wt, [DK * 2 * i, DK * (2 * i + 1)], DK)
            pe.wait_ge(sem("mem_ready"), 2)
            transposes("TM", mixed)
            pe.wait_ge(sem("log_gates"), 1)
            for i in range(2):
                free(pe, f"B{i}")
                for j in range(2):
                    for b in range(TB):
                        lo = DK * (2 * i + j)
                        last = mm(bank(f"B{i}")[0:DK, 256 * j + P * b:256 * j + P * b + P], la_v[:, b, lo:lo + DK],
                                  const("tri16"), start=True, stop=True)
                last.then_inc(full_sem(f"B{i}"), 1)
            columns_by("MQ", hT, wgm, [16, 144], P)
            for i in range(4):
                read(pe, f"TM{i}")
            wkv = weights(pe, "mem0")
            columns_by("KM0", mT0, wkv, [0, P], P)

            def memory_values_of(name, src, wt):
                project(name, [(bank(name)[:, 256 * b:256 * b + 256], lambda c, b=b: src[:, c, tok(b)],
                                lambda c: wt[:, c, 256:512]) for b in range(TB)])

            memory_values_of("VM0", mT0, wkv)

            def level(n):
                if n < LEVELS:
                    pe.wait_ge(sem("level_ready"), n + 1)
                for b in range(TB):
                    free(pe, f"L{n}_{b}")
                    for h in range(GH):
                        at_ = slice(S * h + P * b, S * h + P * b + P)
                        lhs, rhs = (kT, qT) if n == LEVELS else (prod[n % 2], prod[n % 2])
                        last = mm(bank(f"L{n}_{b}")[:, P * h:P * h + P], lhs[0:DK, at_], rhs[0:DK, at_], start=True, stop=True)
                    last.then_inc(full_sem(f"L{n}_{b}"), 1)

            def memory_scores(name, i, q, k_):
                b, j = divmod(i, 2)
                free(pe, name)
                for h in range(2):
                    last = mm(bank(name)[:, 256 * h:256 * h + 256], q[0:64, 2 * j + h, tok(b)], k_[0:64, 2 * j + h, :],
                              start=True, stop=True)
                last.then_inc(full_sem(name), 1)

            level(0)
            for i in range(2):
                wv = weights(pe, f"v{i}")
                for b in range(TB):
                    tokens_by(f"V{b}{i}", b, hT, wv, 0, 384)
                level(i + 1)
            wkv1 = weights(pe, "mem1")
            columns_by("KM1", mT1, wkv1, [0, P], P)
            level(3)
            memory_values_of("VM1", mT1, wkv1)
            level(4)
            read(pe, "MQ"), read(pe, "KM0")
            memory_scores("SM0", 0, mqT0, kmT0)
            memory_scores("SM1", 1, mqT0, kmT0)
            level(5)
            memory_scores("SM2", 2, mqT0, kmT0)
            memory_scores("SM3", 3, mqT0, kmT0)
            level(6)
            pe.wait_ge(sem("key_prod"), 1)
            for b in range(TB):
                free(pe, f"KH{b}")
                for h in range(GH):
                    last = nc.tensor.transpose(bank(f"KH{b}")[:, DK * h:DK * h + DK], prod[1][0:DK, S * h + P * b:S * h + P * b + P],
                                               ident[0:DK, 0:DK])
                last.then_inc(full_sem(f"KH{b}"), 1)
            for i in range(2):
                wr_ = weights(pe, f"r{i}")
                for b in range(TB):
                    tokens_by(f"R{b}{i}", b, hT, wr_, 0, 384)
            read(pe, "KH0"), read(pe, "KH1")
            for b in range(TB):
                read(pe, f"V{b}0"), read(pe, f"V{b}1")
            for c in range(3):
                b, r = c // 2, slice(64 * (c % 2), 64 * (c % 2) + 64)
                for i in range(2):
                    free(pe, f"U{c}_{i}")
                    for j in range(2):
                        h = 2 * i + j
                        last = mm(bank(f"U{c}_{i}")[0:DK, DV * j:DV * j + DV], khat[r, b, h, :], val[r, b, DV * h:DV * (h + 1)],
                                  start=True, stop=True)
                    last.then_inc(full_sem(f"U{c}_{i}"), 1)

            def memory_transposes(prefix, probs):
                for i in range(4):
                    b, mc = divmod(i, 2)
                    name = f"{prefix}{i}"
                    free(pe, name)
                    for h in range(MH):
                        last = nc.tensor.transpose(bank(name)[:, P * h:P * h + P], probs[:, b, h, P * mc:P * mc + P], ident)
                    last.then_inc(full_sem(name), 1)

            def memory_outputs(name, prefix, probsT, vm):
                for i in range(4):
                    read(pe, f"{prefix}{i}")
                free(pe, name)
                for b in range(TB):
                    for h in range(MH):
                        for mc in range(2):
                            last = mm(bank(name)[:, 256 * b + MD * h:256 * b + MD * h + MD], probsT[:, mc, b, h, :],
                                      vm[:, mc, MD * h:MD * h + MD], start=(mc == 0), stop=(mc == 1))
                last.then_inc(full_sem(name), 1)

            for i in range(4):
                read(pe, f"SM{i}")
            memory_transposes("PM", pm0)
            memory_outputs("MV", "PM", pmT0, vm0)
            read(pe, "L6_1"), read(pe, "U2_1")
            for b in range(TB):
                for i in range(2):
                    free(pe, f"O{b}{i}")
                    for j in range(2):
                        h = 2 * i + j
                        for c in (2 * b, 2 * b + 1):
                            r = slice(64 * (c % 2), 64 * (c % 2) + 64)
                            o = bank(f"O{b}{i}")[r, DV * j:DV * j + DV]
                            last = mm(o, scoreT[:, b, h, r], val[:, b, DV * h:DV * (h + 1)], start=True, stop=(c == 0))
                            if c > 0:
                                last = mm(o, prod[0][0:DK, S * h + CHUNK * c:S * h + CHUNK * (c + 1)],
                                          state[0:DK, c - 1, h, :], start=False, stop=True)
                    last.then_inc(full_sem(f"O{b}{i}"), 1)

            def output_projection(prefix, units):
                for unit_, n_ in zip(units, "AB"):
                    wt = weights(pe, unit_)
                    for b in range(TB):
                        tokens_by(f"{prefix}{n_}{b}", b, hT, wt, 0, 512)

            read(pe, "O11"), read(pe, "MV")
            transposes("TO", mixed)
            for i in range(4):
                read(pe, f"TO{i}")
            output_projection("W", ("out0a", "out0b"))
            pe.wait_ge(sem("ffn0_ready"), 2)
            transposes("TF", xs)
            for i in range(4):
                read(pe, f"TF{i}")

            def three(o, lhs, rhs, first, last_):
                mm(o, lhs[0], rhs[0], start=first, stop=False)
                mm(o, lhs[0], rhs[1], start=False, stop=False)
                return mm(o, lhs[1], rhs[0], start=False, stop=last_)

            gate_up = [[t_.rearrange("p (a c n) -> p c a n", a=2, c=KC) for t_ in pair] for pair in zip(gu_hi, gu_lo)]
            down_w = [t_.rearrange("p (j n) -> p j n", j=2) for t_ in (down_hi, down_lo)]

            def dense_up(fc, b):
                pe.wait_ge(sem("gu_split"), GU_PARTS * (fc + 1))
                name, wt = f"G{fc}_{b}", gate_up[fc % 2]
                free(pe, name)
                for c in range(KC):
                    last = three(bank(name)[:, :].rearrange("p (a n) -> p a n", a=2), [t_[:, c, tok(b)] for t_ in d_xT],
                                 [t_[:, c] for t_ in wt], c == 0, c == KC - 1)
                last.then_inc(full_sem(name), 1)

            dense_up(0, 0)
            dense_up(0, 1)
            for fc in range(NF):
                if fc < NF - 1:
                    dense_up(fc + 1, 0)
                read(pe, f"G{fc}_0"), read(pe, f"G{fc}_1")
                free(pe, f"T{fc}")
                for j in range(2):
                    for b in range(TB):
                        last = nc.tensor.transpose(bank(f"T{fc}")[:, (2 * j + b) * P:(2 * j + b + 1) * P], d_h[:, b, j::2], ident)
                last.then_inc(full_sem(f"T{fc}"), 1)
                if fc < NF - 1:
                    dense_up(fc + 1, 1)
                read(pe, f"T{fc}")
                pe.wait_ge(sem("down_split"), D_PARTS * (fc + 1))
                for b in range(TB):
                    for half in range(2):
                        name, at_ = f"Y{2 * b + half}", slice(512 * half, 512 * half + 512)
                        if fc == 0:
                            free(pe, name)
                        for j in range(2):
                            last = three(bank(name)[:, :], [t_[:, j, tok(b)] for t_ in d_hT], [t_[:, j, at_] for t_ in down_w],
                                         fc == 0 and j == 0, fc == NF - 1 and j == 1)
                        if fc == NF - 1:
                            last.then_inc(full_sem(name), 1)
                if fc < NF - 1:
                    last.then_inc(sem("dense_chunks"), 1)

            pe.wait_ge(sem("kv_ready"), 2)
            transposes("TK", xs)
            for i in range(4):
                read(pe, f"TK{i}")
            project("FG", [(bank("FG")[:, FH * b:FH * b + FH], lambda c, b=b: hT[:, c, tok(b)], lambda c: wf[:, c, :])
                           for b in range(TB)])
            def head_pairs(prefix, units, src):
                wts = [weights(pe, units[0])]
                for i in range(3):
                    if i == 1:
                        wts.append(weights(pe, units[1]))
                    name = f"{prefix}{i}"
                    project(name, [(bank(name)[:, 256 * j:256 * j + 256],
                                    lambda c, q_=2 * i + j: wts[q_ // 3][:, c, P * (q_ % 3):P * (q_ % 3) + P],
                                    lambda c: src[:, c, :]) for j in range(2)])

            head_pairs("FK", ("fk0", "fk1"), hT)
            pe.wait_ge(sem("log_forget"), 1)
            free(pe, "CC")
            mm(bank("CC")[0:FH, 0:P], fl[:, 0, :], const("tri"), start=True, stop=True)
            mm(bank("CC")[0:FH, P:2 * P], fl[:, 0, :], const("ones"), start=True, stop=False)
            mm(bank("CC")[0:FH, P:2 * P], fl[:, 1, :], const("tri"), start=False, stop=True).then_inc(full_sem("CC"), 1)
            for i in range(2):
                wt = weights(pe, f"fv{i}")
                for b in range(TB):
                    tokens_by(f"FV{b}{i}", b, hT, wt, 0, 384)
            head_pairs("FQ", ("fq0", "fq1"), hT2)
            columns_by("MQ1", hT2, weights(pe, "fmq"), [0, P], P)
            read(pe, "MQ1"), read(pe, "KM1"), read(pe, "VM1")
            for i in range(4):
                memory_scores(f"N{i}", i, mqT1, kmT1)
            pe.wait_ge(sem("aug_loaded"), 32)
            read(pe, "FQ2"), read(pe, "FK2")
            for h in range(FH):
                name = f"S{h}"
                free(pe, name)
                mm(bank(name)[:, 0:P], fqT[0:66, h, 0:P], fkT[0:66, h, 0:P], start=True, stop=True)
                mm(bank(name)[:, P:3 * P], fqT[0:66, h, P:S], fkT[0:66, h, :], start=True, stop=True).then_inc(full_sem(name), 1)
            for i in range(4):
                read(pe, f"N{i}")
            memory_transposes("PN", pm1)
            memory_outputs("MW", "PN", pmT1, vm1)

            def fox_output(h):
                read(pe, f"PF{h}")
                g_, hh = divmod(h, 4)
                if hh == 0:
                    free(pe, f"FO{g_}")
                vh = [val[:, b, FD * h:FD * h + FD] for b in range(TB)]
                mm(bank(f"FO{g_}")[:, FD * hh:FD * hh + FD], probT[hh][:, 0:P], vh[0], start=True, stop=True)
                o = bank(f"FO{g_}")[:, 256 + FD * hh:256 + FD * hh + FD]
                mm(o, probT[hh][:, P:2 * P], vh[0], start=True, stop=False)
                mm(o, probT[hh][:, 2 * P:3 * P], vh[1], start=False,
                   stop=True).then_inc(full_sem(f"FO{g_}") if hh == 3 else sem("fox_heads"), 1)

            for b in range(TB):
                read(pe, f"FV{b}0"), read(pe, f"FV{b}1")
            for h in range(FH):
                free(pe, f"PF{h}")
                pe.wait_ge(sem("fox_exp"), 2 * h + 2)
                for i in range(3):
                    last = nc.tensor.transpose(bank(f"PF{h}")[:, P * i:P * i + P], logits[:, h, P * i:P * i + P], ident)
                last.then_inc(full_sem(f"PF{h}"), 1)
                if h >= 2:
                    fox_output(h - 2)
            fox_output(FH - 2)
            fox_output(FH - 1)
            read(pe, "FO2"), read(pe, "MW")
            transposes("TP", mixed)
            for i in range(4):
                read(pe, f"TP{i}")
            output_projection("X", ("out1a", "out1b"))
            pe.wait_ge(sem("ffn1_ready"), 2)
            transposes("TR", xs)
            for i in range(4):
                read(pe, f"TR{i}")
            project("RL", [(bank("RL")[:, NE * b:NE * b + NE], lambda c, b=b: hT[:, c, tok(b)], lambda c: wr[:, c, :])
                           for b in range(TB)])
            pe.wait_ge(sem("chosen"), 2)
            free(pe, "POS")
            mm(bank("POS")[:, 0:NE], const("tri"), sel[:, 0, :], start=True, stop=True)
            mm(bank("POS")[:, NE:2 * NE], const("ones"), sel[:, 0, :], start=True, stop=False)
            mm(bank("POS")[:, NE:2 * NE], const("tri"), sel[:, 1, :], start=False, stop=True).then_inc(full_sem("POS"), 1)
            free(pe, "CNT")
            for b in range(TB):
                last = mm(bank("CNT")[0:1, 0:NE], const("ones")[:, 0:1], sel[:, b, :], start=(b == 0), stop=(b == 1))
            last.then_inc(full_sem("CNT"), 1)

            def gather(parts, n_built):
                pe.wait_ge(sem("perm_built"), n_built)
                for name, count in parts:
                    src, i = e_x["HL".index(name[1])], int(name[2])
                    count_read(pe, count)
                    for c in range(4):
                        for b in range(TB):
                            last = mm(psum[count[0]][:, CAP * c:CAP * (c + 1)], by_chunk(src, b, 4 * i + c), perm_r[:, b, :],
                                      start=(b == 0), stop=(b == 1))
                    last.then_inc(sem(f"bank{count[0]}_full"), 1)

            def scatter(parts):
                for q, count in parts:
                    b, half = divmod(q, 2)
                    count_read(pe, count)
                    for i in range(2):
                        last = mm(psum[count[0]][:, :], scat[0:CAP, b, :], e_y[i][0:CAP, 512 * half:512 * half + 512],
                                  start=(i == 0), stop=(i == 1))
                    last.then_inc(sem(f"bank{count[0]}_full"), 1)

            PARTS = ("GH0", "GH1", "GL0", "GL1")

            def former(count):
                return count[0], count[1] - 1

            def up(n, j, count, chunks):
                if 0 in chunks:
                    pe.wait_ge(sem("gu_split"), (chunk_no(n, j) + 1) * GU_PARTS)
                    count_read(pe, former(count))
                for c in chunks:
                    last = three(psum[count[0]][0:CAP, :].rearrange("p (a n) -> p a n", a=2),
                                 [t_[:, c, :] for t_ in e_xT[j // NF % 2]], [t_[:, c] for t_ in gate_up[j % 2]], c == 0, c == KC - 1)
                if KC - 1 in chunks:
                    last.then_inc(sem(f"bank{count[0]}_full"), 1)

            def experts(k):
                def turn(t_, final):
                    T, n = (k, t_), t_ + TURNS * k
                    for j in range(NBODY):
                        u, fc = divmod(j, NF)
                        alone = final and j == NBODY - 1
                        v_ = (j + 1) // NF
                        following = e_count(T, v_, f"G{(j + 1) % NF}")
                        if fc == NF - 1 and not alone:
                            for name in PARTS:
                                e_read(pe, T, u + 1, name)
                        if not alone:
                            up(n, j + 1, following, range(2))
                        e_read(pe, T, u, f"G{fc}")
                        e_free(pe, T, u, f"T{fc}")
                        for i in range(2):
                            last = nc.tensor.transpose(e_bank(f"T{fc}")[:, CAP * i:CAP * (i + 1)], e_h[0:CAP, i::2],
                                                       ident[0:CAP, 0:CAP])
                        last.then_inc(e_full_sem(f"T{fc}"), 1)
                        if not alone:
                            up(n, j + 1, following, range(2, KC))
                        e_read(pe, T, u, f"T{fc}")
                        pe.wait_ge(sem("down_split"), (chunk_no(n, j) + 1) * D_PARTS)
                        for half in range(2):
                            if fc == 0:
                                e_free(pe, T, u, f"D{half}")
                            for i in range(2):
                                last = three(psum[half][0:CAP, :], [t_[:, i, :] for t_ in e_hT],
                                             [t_[:, i, 512 * half:512 * half + 512] for t_ in down_w],
                                             fc == 0 and i == 0, fc == NF - 1 and i == 1)
                            if fc == NF - 1:
                                last.then_inc(sem(f"bank{half}_full"), 1)
                        if fc < NF - 1:
                            last.then_inc(sem("expert_chunks"), 1)
                        if fc in (1, 2):
                            scatter([(q, e_count(T, u, f"SC{q}", less=1)) for q in (2 * fc - 2, 2 * fc - 1)])
                        if fc == 3:
                            e_free(pe, T, u, "ST")
                            for b in range(TB):
                                nc.tensor.transpose(e_bank("ST")[0:CAP, P * b:P * b + P], perm[:, b, :], ident)
                            for b in range(TB):
                                last = mm(e_bank("ST")[0:CAP, S:S + 1], perm[:, b, :], gate[:, b, bass.ds(t_ * 2 + u, 1)],
                                          start=(b == 0), stop=(b == 1))
                            last.then_inc(e_full_sem("ST"), 1)
                        if fc in (5, 6) and not (final and u == 1):
                            names = PARTS[0:2] if fc == 5 else PARTS[2:4]
                            gather([(name, e_count(T, u + 1, name, less=1)) for name in names], t_ * 2 + (NE * k + u + 2))

                pe.wait_ge(sem("x_split"), 2)
                pe.wait_ge(sem("scatter_cleared"), k + 1)
                gather([(name, former(around[k][name])) for name in PARTS], NE * k + 1)
                for half in range(2):
                    count_read(pe, former(around[k][f"D{half}"]))
                    mm(psum[half][0:CAP, :], scat[:, 0, :], e_y[0][:, 512 * half:512 * half + 512], start=True,
                       stop=True).then_inc(sem(f"bank{half}_full"), 1)
                for name in PARTS:
                    count_read(pe, around[k][name])
                up(TURNS * k, 0, around[k]["G0"], range(KC))
                with pe.Fori(0, TURNS - 1) as t_:
                    turn(t_, False)
                turn(TURNS - 1, True)
                e_read(pe, (k, TURNS), -1, "D0"), e_read(pe, (k, TURNS), -1, "D1")
                scatter([(q, former(around[k][f"SC{q}"])) for q in range(4)])

            experts(0)
            overflow(pe, lambda: experts(1))


_INS = ["x", "mem", "norm_mix", "norm_mem", "norm_ffn", "norm_kv", "norm_final", "w_in_a", "w_gla_gate2", "b_gla_gate2",
        "gla_onorm", "w_in_b", "w_kv", "b_forget", "w_mem_kv", "w_out", "w_ff_gate", "w_ff_up", "w_ff_down", "w_router",
        "w_moe_gate", "w_moe_up", "w_moe_down"]


def kernel(**inputs):
    import concourse.bacc as _bacc
    from concourse.bass_utils import run_bass_kernel_spmd as _run

    nc = _bacc.Bacc("TRN2", target_bir_lowering=False, num_devices=1)
    arrays, args = {}, {}
    for name in _INS:
        arr = np.ascontiguousarray(inputs[name])
        arrays[f"in_{name}"] = arr
        args[name] = nc.dram_tensor(f"in_{name}", arr.shape, mybir.dt.from_np(arr.dtype), kind="ExternalInput").ap()
    arrays["in_table"] = constant_table()
    table = nc.dram_tensor("in_table", arrays["in_table"].shape, F32, kind="ExternalInput").ap()
    out = nc.dram_tensor("out", (1, S, D), F32, kind="ExternalOutput").ap()
    program(nc, args, table, out)
    return _run(nc, [arrays], core_ids=[0]).results[0]["out"]
```

```python
import concourse.bass as bass
from concourse import mybir
from contextlib import ExitStack
import numpy as np

F32 = mybir.dt.float32
F32R = mybir.dt.float32r
I32 = mybir.dt.int32
U32 = mybir.dt.uint32
ALU = mybir.AluOpType
ACT = mybir.ActivationFunctionType
AX = mybir.AxisListType.X

P = 128
D = 1024
KC = D // P
S = 256
TB = S // P
EPS = 1e-6
MAIN = 768
MEMW = 256
MH, MD = 4, 64
GH, DK, DV = 4, 96, 192
RANK = 16
CHUNK = 64
LEVELS = 6
FH, FD = 12, 64
DFF = 2816
FC = 256
NF = DFF // FC
NE = 8
CAP = 128
UNIT = 4096
DOWN = 2048
NBODY = 2 * NF
TURNS = NE // 2
GU_SLOTS = (0, 1, 2) * 6 + (0, 1, 0, 2)
GU_PARTS, D_PARTS = 4, 2
NEG = -1e30


def constant_columns():
    at, cols = {}, 0
    for name, n in (("ident", P), ("tri16", P), ("tri", P), ("ones", P), ("levels", LEVELS * P),
                    ("causal", 3 * P), ("slots", 2 * P), ("earlier", NE * NE), ("mhalf", 8)):
        at[name] = (cols, n)
        cols += n
    return at, cols


def constant_table():
    at, cols = constant_columns()
    c = np.zeros((P, cols), np.float32)
    i = np.arange(P)
    s, t = i[:, None], i[None, :]

    def put(name, value):
        c[:, at[name][0]:at[name][0] + at[name][1]] = value

    put("ident", s == t)
    put("tri16", ((s <= t) & (s // CHUNK == t // CHUNK)) / 16.0)
    put("tri", s <= t)
    put("ones", 1.0)
    put("levels", np.concatenate(
        [(s // (2 * h) == t // (2 * h)) & (s % (2 * h) < h) & (t % (2 * h) >= h)
         for h in (CHUNK // 2 >> n for n in range(LEVELS))], axis=1))
    later = np.where(t <= s, 0.0, NEG)
    put("causal", np.concatenate([later, 0.0 * later, later], axis=1))
    put("slots", np.arange(2 * P)[None, :])
    e = np.arange(NE)
    put("earlier", (e[None, :] < e[:, None]).reshape(1, -1))
    put("mhalf", -0.5)
    return c


def early_jobs():
    names = [f"TX{i}" for i in range(4)] + ["GLR", "Z0", "Z1", "Q0", "Q1", "K0", "K1"]
    names += [f"TM{i}" for i in range(4)] + ["MQ", "B0", "B1", "KM0", "VM0"]
    names += ["V00", "V10", "L0_0", "L0_1", "V01", "V11", "L1_0", "L1_1", "KM1", "L2_0", "L2_1", "VM1", "L3_0", "L3_1"]
    names += ["SM0", "SM1", "R00", "L4_0", "L4_1", "R10", "SM2", "SM3", "L5_0", "L5_1", "R01", "R11", "L6_0", "L6_1"]
    names += ["KH0", "KH1"]
    names += [f"U{c}_{hp}" for c in range(3) for hp in range(2)]
    names += ["O00", "O01", "O10", "O11"] + [f"PM{i}" for i in range(4)] + ["MV"]
    names += [f"TO{i}" for i in range(4)] + ["WA0", "WB0", "WA1", "WB1"]
    names += [f"TF{i}" for i in range(4)]
    jobs = [(n, names.index("PM0") % 8 if n == "MV" else i % 8) for i, n in enumerate(names)]
    jobs += [(f"Y{i}", i) for i in range(4)]
    for f in range(NF):
        jobs += [(f"G{f}_{b}", 4 + b) for b in range(TB)] + [(f"T{f}", 6 + f % 2)]
    names = [f"TK{i}" for i in range(4)] + ["FG", "FK0", "FK1", "FK2", "CC"]
    names += ["FV00", "FV10", "FV01", "FV11", "FQ0", "FQ1", "FQ2", "MQ1"]
    names += [f"N{i}" for i in range(4)]
    names += [f"S{h}" for h in range(FH)] + [f"PN{i}" for i in range(4)]
    for h in range(FH):
        names += [f"PF{h}"] + ([f"FO{(h - 2) // 4}"] if h >= 2 and (h - 2) % 4 == 0 else []) + ["MW"] * (h == 4)
    names += [f"TP{i}" for i in range(4)] + ["XA0", "XB0", "XA1", "XB1"]
    names += [f"TR{i}" for i in range(4)] + ["RL", "POS", "CNT"]
    jobs += [(n, i % 8) for i, n in enumerate(names)]
    return jobs


def expert_jobs():
    jobs = []
    for u in range(2):
        jobs += [((u, f"D{half}"), half) for half in range(2)]
        for fc in range(NF):
            jobs += [((u, f"T{fc}"), 4)]
            jobs += [((u + 1, "G0") if fc == NF - 1 else (u, f"G{fc + 1}"), g_bank(NF * u + fc + 1))]
        jobs += [((u, "SC0"), 5), ((u, "SC1"), 6), ((u, "SC2"), 7), ((u, "SC3"), 5), ((u, "ST"), 6)]
        jobs += [((u + 1, "GH0"), 7), ((u + 1, "GH1"), 5), ((u + 1, "GL0"), 6), ((u + 1, "GL1"), 7)]
    return jobs


def g_bank(j):
    return 2 + j % 2


GAINS = ("mix0", "mem0", "mem1", "mix1", "ffn0", "kv", "onorm")
PACKED = {name: (KC * i, KC) for i, name in enumerate(GAINS)}
PACKED |= {"wf": (64, KC * FH), "wr": (64 + KC * FH, KC * NE), "bf": (64 + KC * (FH + NE), FH)}
PACKED_COLUMNS = 240


def packed(inputs):
    c = np.zeros((P, PACKED_COLUMNS), np.float32)
    rows = {"mix0": inputs["norm_mix"][0], "mix1": inputs["norm_mix"][1], "mem0": inputs["norm_mem"][0],
            "mem1": inputs["norm_mem"][1], "ffn0": inputs["norm_ffn"][0], "kv": inputs["norm_kv"],
            "onorm": np.concatenate([np.tile(inputs["gla_onorm"][0], GH), np.ones(MEMW, np.float32)]),
            "wf": inputs["w_kv"][:, 2 * MAIN:], "wr": inputs["w_router"][0]}
    for name, value in rows.items():
        lo, n = PACKED[name]
        c[:, lo:lo + n] = np.reshape(value, (P, n))
    lo, n = PACKED["bf"]
    c[:, lo:lo + n] = inputs["b_forget"]
    return c


def program(nc, a, table, params, out):
    at, ncols = constant_columns()
    ctx = ExitStack()
    with ctx:
        base = (nc.sbuf_base + 63) // 64 * 64

        def place(name, at_, n, dt=F32):
            return nc.alloc_sbuf_tensor_at(name, [P, n], dt, offset=base + 4 * at_)[:, :]

        sems = {}

        def sem(name):
            if name not in sems:
                sems[name] = ctx.enter_context(nc.semaphore(name))
            return sems[name]

        X, CONST, SMALLS, ROW = 0, 2048, 4096, 4736
        XS, MIXED, HT, EXTRA = 5760, 7808, 9856, 11904
        RAW, SPLIT = 16104, 16104 + 4 * UNIT
        assert ncols <= 2048 and base + 4 * (SPLIT + 4 * UNIT + 2 * DOWN) <= nc.sbuf_usable_end
        consts = place("consts", CONST, ncols)
        x = place("x", X, TB * D).rearrange("p (b d) -> p b d", b=TB)
        xs = place("xs", XS, TB * D).rearrange("p (b d) -> p b d", b=TB)
        hT = place("hT", HT, KC * S).rearrange("p (c s) -> p c s", c=KC)
        mixed = place("mixed", MIXED, TB * D).rearrange("p (b d) -> p b d", b=TB)
        extra = place("extra", EXTRA, 4200)
        small = place("small", SMALLS, 640)
        gain_row = place("gain_row", ROW, D)
        raw = place("raw", RAW, 4 * UNIT).rearrange("p (s n) -> p s n", s=4)
        raw_down = raw[:, 3, :].rearrange("p (s n) -> p s n", s=2)
        arena = place("arena", SPLIT, 4 * UNIT + 2 * DOWN)
        gu_hi, gu_lo = ([place(f"gu_{n_}{i}", SPLIT + (2 * i + j) * UNIT, UNIT, F32R) for i in range(2)]
                        for j, n_ in enumerate(("hi", "lo")))
        down_hi, down_lo = (place(f"down_{n_}", SPLIT + 4 * UNIT + j * DOWN, DOWN, F32R)
                            for j, n_ in enumerate(("hi", "lo")))
        psum = [ctx.enter_context(nc.psum_tensor(f"bank{i}", [P, 512], F32)) for i in range(8)]
        counts = place("counts", SMALLS + 600, 16)
        over = place("over", SMALLS + 616, 2, I32)

        class Carve:
            def __init__(self, base):
                self.base, self.n = base, 0

            def __call__(self, n, at=None):
                lo = self.n if at is None else at
                self.n = lo + n
                assert self.n <= self.base.shape[1], (self.n, self.base.shape)
                return self.base[:, lo:lo + n]

        def const(name):
            lo, n = at[name]
            return consts[:, lo:lo + n]

        ident = const("ident")
        g = Carve(arena)
        mT0 = g(2048).rearrange("p (c s) -> p c s", c=KC)
        mT1 = g(2048).rearrange("p (c s) -> p c s", c=KC)
        zbuf = g(2304)
        qT, kT, bT = (g(1024) for _ in range(3))
        decay = g(1024)
        prod = [g(1024), g(1024)]
        scoreT = g(1024).rearrange("p (b h t) -> p b h t", b=TB, h=GH)
        khat = g(768).rearrange("p (b h k) -> p b h k", b=TB, h=GH)
        kmT0 = g(1024).rearrange("p (h s) -> p h s", h=MH)
        mqT0 = g(1024).rearrange("p (h s) -> p h s", h=MH)
        vm0 = g(512).rearrange("p (b n) -> p b n", b=TB)
        alast, blast = g(16), g(16)
        zz, ez, la = (zbuf[:, 768 * i:768 * i + 768] for i in range(3))
        la_v = la.rearrange("p (b n) -> p b n", b=TB)
        state = zbuf.rearrange("p (c h v) -> p c h v", c=3, h=GH)
        pm0 = mT0.rearrange("p c s -> p (c s)").rearrange("p (b h m) -> p b h m", b=TB, h=MH)
        pmT0 = mT1.rearrange("p c s -> p (c s)").rearrange("p (m b h t) -> p m b h t", m=2, b=TB, h=MH)

        f = Carve(arena)
        fqT = f(FH * S).rearrange("p (h s) -> p h s", h=FH)
        fkT = f(FH * S).rearrange("p (h s) -> p h s", h=FH)
        logits = f(FH * 384).rearrange("p (h s) -> p h s", h=FH)
        probT = [f(384) for _ in range(4)]
        cT = f(256)
        negcT = f(256)
        hT2 = logits[:, 0:6, :].rearrange("p h s -> p (h s)")[:, 0:KC * S].rearrange("p (c s) -> p c s", c=KC)
        mqT1 = f(1024).rearrange("p (h s) -> p h s", h=MH)
        pm1 = f(2048).rearrange("p (b h m) -> p b h m", b=TB, h=MH)
        pmT1 = f(2048).rearrange("p (m b h t) -> p m b h t", m=2, b=TB, h=MH)

        def split_tile(name, hi_at, lo_at, n):
            return place(name + "_hi", hi_at, n, F32R), place(name + "_lo", lo_at, n, F32R)

        d_xT = [t_.rearrange("p (c s) -> p c s", c=KC) for t_ in split_tile("dense_xT", HT, MIXED, KC * S)]
        d_sg = place("dense_silu", XS, 512).rearrange("p (b n) -> p b n", b=TB)
        d_h = place("dense_h", XS + 512, 512).rearrange("p (b n) -> p b n", b=TB)
        d_hT = [t_.rearrange("p (j t) -> p j t", j=2) for t_ in split_tile("dense_hT", XS + 1024, XS + 1536, 512)]

        v = Carve(extra)
        kmT1 = v(1024).rearrange("p (h s) -> p h s", h=MH)
        vm1 = v(512).rearrange("p (b n) -> p b n", b=TB)
        val = v(1536).rearrange("p (b n) -> p b n", b=TB)
        glrT = v(256)
        w2 = v(384)
        pack = v(PACKED_COLUMNS, at=3936)

        e_x = [t_.rearrange("p (b d) -> p b d", b=TB) for t_ in split_tile("expert_x", MIXED, EXTRA, TB * D)]
        e_xT = [[t_.rearrange("p (c s) -> p c s", c=KC) for t_ in split_tile(f"expert_xT{i}", hi_at, lo_at, KC * CAP)]
                for i, (hi_at, lo_at) in enumerate(((HT, HT + KC * CAP), (ROW, CONST + at["levels"][0])))]
        assert KC * CAP <= at["levels"][1] + at["causal"][1] and KC * CAP <= D
        final_gain = raw[:, 1, 0:D]
        e_y = list(split_tile("expert_y", XS, XS + D, D))
        at_ = EXTRA + TB * D
        e_sg, e_h = place("expert_silu", at_, FC), place("expert_h", at_ + FC, FC)
        e_hT = [t_.rearrange("p (j t) -> p j t", j=2) for t_ in split_tile("expert_hT", at_ + 512, at_ + 768, 2 * CAP)]
        perm = place("perm", at_ + 1024, TB * CAP).rearrange("p (b s) -> p b s", b=TB)
        perm_r = place("perm_r", at_ + 1280, TB * CAP, F32R).rearrange("p (b s) -> p b s", b=TB)
        scat = place("scat", at_ + 1536, S, F32R).rearrange("p (b t) -> p b t", b=TB)
        slot_gate = place("slot_gate", SMALLS + 624, 2)[:, 0:1]

        w = Carve(small)

        def parameter(name):
            lo, n = PACKED[name]
            return pack[:, lo:lo + n]

        gains = {n: parameter(n) for n in GAINS}
        wf = parameter("wf").rearrange("p (c n) -> p c n", c=KC)
        wr = parameter("wr").rearrange("p (c n) -> p c n", c=KC)
        bf = parameter("bf")
        square = {n: w(2) for n in ("x", "mem", "ffn0", "kv", "ffn1", "final")}
        mean = {n: w(2) for n in square}
        rstd = {n: w(2) for n in square}
        o_sq, o_mean, o_rstd = (w(8) for _ in range(3))
        m_max = [w(8).rearrange("p (b h) -> p b h", b=TB) for _ in range(2)]
        m_sum = [w(8) for _ in range(2)]
        m_inv = [w(8) for _ in range(2)]
        f_max, f_sum, f_inv = (w(24) for _ in range(3))
        fz, fe = w(24), w(24)
        fl = w(24).rearrange("p (b h) -> p b h", b=TB)
        lg, ex, sel = (w(16).rearrange("p (b e) -> p b e", b=TB) for _ in range(3))
        gt, eq = (gain_row[:, i * TB * NE * NE:(i + 1) * TB * NE * NE].rearrange("p (b e o) -> p b e o", b=TB, e=NE) for i in range(2))
        top, den, rden = w(2), w(2), w(2)
        pos = w(16).rearrange("p (b e) -> p b e", b=TB)
        gate = w(16).rearrange("p (b e) -> p b e", b=TB)
        rank = w(16).rearrange("p (b e) -> p b e", b=TB)

        assert w.n <= 600
        fill, fills = {}, [0] * 8
        for name, bank in early_jobs():
            fills[bank] += 1
            fill[name] = (bank, fills[bank])
        per, e_fill = [0] * 8, {}
        for name, b in expert_jobs():
            per[b] += 1
            e_fill[name] = (b, per[b])
        start, around = [], []
        for k in range(2):
            once = {}
            for name, b in (("GH0", 7), ("GH1", 5), ("GL0", 6), ("GL1", 7), ("G0", g_bank(0)), ("D0", 0), ("D1", 1)):
                fills[b] += 1
                once[name] = (b, fills[b])
            start.append(list(fills))
            fills = [n + TURNS * m_ for n, m_ in zip(fills, per)]
            for (u, name), b in expert_jobs():
                fills[b] -= u == 2
            for name, b in (("SC0", 5), ("SC1", 6), ("SC2", 7), ("SC3", 5)):
                fills[b] += 1
                once[name] = (b, fills[b])
            around.append(once)

        def bank(name):
            return psum[fill[name][0]]

        def filled(eng, name):
            b, n = fill[name]
            eng.wait_ge(sem(f"bank{b}_full"), n)

        def read(eng, name):
            b, n = fill[name]
            eng.wait_ge(sem(f"bank{b}_read"), n)

        def free(eng, name):
            b, n = fill[name]
            if n > 1:
                eng.wait_ge(sem(f"bank{b}_read"), n - 1)

        def full_sem(name):
            return sem(f"bank{fill[name][0]}_full")

        def read_sem(name):
            return sem(f"bank{fill[name][0]}_read")

        def e_count(T, u, name, less=0):
            (k, t_), turns = T, 0
            while (u, name) not in e_fill or u < 0:
                u, turns = u + 2, turns + 1
            b, i = e_fill[u, name]
            i += start[k][b] - turns * per[b] - less
            assert i > 0
            return b, t_ * per[b] + i

        def count_filled(eng, count):
            eng.wait_ge(sem(f"bank{count[0]}_full"), count[1])

        def count_read(eng, count):
            eng.wait_ge(sem(f"bank{count[0]}_read"), count[1])

        def e_filled(eng, T, u, name):
            count_filled(eng, e_count(T, u, name))

        def e_read(eng, T, u, name):
            count_read(eng, e_count(T, u, name))

        def e_free(eng, T, u, name):
            count_read(eng, e_count(T, u, name, less=1))

        def e_place(name):
            return e_fill[0, name][0]

        def e_bank(name):
            return psum[e_place(name)]

        def e_full_sem(name):
            return sem(f"bank{e_place(name)}_full")

        def e_read_sem(name):
            return sem(f"bank{e_place(name)}_read")

        def chunk_done(eng, T, j):
            u, fc = divmod(j, NF)
            if fc == NF - 1:
                e_filled(eng, T, u, "D1")
            else:
                n = T[1] + TURNS * T[0]
                eng.wait_ge(sem("expert_chunks"), n * (2 * (NF - 1)) + ((NF - 1) * u + fc + 1))

        def chunk_no(n, j):
            return n * NBODY + (NF + j)

        def cols(wt, lo, hi):
            return wt.rearrange("(p c) n -> p c n", c=KC)[:, :, lo:hi]

        w_in_a, w_in_b = a["w_in_a"][0], a["w_in_b"][0]
        GLA_UNITS = [
            ("gates", 0, cols(w_in_a, 2304, 2576), "MQ"),
            ("q", 1, cols(w_in_a, 0, 384), "Q1"),
            ("k", 2, cols(w_in_a, 384, 768), "K1"),
            ("mem0", 3, cols(a["w_mem_kv"][0], 0, 512), "VM0"),
            ("v0", 1, cols(w_in_a, 768, 1152), "V10"),
            ("v1", 2, cols(w_in_a, 1152, 1536), "V11"),
            ("mem1", 0, cols(a["w_mem_kv"][1], 0, 512), "VM1"),
            ("r0", 3, cols(w_in_a, 1536, 1920), "R10"),
            ("r1", 1, cols(w_in_a, 1920, 2304), "R11"),
            ("out0a", 2, cols(a["w_out"][0], 0, 512), "WA1"),
            ("out0b", 0, cols(a["w_out"][0], 512, 1024), "WB1"),
        ]
        FOX_UNITS = [
            ("fk0", 0, cols(a["w_kv"], 0, 384), "FK1"),
            ("fk1", 1, cols(a["w_kv"], 384, 768), "FK2"),
            ("fv0", 2, cols(a["w_kv"], 768, 1152), "FV10"),
            ("fv1", 3, cols(a["w_kv"], 1152, 1536), "FV11"),
            ("fq0", 0, cols(w_in_b, 0, 384), "FQ1"),
            ("fq1", 1, cols(w_in_b, 384, 768), "FQ2"),
            ("fmq", 2, cols(w_in_b, 768, 1024), "MQ1"),
            ("out1a", 3, cols(a["w_out"][1], 0, 512), "XA1"),
            ("out1b", 2, cols(a["w_out"][1], 512, 1024), "XB1"),
        ]
        DENSE_GU = [(1 + f_) % 3 for f_ in range(NF)]
        arrived, unit_slot, loaded = {}, {}, [0] * 4
        for name, s_, _, _ in GLA_UNITS:
            loaded[s_] += 16
            arrived[name], unit_slot[name] = loaded[s_], s_
        for f_ in range(NF):
            loaded[DENSE_GU[f_]] += 32
            arrived[f"gu{f_}"] = loaded[DENSE_GU[f_]]
        for name, s_, _, _ in FOX_UNITS:
            loaded[s_] += 16
            arrived[name], unit_slot[name] = loaded[s_], s_
        DENSE_DOWN = [16 * (f_ // 2 + 1) for f_ in range(NF)]
        down_loaded = [16 * len(range(s_, NF, 2)) for s_ in range(2)]

        def weights(eng, name):
            s_ = unit_slot[name]
            eng.wait_ge(sem(f"raw{s_}_loaded"), arrived[name])
            src = next(u[2] for u in GLA_UNITS + FOX_UNITS if u[0] == name)
            return piece(raw[:, s_, :], 0, KC, src.shape[2])

        def piece(slot, lo, nc_, n):
            return slot[:, lo:lo + nc_ * n].rearrange("p (c n) -> p c n", c=nc_)

        def gu_arrived(eng, n, j):
            s_ = GU_SLOTS[j]
            eng.wait_ge(sem(f"raw{s_}_loaded"), n * (32 * GU_SLOTS.count(s_)) + (loaded[s_] + 32 * GU_SLOTS[:j + 1].count(s_)))
            return raw[:, s_, :]

        def dense_gu_arrived(eng, fc):
            eng.wait_ge(sem(f"raw{DENSE_GU[fc]}_loaded"), arrived[f"gu{fc}"])

        def down_arrived(eng, n, j):
            s_ = j % 2
            eng.wait_ge(sem(f"down{s_}_loaded"), n * (16 * NF) + (down_loaded[s_] + 16 * (j // 2 + 1)))
            return raw_down[:, s_, :]

        def fox_head_done(eng, h):
            if h % 4 == 3:
                filled(eng, f"FO{h // 4}")
            else:
                eng.wait_ge(sem("fox_heads"), 3 * (h // 4) + h % 4 + 1)

        def overflow(eng, second_pass):
            eng.wait_ge(sem("overflow_known"), 1)
            most = eng.value_load(over[0:1, 0:1], min_val=0, max_val=S)
            with eng.If(most > CAP):
                second_pass()

        block = ctx.enter_context(nc.Block())

        @block.sync
        def _(sp):
            def unit(name, s_, src):
                n = src.shape[2]
                sp.dma_start(piece(raw[:, s_, :], 0, KC, n), src).then_inc(sem(f"raw{s_}_loaded"), 16)

            def gate_up(s_, wg, wu):
                for i, src in enumerate((wg, wu)):
                    sp.dma_start(piece(raw[:, s_, :], 2048 * i, KC, FC), src).then_inc(sem(f"raw{s_}_loaded"), 16)

            def down(s_, wd):
                sp.dma_start(raw_down[:, s_, :].rearrange("p (j n) -> p j n", j=2), wd).then_inc(sem(f"down{s_}_loaded"), 16)

            DENSE_LAG, LAG = 3, 2

            def dense_downs(f_):
                return {0: [0], 1: [], 2: [1], 3: [], 4: [], NF - 1: list(range(NF - 1 - DENSE_LAG, NF))}.get(f_, [f_ - DENSE_LAG])

            sp.dma_start(x[:, :, :], a["x"].rearrange("a (b p) d -> p (a b) d", p=P)).then_inc(sem("x_loaded"), 16)
            sp.dma_start(pack, params).then_inc(sem("small_loaded"), 16)
            last = {}
            for name, s_, src, job in GLA_UNITS:
                if s_ in last:
                    filled(sp, last[s_])
                unit(name, s_, src)
                last[s_] = job
            wg, wu, wd = a["w_ff_gate"][0], a["w_ff_up"][0], a["w_ff_down"][0]
            for f_ in range(NF):
                s_ = DENSE_GU[f_]
                if f_ < 3:
                    filled(sp, last[s_])
                else:
                    sp.wait_ge(sem("gu_split"), GU_PARTS * (f_ - 2))
                gate_up(s_, cols(wg, f_ * FC, (f_ + 1) * FC), cols(wu, f_ * FC, (f_ + 1) * FC))
                for i in dense_downs(f_):
                    if i == 0:
                        filled(sp, last[3])
                    elif i >= 2:
                        sp.wait_ge(sem("down_split"), D_PARTS * (i - 1))
                    down(i % 2, wd[i * FC:(i + 1) * FC, :].rearrange("(p j) n -> p j n", j=2))
            last = {}
            for name, s_, src, job in FOX_UNITS:
                if s_ in last:
                    filled(sp, last[s_])
                elif s_ == 3:
                    sp.wait_ge(sem("down_split"), D_PARTS * NF)
                else:
                    was = max(f_ for f_ in range(NF) if DENSE_GU[f_] == s_)
                    sp.wait_ge(sem("gu_split"), GU_PARTS * (was + 1))
                unit(name, s_, src)
                last[s_] = job

            def expert_gate_up(e, j):
                lo = (j % NF) * FC
                gate_up(GU_SLOTS[j], *(a[wt][0, bass.ds(e, 1), :, lo:lo + FC].rearrange("a (p c) n -> (a p) c n", c=KC)
                                       for wt in ("w_moe_gate", "w_moe_up")))

            def expert_down(e, j):
                lo = (j % NF) * FC
                down(j % 2, a["w_moe_down"][0, bass.ds(e, 1), lo:lo + FC, :].rearrange("a (p j) n -> (a p) j n", j=2))

            AHEAD = 4

            def load_gate_up(n, t_, j, first):
                s_ = GU_SLOTS[j]
                was = max(i for i in range(j - NBODY, j) if GU_SLOTS[i] == s_)
                if not first or was >= 0:
                    sp.wait_ge(sem("gu_split"), (chunk_no(n, was) + 1) * GU_PARTS)
                else:
                    filled(sp, last[s_])
                expert_gate_up(t_ * 2 + j // NF, j)

            def load_down(n, t_, j, first=False):
                if not first or j >= 2:
                    sp.wait_ge(sem("down_split"), (chunk_no(n, j - 2) + 1) * D_PARTS)
                elif j == 0:
                    filled(sp, last[3])
                expert_down(t_ * 2 + j // NF, j)

            def experts(k):
                n = TURNS * k
                if k > 0:
                    sp.wait_ge(sem("final_gain_loaded"), 16)
                for j in (0, 1, 3):
                    load_gate_up(n, 0, j, k == 0)
                for j in range(AHEAD - LAG):
                    load_down(n, 0, j, k == 0)
                load_gate_up(n, 0, 2, k == 0)

                def turn(t_, final):
                    n = t_ + TURNS * k
                    for j in range(AHEAD, NBODY):
                        load_down(n, t_, j - LAG)
                        load_gate_up(n, t_, j, False)
                    if final:
                        for j in range(NBODY - LAG, NBODY):
                            load_down(n, t_, j)
                    else:
                        following = t_ + (TURNS * k + 1), t_ + 1
                        for j in range(AHEAD):
                            if j < LAG:
                                load_down(n, t_, NBODY - LAG + j)
                            else:
                                load_down(*following, j - LAG)
                            load_gate_up(*following, j, False)

                with sp.Fori(0, TURNS - 1) as t_:
                    turn(t_, False)
                turn(TURNS - 1, True)
                was = max(j for j in range(NBODY) if GU_SLOTS[j] == 1)
                sp.wait_ge(sem("gu_split"), (chunk_no(TURNS * k + TURNS - 1, was) + 1) * GU_PARTS)
                sp.dma_start(final_gain, a["norm_final"].rearrange("(a n) -> a n", a=1).partition_broadcast(P)).then_inc(
                    sem("final_gain_loaded"), 16)

            experts(0)
            overflow(sp, lambda: experts(1))
            for b in range(TB):
                sp.wait_ge(sem("out_ready"), b + 1)
                sp.dma_start(out[0, b * P:(b + 1) * P, :], xs[:, b, :]).then_inc(sem("stored"), 16)
            sp.wait_ge(sem("stored"), 32)

        @block.scalar
        def _(act):
            act.dma_start(consts[:, :], table).then_inc(sem("table_loaded"), 16)
            act.dma_start(mixed[:, :, :], a["mem"].rearrange("a (b p) d -> p (a b) d", p=P)).then_inc(sem("mem_loaded"), 16)

            def evacuate(name, outs_ins):
                filled(act, name)
                for o, i, sc in outs_ins:
                    last = nc.scalar.activation(o, i, ACT.Copy, scale=sc)
                last.then_inc(read_sem(name), 1)

            def split_high(src, dst, parts, done, which=None):
                n = src.shape[1] // parts
                for i in range(parts) if which is None else which:
                    nc.scalar.activation(dst[:, n * i:n * i + n], src[:, n * i:n * i + n], ACT.Copy).then_inc(sem(done), 1)

            for name, src in (("x", x), ("mem", mixed)):
                act.wait_ge(sem(f"{name}_loaded"), 16)
                for b in range(TB):
                    if name == "mem":
                        act.wait_ge(sem("squares_x"), b + 1)
                    nc.scalar.activation(prod[b], src[:, b, :], ACT.Square,
                                         accum_out=square[name][:, b:b + 1]).then_inc(sem(f"squares_{name}"), 1)

            act.wait_ge(sem("small_loaded"), 16)
            def two_chunks(name, dst, gain, i):
                return [(dst[:, 2 * i + j, :], bank(name)[:, 256 * j:256 * j + 256], gains[gain][:, 2 * i + j:2 * i + j + 1])
                        for j in range(2)]
            for i in (0, 2):
                evacuate(f"TX{i}", two_chunks(f"TX{i}", hT, "mix0", i))
            act.wait_ge(sem("gate_abs"), 1)
            nc.scalar.activation(ez, ez, ACT.Exp).then_inc(sem("gate_exp"), 1)
            act.wait_ge(sem("gate_exp"), 1)
            nc.scalar.activation(ez, ez, ACT.Ln, bias=1.0).then_inc(sem("gate_log"), 1)
            for i in range(2):
                evacuate(f"Q{i}", [(qT[0:DK, 512 * i:512 * i + 512], bank(f"Q{i}")[0:DK, :], DK ** -0.5)])
            for i in range(2):
                evacuate(f"K{i}", [(kT[0:DK, 512 * i:512 * i + 512], bank(f"K{i}")[0:DK, :], 1.0)])
            for i in (0, 2):
                evacuate(f"TM{i}", two_chunks(f"TM{i}", mT0, "mem0", i) + two_chunks(f"TM{i}", mT1, "mem1", i))

            def two_heads(name, dst, scale):
                src = bank(name)[:, :].rearrange("p (a s) -> p a s", a=2)
                return [(dst[0:64, j::2, :], src[64 * j:64 * j + 64], scale) for j in range(2)]

            evacuate("MQ", two_heads("MQ", mqT0, MD ** -0.5))
            evacuate("VM0", [(vm0[:, :, :].rearrange("p b n -> p (b n)"), bank("VM0")[:, :], 1.0)])

            def level_exp(n):
                act.wait_ge(sem("decay_diff"), n + 1)
                nc.scalar.activation(decay[0:DK, :], decay[0:DK, :], ACT.Exp).then_inc(sem("decay_exp"), 1)

            def softmax_mem(layer, name, i, first):
                b, j = divmod(i, 2)
                act.wait_ge(sem("mem_max"), first + i + 1)
                pmx, p_ = m_max[layer], (pm0, pm1)[layer]
                for h in range(2):
                    last = nc.scalar.activation(p_[:, b, 2 * j + h, :], bank(name)[:, 256 * h:256 * h + 256], ACT.Exp,
                                                bias=pmx[:, b, 2 * j + h:2 * j + h + 1],
                                                accum_out=m_sum[layer][:, 4 * b + 2 * j + h:4 * b + 2 * j + h + 1])
                last.then_inc(read_sem(name), 1)

            def output_gate(b, i):
                if b + i == 0:
                    read(act, "TM3")
                evacuate(f"R{b}{i}", [(mixed[:, b, 384 * i:384 * i + 384], bank(f"R{b}{i}")[:, 0:384], 1.0)])

            level_exp(0)
            evacuate("V00", [(val[:, 0, 0:384], bank("V00")[:, 0:384], 1.0)])
            evacuate("V10", [(val[:, 1, 0:384], bank("V10")[:, 0:384], 1.0)])
            level_exp(1)
            level_exp(2)
            level_exp(3)
            evacuate("VM1", [(vm1[:, :, :].rearrange("p b n -> p (b n)"), bank("VM1")[:, :], 1.0)])
            level_exp(4)
            level_exp(5)
            softmax_mem(0, "SM0", 0, 0)
            softmax_mem(0, "SM1", 1, 0)
            output_gate(0, 0)
            output_gate(1, 0)
            softmax_mem(0, "SM2", 2, 0)
            softmax_mem(0, "SM3", 3, 0)
            act.wait_ge(sem("decay_diff"), LEVELS + 1)
            nc.scalar.activation(decay[0:DK, :], bT[0:DK, :], ACT.Exp).then_inc(sem("decay_exp"), 1)
            act.wait_ge(sem("key_diff"), 1)
            nc.scalar.activation(bT[0:DK, :], bT[0:DK, :], ACT.Exp).then_inc(sem("key_exp"), 1)
            output_gate(0, 1)
            output_gate(1, 1)
            evacuate("KH0", [(khat[:, 0, :, :].rearrange("p h k -> p (h k)"), bank("KH0")[:, 0:384], 1.0)])
            evacuate("KH1", [(khat[:, 1, :, :].rearrange("p h k -> p (h k)"), bank("KH1")[:, 0:384], 1.0)])
            read(act, "R11")
            for b in range(TB):
                nc.scalar.activation(mixed[:, b, 0:MAIN], mixed[:, b, 0:MAIN], ACT.Silu).then_inc(sem("output_gates"), 1)
            act.wait_ge(sem("key_prod"), 1)
            for b in range(TB):
                for i in range(2):
                    filled(act, f"O{b}{i}")
                    for h in range(2):
                        n = 4 * b + 2 * i + h
                        nc.scalar.activation(decay[:, 192 * (n % 4):192 * (n % 4) + 192], bank(f"O{b}{i}")[:, 192 * h:192 * h + 192],
                                             ACT.Square, accum_out=o_sq[:, n:n + 1]).then_inc(sem("o_squares"), 1)
                    if b == 0 and i == 1:
                        act.wait_ge(sem("o_squares"), 4)
                if b == 0:
                    for i in (0, 2):
                        evacuate(f"PM{i}", [(pmT0[:, i % 2, i // 2, :, :].rearrange("p h t -> p (h t)"), bank(f"PM{i}")[:, :], 1.0)])
            for i in (0, 2):
                evacuate(f"TO{i}", two_chunks(f"TO{i}", hT, "onorm", i))
            act.wait_ge(sem("o_squares"), 8)
            read(act, "O11"), read(act, "MV")
            dense_gu_arrived(act, 0)
            split_high(raw[:, DENSE_GU[0], :], gu_hi[0], GU_PARTS, "gu_high")
            act.wait_ge(sem("down0_loaded"), DENSE_DOWN[0])
            split_high(raw_down[:, 0, :], down_hi, D_PARTS, "down_high")

            def x_squares(name, last):
                for b in range(TB):
                    read(act, last[b])
                    nc.scalar.activation(xs[:, b, :], x[:, b, :], ACT.Square,
                                         accum_out=square[name][:, b:b + 1]).then_inc(sem(f"squares_{name}"), 1)
            x_squares("ffn0", ("WB0", "WB1"))
            for i in range(4):
                filled(act, f"TF{i}")
                for o, src, gain in two_chunks(f"TF{i}", d_xT[0], "ffn0", i):
                    last = nc.scalar.activation(o, src, ACT.Copy, scale=gain)
                last.then_inc(sem("dense_x_high"), 1)

            def dense_gu_high(fc, which):
                if fc >= NF:
                    return
                if 0 in which:
                    dense_gu_arrived(act, fc)
                    if fc >= 2:
                        filled(act, f"G{fc - 2}_1")
                split_high(raw[:, DENSE_GU[fc], :], gu_hi[fc % 2], GU_PARTS, "gu_high", which)

            def dense_down_high(fc):
                if fc >= NF:
                    return
                act.wait_ge(sem(f"down{fc % 2}_loaded"), DENSE_DOWN[fc])
                if fc > 0:
                    act.wait_ge(sem("dense_chunks"), fc)
                split_high(raw_down[:, fc % 2, :], down_hi, D_PARTS, "down_high")

            def dense_silu(fc, b):
                filled(act, f"G{fc}_{b}")
                if fc > 0:
                    read(act, f"G{fc - 1}_{b}")
                nc.scalar.activation(d_sg[:, b, :], bank(f"G{fc}_{b}")[:, 0:FC], ACT.Silu).then_inc(sem("dense_silu"), 1)

            dense_gu_high(1, range(GU_PARTS))
            for b in range(TB):
                dense_silu(0, b)
            for fc in range(NF):
                if fc > 0:
                    dense_down_high(fc)
                dense_gu_high(fc + 2, (0, 1))
                filled(act, f"T{fc}")
                if fc > 0:
                    act.wait_ge(sem("dense_chunks"), fc)
                nc.scalar.activation(d_hT[0][:, :, :].rearrange("p j t -> p (j t)"), bank(f"T{fc}")[:, :],
                                     ACT.Copy).then_inc(sem("dense_hT_high"), 1)
                if fc + 1 < NF:
                    dense_silu(fc + 1, 0)
                dense_gu_high(fc + 2, (2, 3))
                if fc + 1 < NF:
                    dense_silu(fc + 1, 1)
            x_squares("kv", ("Y1", "Y3"))
            for i in (0, 2):
                filled(act, f"TK{i}")
                for o, src, gain in two_chunks(f"TK{i}", hT, "kv", i):
                    last = nc.scalar.activation(o, src, ACT.Copy, scale=gain)
                last.then_inc(sem("kv_channels_act"), 1)
            for i in (0, 2):
                evacuate(f"TK{i}", two_chunks(f"TK{i}", hT2, "mix1", i))
            act.wait_ge(sem("forget_abs"), 1)
            nc.scalar.activation(fe, fe, ACT.Exp).then_inc(sem("forget_exp"), 1)
            act.wait_ge(sem("forget_exp"), 1)
            nc.scalar.activation(fe, fe, ACT.Ln, bias=1.0).then_inc(sem("forget_log"), 1)
            for i in range(3):
                evacuate(f"FK{i}", [(fkT[0:64, 4 * i + j:4 * i + j + 3:2, :],
                                     bank(f"FK{i}")[64 * j:64 * j + 64, :].rearrange("p (a s) -> p a s", a=2), 1.0) for j in range(2)])
            filled(act, "CC")
            nc.scalar.activation(negcT[0:FH, :], bank("CC")[0:FH, 0:256], ACT.Copy, scale=-1.0)
            nc.scalar.activation(cT[0:FH, :], bank("CC")[0:FH, 0:256], ACT.Copy).then_inc(read_sem("CC"), 1)
            read(act, "CC")
            act.wait_ge(sem("aug_set"), 2)
            act.dma_start(fkT[64:65, :, :], negcT[0:FH, :]).then_inc(sem("aug_loaded"), 16)
            act.dma_start(fqT[65:66, :, :], cT[0:FH, :]).then_inc(sem("aug_loaded"), 16)
            for b in range(TB):
                evacuate(f"FV{b}0", [(val[:, b, 0:384], bank(f"FV{b}0")[:, 0:384], 1.0)])
            for i in range(3):
                evacuate(f"FQ{i}", [(fqT[0:64, 4 * i + j:4 * i + j + 3:2, :],
                                     bank(f"FQ{i}")[64 * j:64 * j + 64, :].rearrange("p (a s) -> p a s", a=2), FD ** -0.5) for j in range(2)])
            evacuate("MQ1", two_heads("MQ1", mqT1, MD ** -0.5))
            for i in range(4):
                softmax_mem(1, f"N{i}", i, 4)
            def head_transposed(h):
                if h >= 4:
                    fox_head_done(act, h - 4)
                evacuate(f"PF{h}", [(probT[h % 4], bank(f"PF{h}")[:, 0:384], 1.0)])

            act.wait_ge(sem("fox_max"), 1)
            for h in range(FH):
                if h == 6:
                    for i in (0, 2):
                        evacuate(f"PN{i}", [(pmT1[:, i % 2, i // 2, :, :].rearrange("p h t -> p (h t)"), bank(f"PN{i}")[:, :], 1.0)])
                if 4 <= h < 8:
                    head_transposed(h - 4)
                for b in range(TB):
                    lo, hi = (0, 128) if b == 0 else (128, 384)
                    if h % 4 == 0 and b == 0 and h > 0:
                        act.wait_ge(sem("fox_max"), h // 4 + 1)
                    nc.scalar.activation(logits[:, h, lo:hi], logits[:, h, lo:hi], ACT.Exp, bias=f_max[:, 2 * h + b:2 * h + b + 1],
                                         accum_out=f_sum[:, 2 * h + b:2 * h + b + 1]).then_inc(sem("fox_exp"), 1)
            for h in range(8, FH, 2):
                head_transposed(h)
            for i in (0, 2):
                evacuate(f"TP{i}", [(hT[:, 2 * i:2 * i + 2, :].rearrange("p c s -> p (c s)"), bank(f"TP{i}")[:, :], 1.0)])
            read(act, "FO2"), read(act, "MW")
            for j in range(2):
                split_high(gu_arrived(act, 0, j), gu_hi[j], GU_PARTS, "gu_high")
            x_squares("ffn1", ("XB0", "XB1"))
            for b in range(TB):
                act.wait_ge(sem("ffn1_ready"), b + 1)
                nc.scalar.activation(e_x[0][:, b, :], xs[:, b, :], ACT.Copy).then_inc(sem("x_high"), 1)
            for i in (0, 2):
                evacuate(f"TR{i}", [(hT[:, 2 * i:2 * i + 2, :].rearrange("p c s -> p (c s)"), bank(f"TR{i}")[:, :], 1.0)])
            act.wait_ge(sem("logit_diff"), 1)
            nc.scalar.activation(ex[:, :, :], ex[:, :, :], ACT.Exp).then_inc(sem("logit_exp"), 1)

            def gu_high(n, T, j, which):
                if 0 in which:
                    gu_arrived(act, n, j)
                    e_filled(act, T, (j - 2) // NF, f"G{(j - 2) % NF}")
                split_high(raw[:, GU_SLOTS[j], :], gu_hi[j % 2], GU_PARTS, "gu_high", which)

            def tokens(dst, *counts_):
                for i, count in enumerate(counts_):
                    count_filled(act, count)
                    nc.scalar.activation(dst[:, 4 * i:4 * i + 4, :].rearrange("p c s -> p (c s)"), psum[count[0]][:, 0:4 * CAP],
                                         ACT.Copy).then_inc(sem(f"bank{count[0]}_read"), 1)

            def silu(count):
                count_filled(act, count)
                nc.scalar.activation(e_sg[0:CAP, :], psum[count[0]][0:CAP, 0:FC], ACT.Silu).then_inc(sem("expert_silu"), 1)

            def outputs(*counts_):
                for half, count in enumerate(counts_):
                    count_filled(act, count)
                    nc.scalar.activation(e_y[0][0:CAP, 512 * half:512 * half + 512], psum[half][0:CAP, :], ACT.Copy,
                                         scale=slot_gate[0:CAP, :]).then_inc(sem("y_high"), 1)

            def experts(k):
                def turn(t_, final):
                    T, n = (k, t_), t_ + TURNS * k
                    for j in range(NBODY):
                        u, fc = divmod(j, NF)
                        ahead2 = None if final and j + 2 >= NBODY else ((n, T, j + 2) if j + 2 < NBODY else (n + 1, (k, t_ + 1), j + 2 - NBODY))
                        if fc == 0:
                            outputs(*(e_count(T, u - 1, f"D{half}") for half in range(2)))
                        down_arrived(act, n, j)
                        chunk_done(act, T, j - 1)
                        split_high(raw_down[:, j % 2, :], down_hi, D_PARTS, "down_high")
                        e_filled(act, T, u, f"T{fc}")
                        nc.scalar.activation(e_hT[0][:, :, :].rearrange("p j t -> p (j t)"), e_bank(f"T{fc}")[:, 0:2 * CAP],
                                             ACT.Copy).then_inc(sem("hT_high"), 1)
                        if fc == 4:
                            e_filled(act, T, u, "ST")
                            nc.scalar.activation(scat[0:CAP, :, :].rearrange("p b t -> p (b t)"), e_bank("ST")[0:CAP, 0:S], ACT.Copy)
                            nc.scalar.activation(slot_gate[0:CAP, :], e_bank("ST")[0:CAP, S:S + 1], ACT.Copy).then_inc(e_read_sem("ST"), 1)
                        if ahead2:
                            gu_high(*ahead2, (0, 1))
                        if fc == 6 and not (final and u == 1):
                            tokens(e_xT[(u + 1) % 2][0], e_count(T, u + 1, "GH0"), e_count(T, u + 1, "GH1"))
                        if ahead2:
                            gu_high(*ahead2, (2, 3))
                        if not (final and j == NBODY - 1):
                            e_read(act, T, u, f"G{fc}")
                            silu(e_count(T, (j + 1) // NF, f"G{(j + 1) % NF}"))

                if k > 0:
                    for j in range(2):
                        gu_high(TURNS * k, (k, 0), j, range(GU_PARTS))
                tokens(e_xT[0][0], around[k]["GH0"], around[k]["GH1"])
                silu(around[k]["G0"])
                with act.Fori(0, TURNS - 1) as t_:
                    turn(t_, False)
                turn(TURNS - 1, True)
                outputs(*(e_count((k, TURNS - 1), 1, f"D{half}") for half in range(2)))

            experts(0)
            overflow(act, lambda: experts(1))
            act.wait_ge(sem("y_done"), 1)
            for b in range(TB):
                nc.scalar.activation(xs[:, b, :], x[:, b, :], ACT.Square,
                                     accum_out=square["final"][:, b:b + 1]).then_inc(sem("squares_final"), 1)

        @block.gpsimd
        def _(pool):
            pool.dma_start(w2[0:RANK, :], a["w_gla_gate2"][0]).then_inc(sem("gates_loaded"), 16)
            pool.dma_start(w2[RANK:RANK + 1, :], a["b_gla_gate2"]).then_inc(sem("gates_loaded"), 16)
            pool.dma_start(gain_row, a["norm_ffn"][1:2, :].partition_broadcast(P)).then_inc(sem("gain_row_loaded"), 16)
            pool.wait_ge(sem("table_loaded"), 16)
            half = const("mhalf")
            for name in ("x", "mem", "gla", "ffn0", "kv", "ffn1", "final"):
                pairs = [(o_rstd, o_mean)] if name == "gla" else [(rstd[name][:, b:b + 1], mean[name][:, b:b + 1]) for b in range(TB)]
                for b, (dst, src) in enumerate(pairs):
                    pool.wait_ge(sem(f"mean_{name}"), b + 1)
                    nc.gpsimd.tensor_tensor(dst, src, half[:, 0:dst.shape[1]], ALU.pow).then_inc(sem(f"rstd_{name}"), 1)
                if name == "kv":
                    filled(pool, "Y3")
                    pool.wait_ge(sem("rstd_kv"), TB)
                    for i, t_ in enumerate((fqT, fkT)):
                        nc.gpsimd.memset(t_[64:66, :, :], 1.0).then_inc(sem("aug_set"), 1)
                        pool.wait_ge(sem("aug_set"), i + 1)

        @block.vector
        def _(dve):
            order = [0]

            def link(ins):
                order[0] += 1
                ins.then_inc(sem("dve_order"), 1)
                dve.wait_ge(sem("dve_order"), order[0])

            def evacuate(name, outs_ins):
                filled(dve, name)
                for o, i, sc in outs_ins:
                    last = nc.vector.tensor_copy(o, i) if sc is None else nc.vector.tensor_scalar(o, i, sc, None, ALU.mult)
                last.then_inc(read_sem(name), 1)

            def root(name, b):
                dve.wait_ge(sem(f"squares_{name}"), b + 1)
                nc.vector.tensor_scalar(mean[name][:, b:b + 1], square[name][:, b:b + 1], 1.0 / D, EPS, ALU.mult,
                                        ALU.add).then_inc(sem(f"mean_{name}"), 1)
                dve.wait_ge(sem(f"rstd_{name}"), b + 1)

            def normed(name, src, dst, key):
                for b in range(TB):
                    root(name, b)
                    nc.vector.tensor_scalar(dst[:, b, :], src[:, b, :], rstd[name][:, b:b + 1], None,
                                            ALU.mult).then_inc(sem(key), 1)

            nc.vector.memset(glrT[0:RANK + 1, :], 1.0)
            normed("x", x, xs, "xs_ready")
            dve.wait_ge(sem("small_loaded"), 16)

            def two_chunks(name, dst, gain, i):
                return [(dst[:, 2 * i + j, :], bank(name)[:, 256 * j:256 * j + 256], gains[gain][:, 2 * i + j:2 * i + j + 1])
                        for j in range(2)]

            def two_heads(name, dst):
                src = bank(name)[:, :].rearrange("p (a s) -> p a s", a=2)
                return [(dst[0:64, j::2, :], src[64 * j:64 * j + 64], None) for j in range(2)]

            for i in (1, 3):
                evacuate(f"TX{i}", two_chunks(f"TX{i}", hT, "mix0", i))
            normed("mem", mixed, mixed, "mem_ready")
            evacuate("GLR", [(glrT[0:RANK, :], bank("GLR")[0:RANK, 0:256], None)])
            for b in range(TB):
                evacuate(f"Z{b}", [(zz[:, 384 * b:384 * b + 384], bank(f"Z{b}")[:, 0:384], None)])
            read(dve, "Z1")
            nc.vector.scalar_tensor_tensor(ez, zz, -1.0, zz, ALU.mult, ALU.min).then_inc(sem("gate_abs"), 1)
            link(nc.vector.tensor_scalar(la, zz, 0.0, None, ALU.min))
            for i in (1, 3):
                evacuate(f"TM{i}", two_chunks(f"TM{i}", mT0, "mem0", i) + two_chunks(f"TM{i}", mT1, "mem1", i))
            dve.wait_ge(sem("gate_log"), 1)
            nc.vector.tensor_tensor(la, la, ez, ALU.subtract).then_inc(sem("log_gates"), 1)
            for i in range(2):
                evacuate(f"B{i}", [(bT[0:DK, 512 * i:512 * i + 512], bank(f"B{i}")[0:DK, :], None)])
            read(dve, "B1")

            def halves(tile, half):
                return tile[0:DK, :].rearrange("k (n two t) -> k n two t", two=2, t=half)

            def level_diff(n):
                half = CHUNK // 2 >> n
                bh, dh = halves(bT, half), halves(decay, half)
                mid = bh[:, :, 1, 0:1].to_broadcast([DK, S * GH // (2 * half), half])
                nc.vector.tensor_tensor(dh[:, :, 1, :], bh[:, :, 1, :], mid, ALU.subtract)
                nc.vector.tensor_tensor(dh[:, :, 0, :], mid, bh[:, :, 0, :], ALU.subtract).then_inc(sem("decay_diff"), 1)

            def level_prod(n):
                half = CHUNK // 2 >> n
                dh, ph = halves(decay, half), halves(prod[n % 2], half)
                dve.wait_ge(sem("decay_exp"), n + 1)
                if n == 0:
                    read(dve, "Q1"), read(dve, "K1")
                if n >= 2:
                    filled(dve, f"L{n - 2}_1")
                nc.vector.tensor_tensor(ph[:, :, 1, :], dh[:, :, 1, :], halves(qT, half)[:, :, 1, :], ALU.mult)
                nc.vector.tensor_tensor(ph[:, :, 0, :], dh[:, :, 0, :], halves(kT, half)[:, :, 0, :],
                                        ALU.mult).then_inc(sem("level_ready"), 1)
                dve.wait_ge(sem("level_ready"), n + 1)

            def level_mask(n):
                for b in range(TB):
                    filled(dve, f"L{n}_{b}")
                    src = bank(f"L{n}_{b}")[:, :].rearrange("s (h t) -> s h t", h=GH)
                    keep = ident if n == LEVELS else const("levels")[:, n * P:(n + 1) * P]
                    keep = keep.unsqueeze(1)
                    if n == 0:
                        ins = nc.vector.tensor_tensor(scoreT[:, b], src, keep.to_broadcast([P, GH, P]), ALU.mult)
                    else:
                        ins = nc.vector.copy_predicated(scoreT[:, b], keep.bitcast(U32).to_broadcast([P, GH, P]), src)
                    ins.then_inc(read_sem(f"L{n}_{b}"), 1)
                    read(dve, f"L{n}_{b}")

            def mem_max(layer, name, i):
                b, j = divmod(i, 2)
                filled(dve, name)
                part = m_max[layer][:, b, 2 * j:2 * j + 2]
                link(nc.vector.reduce_max(part, bank(name)[:, :].rearrange("p (h m) -> p h m", h=2), AX))
                nc.vector.tensor_scalar(part, part, -1.0, None, ALU.mult).then_inc(sem("mem_max"), 1)

            level_diff(0)
            evacuate("KM0", two_heads("KM0", kmT0))
            level_prod(0)
            level_diff(1)
            level_mask(0)
            level_prod(1)
            level_diff(2)
            evacuate("V01", [(val[:, 0, 384:768], bank("V01")[:, 0:384], None)])
            evacuate("V11", [(val[:, 1, 384:768], bank("V11")[:, 0:384], None)])
            level_mask(1)
            level_prod(2)
            level_diff(3)
            evacuate("KM1", two_heads("KM1", kmT1))
            level_mask(2)
            level_prod(3)
            level_diff(4)
            level_mask(3)
            level_prod(4)
            level_diff(5)
            mem_max(0, "SM0", 0)
            mem_max(0, "SM1", 1)
            level_mask(4)
            level_prod(5)
            nc.vector.tensor_copy(blast[0:DK, :], bT[0:DK, CHUNK - 1::CHUNK]).then_inc(sem("decay_diff"), 1)
            mem_max(0, "SM2", 2)
            mem_max(0, "SM3", 3)
            level_mask(5)
            dve.wait_ge(sem("decay_exp"), LEVELS + 1)
            by_chunk = bT[0:DK, :].rearrange("k (n t) -> k n t", t=CHUNK)
            nc.vector.tensor_tensor(by_chunk, blast[0:DK, :].unsqueeze(2).to_broadcast([DK, S * GH // CHUNK, CHUNK]),
                                    by_chunk, ALU.subtract).then_inc(sem("key_diff"), 1)
            nc.vector.tensor_copy(alast[0:DK, :], decay[0:DK, CHUNK - 1::CHUNK])
            filled(dve, "L4_1")
            nc.vector.tensor_tensor(prod[0][0:DK, :], decay[0:DK, :], qT[0:DK, :], ALU.mult).then_inc(sem("query_prod"), 1)
            dve.wait_ge(sem("key_exp"), 1)
            filled(dve, "L5_1")
            nc.vector.tensor_tensor(prod[1][0:DK, :], bT[0:DK, :], kT[0:DK, :], ALU.mult).then_inc(sem("key_prod"), 1)
            level_mask(6)
            for c in range(3):
                for i in range(2):
                    name = f"U{c}_{i}"
                    filled(dve, name)
                    if c == 0:
                        ins = nc.vector.tensor_copy(state[0:DK, 0, 2 * i:2 * i + 2, :].rearrange("k h v -> k (h v)"),
                                                    bank(name)[0:DK, 0:384])
                        if i == 0:
                            dve.wait_ge(sem("key_prod"), 1)
                    else:
                        for j in range(2):
                            h = 2 * i + j
                            ins = nc.vector.scalar_tensor_tensor(
                                state[0:DK, c, h, :], state[0:DK, c - 1, h, :], alast[0:DK, 4 * h + c:4 * h + c + 1],
                                bank(name)[0:DK, 192 * j:192 * j + 192], ALU.mult, ALU.add)
                    ins.then_inc(read_sem(name), 1)
                read(dve, f"U{c}_1")

            def memory_values(layer, name, scores):
                read(dve, scores)
                link(nc.vector.reciprocal(m_inv[layer], m_sum[layer]))
                filled(dve, name)
                inv = m_inv[layer].rearrange("p (b h) -> p b h", b=TB)
                for b in range(TB):
                    last = nc.vector.tensor_tensor(
                        mixed[:, b, MAIN:D].rearrange("p (h n) -> p h n", h=MH),
                        bank(name)[:, 256 * b:256 * b + 256].rearrange("p (h n) -> p h n", h=MH),
                        inv[:, b, :].unsqueeze(2).to_broadcast([P, MH, MD]), ALU.mult)
                last.then_inc(read_sem(name), 1)

            for i in (1, 3):
                evacuate(f"PM{i}", [(pmT0[:, i % 2, i // 2, :, :].rearrange("p h t -> p (h t)"), bank(f"PM{i}")[:, :], None)])
            dve.wait_ge(sem("o_squares"), 8)
            nc.vector.tensor_scalar(o_mean, o_sq, 1.0 / DV, EPS, ALU.mult, ALU.add).then_inc(sem("mean_gla"), 1)
            dve.wait_ge(sem("rstd_gla"), 1)
            dve.wait_ge(sem("output_gates"), 2)
            for b in range(TB):
                for i in range(2):
                    for h in (2 * i, 2 * i + 1):
                        part = mixed[:, b, DV * h:DV * (h + 1)]
                        last = nc.vector.scalar_tensor_tensor(part, bank(f"O{b}{i}")[:, DV * (h % 2):DV * (h % 2) + DV],
                                                              o_rstd[:, 4 * b + h:4 * b + h + 1], part, ALU.mult, ALU.mult)
                    last.then_inc(read_sem(f"O{b}{i}"), 1)
            memory_values(0, "MV", "SM3")
            for i in (1, 3):
                evacuate(f"TO{i}", two_chunks(f"TO{i}", hT, "onorm", i))

            def split_low(src, hi_, lo_, parts, what, count, which=None):
                n = src.shape[1] // parts
                for i in range(parts) if which is None else which:
                    at_ = slice(n * i, n * i + n)
                    dve.wait_ge(sem(f"{what}_high"), count + (i + 1))
                    nc.vector.tensor_tensor(lo_[:, at_], src[:, at_], hi_[:, at_].bitcast(F32),
                                            ALU.subtract).then_inc(sem(f"{what}_split"), 1)

            read(dve, "O11"), read(dve, "MV")
            split_low(raw[:, DENSE_GU[0], :], gu_hi[0], gu_lo[0], GU_PARTS, "gu", 0)
            split_low(raw_down[:, 0, :], down_hi, down_lo, D_PARTS, "down", 0)

            def add_to_stream(name, b, half):
                filled(dve, name)
                part = x[:, b, 512 * half:512 * half + 512]
                nc.vector.tensor_tensor(part, part, bank(name)[:, :], ALU.add).then_inc(read_sem(name), 1)

            for b in range(TB):
                for n_, half in (("WA", 0), ("WB", 1)):
                    add_to_stream(f"{n_}{b}", b, half)
            read(dve, "WB1")
            normed("ffn0", x, xs, "ffn0_ready")
            for i in range(4):
                filled(dve, f"TF{i}")
                dve.wait_ge(sem("dense_x_high"), i + 1)
                for (lo_, src, gain), (hi_, _, _) in zip(two_chunks(f"TF{i}", d_xT[1], "ffn0", i), two_chunks(f"TF{i}", d_xT[0], "ffn0", i)):
                    last = nc.vector.scalar_tensor_tensor(lo_, src, gain, hi_.bitcast(F32), ALU.mult, ALU.subtract)
                last.then_inc(read_sem(f"TF{i}"), 1)

            def dense_gu_low(fc, which):
                if fc < NF:
                    split_low(raw[:, DENSE_GU[fc], :], gu_hi[fc % 2], gu_lo[fc % 2], GU_PARTS, "gu", GU_PARTS * fc, which)

            def dense_product(fc, b):
                if fc > 0:
                    filled(dve, f"T{fc - 1}")
                dve.wait_ge(sem("dense_silu"), TB * fc + b + 1)
                nc.vector.tensor_tensor(d_h[:, b, :], d_sg[:, b, :], bank(f"G{fc}_{b}")[:, FC:2 * FC],
                                        ALU.mult).then_inc(read_sem(f"G{fc}_{b}"), 1)

            dense_gu_low(1, range(GU_PARTS))
            for b in range(TB):
                dense_product(0, b)
            for fc in range(NF):
                if fc > 0:
                    split_low(raw_down[:, fc % 2, :], down_hi, down_lo, D_PARTS, "down", D_PARTS * fc)
                dense_gu_low(fc + 2, (0, 1))
                dve.wait_ge(sem("dense_hT_high"), fc + 1)
                nc.vector.tensor_tensor(d_hT[1][:, :, :].rearrange("p j t -> p (j t)"), bank(f"T{fc}")[:, :],
                                        d_hT[0][:, :, :].rearrange("p j t -> p (j t)").bitcast(F32),
                                        ALU.subtract).then_inc(read_sem(f"T{fc}"), 1)
                if fc + 1 < NF:
                    dense_product(fc + 1, 0)
                dense_gu_low(fc + 2, (2, 3))
                if fc + 1 < NF:
                    dense_product(fc + 1, 1)
            for b in range(TB):
                for half in range(2):
                    add_to_stream(f"Y{2 * b + half}", b, half)
            read(dve, "Y3")
            normed("kv", x, xs, "kv_ready")
            for i in (1, 3):
                filled(dve, f"TK{i}")
                for o, src, gain in two_chunks(f"TK{i}", hT, "kv", i):
                    last = nc.vector.tensor_scalar(o, src, gain, None, ALU.mult)
                last.then_inc(sem("kv_channels_dve"), 1)
            for i in (1, 3):
                evacuate(f"TK{i}", two_chunks(f"TK{i}", hT2, "mix1", i))
            filled(dve, "FG")
            fzb = fz.rearrange("p (b h) -> p b h", b=TB)
            nc.vector.tensor_tensor(fzb, bank("FG")[:, 0:24].rearrange("p (b h) -> p b h", b=TB),
                                    bf.unsqueeze(1).to_broadcast([P, TB, FH]), ALU.add).then_inc(read_sem("FG"), 1)
            read(dve, "FG")
            nc.vector.scalar_tensor_tensor(fe, fz, -1.0, fz, ALU.mult, ALU.min).then_inc(sem("forget_abs"), 1)
            flat = fl.rearrange("p b h -> p (b h)")
            link(nc.vector.tensor_scalar(flat, fz, 0.0, None, ALU.min))
            dve.wait_ge(sem("forget_log"), 1)
            nc.vector.tensor_tensor(flat, flat, fe, ALU.subtract).then_inc(sem("log_forget"), 1)
            for b in range(TB):
                evacuate(f"FV{b}1", [(val[:, b, 384:768], bank(f"FV{b}1")[:, 0:384], None)])
            for i in range(4):
                mem_max(1, f"N{i}", i)
            fm = f_max.rearrange("p (h b) -> p h b", b=TB)
            for h in range(FH):
                filled(dve, f"S{h}")
                nc.vector.tensor_tensor(logits[:, h, :], bank(f"S{h}")[:, 0:384], const("causal"),
                                        ALU.add).then_inc(read_sem(f"S{h}"), 1)
                if h % 4 == 3:
                    read(dve, f"S{h}")
                    g_ = slice(h - 3, h + 1)
                    nc.vector.reduce_max(fm[:, g_, 0], logits[:, g_, 0:128], AX)
                    link(nc.vector.reduce_max(fm[:, g_, 1], logits[:, g_, 128:384], AX))
                    part = f_max[:, 2 * (h - 3):2 * (h + 1)]
                    nc.vector.tensor_scalar(part, part, -1.0, None, ALU.mult).then_inc(sem("fox_max"), 1)
            fi = f_inv.rearrange("p (h b) -> p b h", b=TB)

            def fox_values(g_):
                filled(dve, f"FO{g_}")
                for b in range(TB):
                    last = nc.vector.tensor_tensor(
                        mixed[:, b, 256 * g_:256 * g_ + 256].rearrange("p (h n) -> p h n", h=4),
                        bank(f"FO{g_}")[:, 256 * b:256 * b + 256].rearrange("p (h n) -> p h n", h=4),
                        fi[:, b, 4 * g_:4 * g_ + 4].unsqueeze(2).to_broadcast([P, 4, FD]), ALU.mult)
                last.then_inc(read_sem(f"FO{g_}"), 1)

            for i in (1, 3):
                evacuate(f"PN{i}", [(pmT1[:, i % 2, i // 2, :, :].rearrange("p h t -> p (h t)"), bank(f"PN{i}")[:, :], None)])
            for h in (4, 5, 6, 7, 9, 11):
                fox_head_done(dve, h - 4)
                evacuate(f"PF{h}", [(probT[h % 4], bank(f"PF{h}")[:, 0:384], None)])
                if h == 4:
                    memory_values(1, "MW", "N3")
                if h == 5:
                    dve.wait_ge(sem("fox_exp"), 2 * FH)
                    link(nc.vector.reciprocal(f_inv, f_sum))
                if h in (6, 9):
                    fox_values(h // 7)
            fox_values(2)
            for i in (1, 3):
                evacuate(f"TP{i}", [(hT[:, 2 * i:2 * i + 2, :].rearrange("p c s -> p (c s)"), bank(f"TP{i}")[:, :], None)])
            read(dve, "FO2"), read(dve, "MW")
            for j in range(2):
                split_low(raw[:, GU_SLOTS[j], :], gu_hi[j], gu_lo[j], GU_PARTS, "gu", GU_PARTS * (NF + j))
            for b in range(TB):
                for n_, half in (("XA", 0), ("XB", 1)):
                    add_to_stream(f"{n_}{b}", b, half)
            read(dve, "XB1")
            dve.wait_ge(sem("gain_row_loaded"), 16)
            for b in range(TB):
                root("ffn1", b)
                nc.vector.scalar_tensor_tensor(xs[:, b, :], x[:, b, :], rstd["ffn1"][:, b:b + 1], gain_row,
                                               ALU.mult, ALU.mult).then_inc(sem("ffn1_ready"), 1)
            for b in range(TB):
                dve.wait_ge(sem("x_high"), b + 1)
                nc.vector.tensor_tensor(e_x[1][:, b, :], xs[:, b, :], e_x[0][:, b, :].bitcast(F32),
                                        ALU.subtract).then_inc(sem("x_split"), 1)
            for i in (1, 3):
                evacuate(f"TR{i}", [(hT[:, 2 * i:2 * i + 2, :].rearrange("p c s -> p (c s)"), bank(f"TR{i}")[:, :], None)])
            def clear():
                for t_ in (*e_y, scat[:, :, :].rearrange("p b t -> p (b t)")):
                    n_ = t_.shape[1] // P
                    nc.vector.tensor_scalar(t_.rearrange("p (a n) -> p a n", a=n_), const("ones").unsqueeze(1).to_broadcast([P, n_, P]),
                                            0.0, None, ALU.mult)
                nc.vector.memset(slot_gate, 0.0).then_inc(sem("scatter_cleared"), 1)

            dve.wait_ge(sem("x_split"), 2)
            clear()
            filled(dve, "RL")
            nc.vector.tensor_copy(lg[:, :, :].rearrange("p b e -> p (b e)"), bank("RL")[:, 0:16]).then_inc(read_sem("RL"), 1)
            read(dve, "RL")
            link(nc.vector.reduce_max(top, lg[:, :, :], AX))
            for b in range(TB):
                last = nc.vector.tensor_scalar(ex[:, b, :], lg[:, b, :], top[:, b:b + 1], None, ALU.subtract)
            last.then_inc(sem("logit_diff"), 1)
            mine = lg.unsqueeze(3).to_broadcast([P, TB, NE, NE])
            other = lg.unsqueeze(2).to_broadcast([P, TB, NE, NE])
            nc.vector.tensor_tensor(gt, other, mine, ALU.is_gt)
            link(nc.vector.tensor_tensor(eq, other, mine, ALU.is_equal))
            link(nc.vector.tensor_tensor(eq, eq, const("earlier").rearrange("p (e o) -> p e o", e=NE).unsqueeze(1).to_broadcast(
                [P, TB, NE, NE]), ALU.mult))
            link(nc.vector.tensor_tensor(gt, gt, eq, ALU.add))
            link(nc.vector.reduce_sum(rank, gt, AX))
            nc.vector.tensor_scalar(sel, rank, 1.5, None, ALU.is_lt).then_inc(sem("chosen"), 1)
            dve.wait_ge(sem("chosen"), 1)
            dve.wait_ge(sem("logit_exp"), 1)
            link(nc.vector.tensor_tensor(ex[:, :, :], ex[:, :, :], sel[:, :, :], ALU.mult))
            link(nc.vector.reduce_sum(den, ex[:, :, :], AX))
            link(nc.vector.reciprocal(rden, den))
            nc.vector.tensor_tensor(gate, ex[:, :, :], rden.unsqueeze(2).to_broadcast([P, TB, NE]), ALU.mult)
            filled(dve, "POS")
            nc.vector.tensor_tensor(pos, bank("POS")[:, 0:16].rearrange("p (b e) -> p b e", b=TB), sel[:, :, :],
                                    ALU.mult).then_inc(read_sem("POS"), 1)
            read(dve, "POS")
            link(nc.vector.tensor_scalar(pos, pos, -1.0, None, ALU.add))
            filled(dve, "CNT")
            nc.vector.reduce_max(counts[0:1, 0:1], bank("CNT")[0:1, 0:8], AX).then_inc(read_sem("CNT"), 1)
            read(dve, "CNT")
            nc.vector.tensor_copy(over[0:1, 0:1], counts[0:1, 0:1]).then_inc(sem("overflow_known"), 1)

            def build(e, k):
                slots = const("slots")[:, CAP * k:CAP * (k + 1)]
                for dst in (perm, perm_r):
                    for b in range(TB):
                        last = nc.vector.tensor_scalar(dst[:, b, :], slots, pos[:, b, bass.ds(e, 1)], None, ALU.is_equal)
                last.then_inc(sem("perm_built"), 1)

            def tokens(dst, *counts_):
                for i, count in enumerate(counts_):
                    count_filled(dve, count)
                    nc.vector.tensor_copy(dst[:, 4 * i:4 * i + 4, :].rearrange("p c s -> p (c s)"),
                                          psum[count[0]][:, 0:4 * CAP]).then_inc(sem(f"bank{count[0]}_read"), 1)

            def product(n_silu, count):
                dve.wait_ge(sem("expert_silu"), n_silu)
                nc.vector.tensor_tensor(e_h[0:CAP, :], e_sg[0:CAP, :], psum[count[0]][0:CAP, FC:2 * FC],
                                        ALU.mult).then_inc(sem(f"bank{count[0]}_read"), 1)

            def outputs(n_high):
                for half in range(2):
                    dve.wait_ge(sem("y_high"), n_high + (half + 1))
                    at_ = slice(512 * half, 512 * half + 512)
                    nc.vector.scalar_tensor_tensor(e_y[1][0:CAP, at_], psum[half][0:CAP, :], slot_gate[0:CAP, :],
                                                   e_y[0][0:CAP, at_].bitcast(F32), ALU.mult,
                                                   ALU.subtract).then_inc(sem(f"bank{half}_read"), 1)

            def scattered(counts_, parts=(0, 1, 2, 3)):
                for q, count in zip(parts, counts_):
                    b, half = divmod(q, 2)
                    count_filled(dve, count)
                    part = x[:, b, 512 * half:512 * half + 512]
                    nc.vector.tensor_tensor(part, part, e_bank(f"SC{q}")[:, :], ALU.add).then_inc(e_read_sem(f"SC{q}"), 1)

            def experts(k):
                def turn(t_, final):
                    T, n = (k, t_), t_ + TURNS * k
                    for j in range(NBODY):
                        u, fc = divmod(j, NF)
                        ahead2 = None if final and j + 2 >= NBODY else ((n, j + 2) if j + 2 < NBODY else (n + 1, j + 2 - NBODY))

                        def gu_low(which):
                            if ahead2:
                                m_, i = ahead2
                                split_low(raw[:, GU_SLOTS[i], :], gu_hi[i % 2], gu_lo[i % 2], GU_PARTS, "gu",
                                          chunk_no(m_, i) * GU_PARTS, which)

                        if fc == 0:
                            outputs(n * 4 + (2 * k + 2 * u))
                        split_low(raw_down[:, j % 2, :], down_hi, down_lo, D_PARTS, "down", chunk_no(n, j) * D_PARTS)
                        dve.wait_ge(sem("hT_high"), n * NBODY + (j + 1))
                        nc.vector.tensor_tensor(e_hT[1][:, :, :].rearrange("p j t -> p (j t)"), e_bank(f"T{fc}")[:, 0:2 * CAP],
                                                e_hT[0][:, :, :].rearrange("p j t -> p (j t)").bitcast(F32),
                                                ALU.subtract).then_inc(e_read_sem(f"T{fc}"), 1)
                        gu_low((0, 1))
                        if fc in (2, 3):
                            parts = (2 * fc - 4, 2 * fc - 3)
                            scattered([e_count(T, u, f"SC{q}") for q in parts], parts)
                        if not (final and u == 1):
                            if fc == 4:
                                e_filled(dve, T, u, "ST")
                                build(t_ * 2 + (u + 1), k)
                            if fc == 7:
                                tokens(e_xT[(u + 1) % 2][1], e_count(T, u + 1, "GL0"), e_count(T, u + 1, "GL1"))
                        gu_low((2, 3))
                        if not (final and j == NBODY - 1):
                            e_filled(dve, T, u, f"T{fc}")
                            product(n * NBODY + (j + 2), e_count(T, (j + 1) // NF, f"G{(j + 1) % NF}"))

                if k > 0:
                    count_filled(dve, around[0]["SC3"])
                    count_read(dve, around[0]["SC3"])
                    clear()
                build(0, k)
                if k > 0:
                    for j in range(2):
                        split_low(raw[:, GU_SLOTS[j], :], gu_hi[j], gu_lo[j], GU_PARTS, "gu", chunk_no(TURNS * k, j) * GU_PARTS)
                tokens(e_xT[0][1], around[k]["GL0"], around[k]["GL1"])
                product(TURNS * k * NBODY + 1, around[k]["G0"])
                with dve.Fori(0, TURNS - 1) as t_:
                    turn(t_, False)
                turn(TURNS - 1, True)
                outputs((TURNS * (k + 1)) * 4 + 2 * k)
                scattered([around[k][f"SC{q}"] for q in range(4)])
                dve.wait_ge(sem("final_gain_loaded"), 16 * (k + 1))

            experts(0)
            overflow(dve, lambda: experts(1))
            nc.vector.memset(counts[0:1, 8:16], 0.0).then_inc(sem("y_done"), 1)
            for b in range(TB):
                root("final", b)
                nc.vector.scalar_tensor_tensor(xs[:, b, :], x[:, b, :], rstd["final"][:, b:b + 1], final_gain,
                                               ALU.mult, ALU.mult).then_inc(sem("out_ready"), 1)

        @block.tensor
        def _(pe):
            mm = nc.tensor.matmul

            def by_chunk(tile, b, c):
                return tile[:, b, :].rearrange("t (p c) -> t c p", c=KC)[:, c, :]

            def tok(b):
                return slice(b * P, (b + 1) * P)

            def transposes(prefix, src, ready=None):
                for b in range(TB):
                    if ready:
                        pe.wait_ge(sem(ready), b + 1)
                    for i in range(4):
                        name = f"{prefix}{i}"
                        if b == 0:
                            free(pe, name)
                        for j in range(2):
                            last = nc.tensor.transpose(bank(name)[:, (2 * j + b) * P:(2 * j + b + 1) * P],
                                                       by_chunk(src, b, 2 * i + j), ident)
                        if b == TB - 1:
                            last.then_inc(full_sem(name), 1)

            def project(name, groups, behind=None):
                free(pe, name)
                for n_, (o, lhs, rhs) in enumerate(groups):
                    for c in range(KC):
                        if behind and n_ == 0 and c % 2 == 0:
                            if isinstance(behind, str):
                                read(pe, f"{behind}{c // 2}")
                            else:
                                behind(c // 2)
                        last = mm(o, lhs(c), rhs(c), start=(c == 0), stop=(c == KC - 1))
                last.then_inc(full_sem(name), 1)

            def tokens_by(name, b, src, wt, lo, n, behind=None):
                project(name, [(bank(name)[:, 0:n], lambda c: src[:, c, tok(b)], lambda c: wt[:, c, lo:lo + n])], behind)

            def columns_by(name, src, wt, los, n, behind=None):
                project(name, [(bank(name)[0:n, 256 * j:256 * j + 256], lambda c, lo=lo: wt[:, c, lo:lo + n],
                                lambda c: src[:, c, :]) for j, lo in enumerate(los)], behind)

            pe.wait_ge(sem("table_loaded"), 16)
            transposes("TX", xs, "xs_ready")
            wgm = weights(pe, "gates")
            columns_by("GLR", hT, wgm, [0], RANK, "TX")
            pe.wait_ge(sem("gates_loaded"), 32)
            read(pe, "GLR")
            for b in range(TB):
                free(pe, f"Z{b}")
                mm(bank(f"Z{b}")[:, 0:384], glrT[0:RANK + 1, tok(b)], w2[0:RANK + 1, :], start=True,
                   stop=True).then_inc(full_sem(f"Z{b}"), 1)
            for n_ in ("q", "k"):
                wt = weights(pe, n_)
                for i in range(2):
                    columns_by(f"{n_.upper()}{i}", hT, wt, [DK * 2 * i, DK * (2 * i + 1)], DK)
            transposes("TM", mixed, "mem_ready")
            columns_by("MQ", hT, wgm, [16, 144], P)
            pe.wait_ge(sem("log_gates"), 1)
            for i in range(2):
                free(pe, f"B{i}")
                for j in range(2):
                    for b in range(TB):
                        lo = DK * (2 * i + j)
                        last = mm(bank(f"B{i}")[0:DK, 256 * j + P * b:256 * j + P * b + P], la_v[:, b, lo:lo + DK],
                                  const("tri16"), start=True, stop=True)
                last.then_inc(full_sem(f"B{i}"), 1)
            for i in range(4):
                read(pe, f"TM{i}")
            wkv = weights(pe, "mem0")
            columns_by("KM0", mT0, wkv, [0, P], P)

            def memory_values_of(name, src, wt):
                project(name, [(bank(name)[:, 256 * b:256 * b + 256], lambda c, b=b: src[:, c, tok(b)],
                                lambda c: wt[:, c, 256:512]) for b in range(TB)])

            memory_values_of("VM0", mT0, wkv)

            def level(n):
                if n < LEVELS:
                    pe.wait_ge(sem("level_ready"), n + 1)
                for b in range(TB):
                    free(pe, f"L{n}_{b}")
                    for h in range(GH):
                        at_ = slice(S * h + P * b, S * h + P * b + P)
                        lhs, rhs = (kT, qT) if n == LEVELS else (prod[n % 2], prod[n % 2])
                        last = mm(bank(f"L{n}_{b}")[:, P * h:P * h + P], lhs[0:DK, at_], rhs[0:DK, at_], start=True, stop=True)
                    last.then_inc(full_sem(f"L{n}_{b}"), 1)

            def memory_scores(name, i, q, k_):
                b, j = divmod(i, 2)
                free(pe, name)
                for h in range(2):
                    last = mm(bank(name)[:, 256 * h:256 * h + 256], q[0:64, 2 * j + h, tok(b)], k_[0:64, 2 * j + h, :],
                              start=True, stop=True)
                last.then_inc(full_sem(name), 1)

            def main_values(i):
                wv = weights(pe, f"v{i}")
                for b in range(TB):
                    tokens_by(f"V{b}{i}", b, hT, wv, 0, 384)

            def output_gates(b, i):
                tokens_by(f"R{b}{i}", b, hT, weights(pe, f"r{i}"), 0, 384)

            main_values(0)
            level(0)
            main_values(1)
            level(1)
            wkv1 = weights(pe, "mem1")
            columns_by("KM1", mT1, wkv1, [0, P], P)
            level(2)
            memory_values_of("VM1", mT1, wkv1)
            level(3)
            read(pe, "MQ"), read(pe, "KM0")
            memory_scores("SM0", 0, mqT0, kmT0)
            memory_scores("SM1", 1, mqT0, kmT0)
            output_gates(0, 0)
            level(4)
            output_gates(1, 0)
            memory_scores("SM2", 2, mqT0, kmT0)
            memory_scores("SM3", 3, mqT0, kmT0)
            level(5)
            output_gates(0, 1)
            output_gates(1, 1)
            level(6)
            pe.wait_ge(sem("key_prod"), 1)
            for b in range(TB):
                free(pe, f"KH{b}")
                for h in range(GH):
                    last = nc.tensor.transpose(bank(f"KH{b}")[:, DK * h:DK * h + DK], prod[1][0:DK, S * h + P * b:S * h + P * b + P],
                                               ident[0:DK, 0:DK])
                last.then_inc(full_sem(f"KH{b}"), 1)
            read(pe, "KH0"), read(pe, "KH1")
            for b in range(TB):
                read(pe, f"V{b}0"), read(pe, f"V{b}1")
            for c in range(3):
                b, r = c // 2, slice(64 * (c % 2), 64 * (c % 2) + 64)
                for i in range(2):
                    free(pe, f"U{c}_{i}")
                    for j in range(2):
                        h = 2 * i + j
                        last = mm(bank(f"U{c}_{i}")[0:DK, DV * j:DV * j + DV], khat[r, b, h, :], val[r, b, DV * h:DV * (h + 1)],
                                  start=True, stop=True)
                    last.then_inc(full_sem(f"U{c}_{i}"), 1)

            def memory_transposes(prefix, probs):
                for i in range(4):
                    b, mc = divmod(i, 2)
                    name = f"{prefix}{i}"
                    free(pe, name)
                    for h in range(MH):
                        last = nc.tensor.transpose(bank(name)[:, P * h:P * h + P], probs[:, b, h, P * mc:P * mc + P], ident)
                    last.then_inc(full_sem(name), 1)

            def memory_outputs(name, prefix, probsT, vm):
                for i in range(4):
                    read(pe, f"{prefix}{i}")
                free(pe, name)
                for b in range(TB):
                    for h in range(MH):
                        for mc in range(2):
                            last = mm(bank(name)[:, 256 * b + MD * h:256 * b + MD * h + MD], probsT[:, mc, b, h, :],
                                      vm[:, mc, MD * h:MD * h + MD], start=(mc == 0), stop=(mc == 1))
                last.then_inc(full_sem(name), 1)

            read(pe, "L6_1"), read(pe, "U2_1")
            for b in range(TB):
                for i in range(2):
                    free(pe, f"O{b}{i}")
                    for j in range(2):
                        h = 2 * i + j
                        for c in (2 * b, 2 * b + 1):
                            r = slice(64 * (c % 2), 64 * (c % 2) + 64)
                            o = bank(f"O{b}{i}")[r, DV * j:DV * j + DV]
                            last = mm(o, scoreT[:, b, h, r], val[:, b, DV * h:DV * (h + 1)], start=True, stop=(c == 0))
                            if c > 0:
                                last = mm(o, prod[0][0:DK, S * h + CHUNK * c:S * h + CHUNK * (c + 1)],
                                          state[0:DK, c - 1, h, :], start=False, stop=True)
                    last.then_inc(full_sem(f"O{b}{i}"), 1)

            for i in range(4):
                read(pe, f"SM{i}")
            memory_transposes("PM", pm0)
            memory_outputs("MV", "PM", pmT0, vm0)

            def output_projection(prefix, units, behind):
                for b in range(TB):
                    for unit_, n_ in zip(units, "AB"):
                        tokens_by(f"{prefix}{n_}{b}", b, hT, weights(pe, unit_), 0, 512, behind if n_ == "A" and b == 0 else None)

            read(pe, "O11"), read(pe, "MV")
            transposes("TO", mixed)
            output_projection("W", ("out0a", "out0b"), "TO")
            transposes("TF", xs, "ffn0_ready")
            def three(o, lhs, rhs, first, last_):
                mm(o, lhs[0], rhs[0], start=first, stop=False)
                mm(o, lhs[0], rhs[1], start=False, stop=False)
                return mm(o, lhs[1], rhs[0], start=False, stop=last_)

            gate_up = [[t_.rearrange("p (a c n) -> p c a n", a=2, c=KC) for t_ in pair] for pair in zip(gu_hi, gu_lo)]
            down_w = [t_.rearrange("p (j n) -> p j n", j=2) for t_ in (down_hi, down_lo)]

            def dense_up(fc, b):
                pe.wait_ge(sem("gu_split"), GU_PARTS * (fc + 1))
                name, wt = f"G{fc}_{b}", gate_up[fc % 2]
                free(pe, name)
                for c in range(KC):
                    if fc + b == 0 and c % 2 == 0:
                        read(pe, f"TF{c // 2}")
                    last = three(bank(name)[:, :].rearrange("p (a n) -> p a n", a=2), [t_[:, c, tok(b)] for t_ in d_xT],
                                 [t_[:, c] for t_ in wt], c == 0, c == KC - 1)
                last.then_inc(full_sem(name), 1)

            dense_up(0, 0)
            dense_up(0, 1)
            for fc in range(NF):
                if fc < NF - 1:
                    dense_up(fc + 1, 0)
                read(pe, f"G{fc}_0"), read(pe, f"G{fc}_1")
                free(pe, f"T{fc}")
                for j in range(2):
                    for b in range(TB):
                        last = nc.tensor.transpose(bank(f"T{fc}")[:, (2 * j + b) * P:(2 * j + b + 1) * P], d_h[:, b, j::2], ident)
                last.then_inc(full_sem(f"T{fc}"), 1)
                if fc < NF - 1:
                    dense_up(fc + 1, 1)
                read(pe, f"T{fc}")
                pe.wait_ge(sem("down_split"), D_PARTS * (fc + 1))
                for b in range(TB):
                    for half in range(2):
                        name, at_ = f"Y{2 * b + half}", slice(512 * half, 512 * half + 512)
                        if fc == 0:
                            free(pe, name)
                        for j in range(2):
                            last = three(bank(name)[:, :], [t_[:, j, tok(b)] for t_ in d_hT], [t_[:, j, at_] for t_ in down_w],
                                         fc == 0 and j == 0, fc == NF - 1 and j == 1)
                        if fc == NF - 1:
                            last.then_inc(full_sem(name), 1)
                if fc < NF - 1:
                    last.then_inc(sem("dense_chunks"), 1)

            transposes("TK", xs, "kv_ready")
            project("FG", [(bank("FG")[:, FH * b:FH * b + FH], lambda c, b=b: hT[:, c, tok(b)], lambda c: wf[:, c, :])
                           for b in range(TB)], lambda i: pe.wait_ge(sem(f"kv_channels_{('act', 'dve')[i % 2]}"), i // 2 + 1))
            def head_pairs(prefix, units, src):
                wts = [weights(pe, units[0])]
                for i in range(3):
                    if i == 1:
                        wts.append(weights(pe, units[1]))
                    name = f"{prefix}{i}"
                    project(name, [(bank(name)[:, 256 * j:256 * j + 256],
                                    lambda c, q_=2 * i + j: wts[q_ // 3][:, c, P * (q_ % 3):P * (q_ % 3) + P],
                                    lambda c: src[:, c, :]) for j in range(2)])

            head_pairs("FK", ("fk0", "fk1"), hT)
            pe.wait_ge(sem("log_forget"), 1)
            free(pe, "CC")
            mm(bank("CC")[0:FH, 0:P], fl[:, 0, :], const("tri"), start=True, stop=True)
            mm(bank("CC")[0:FH, P:2 * P], fl[:, 0, :], const("ones"), start=True, stop=False)
            mm(bank("CC")[0:FH, P:2 * P], fl[:, 1, :], const("tri"), start=False, stop=True).then_inc(full_sem("CC"), 1)
            for i in range(2):
                wt = weights(pe, f"fv{i}")
                for b in range(TB):
                    tokens_by(f"FV{b}{i}", b, hT, wt, 0, 384)
            for i in range(4):
                read(pe, f"TK{i}")
            head_pairs("FQ", ("fq0", "fq1"), hT2)
            columns_by("MQ1", hT2, weights(pe, "fmq"), [0, P], P)
            read(pe, "MQ1"), read(pe, "KM1"), read(pe, "VM1")
            for i in range(4):
                memory_scores(f"N{i}", i, mqT1, kmT1)
            pe.wait_ge(sem("aug_loaded"), 32)
            read(pe, "FQ2"), read(pe, "FK2")
            for h in range(FH):
                name = f"S{h}"
                free(pe, name)
                mm(bank(name)[:, 0:P], fqT[0:66, h, 0:P], fkT[0:66, h, 0:P], start=True, stop=True)
                mm(bank(name)[:, P:3 * P], fqT[0:66, h, P:S], fkT[0:66, h, :], start=True, stop=True).then_inc(full_sem(name), 1)
            for i in range(4):
                read(pe, f"N{i}")
            memory_transposes("PN", pm1)

            def fox_output(h):
                read(pe, f"PF{h}")
                g_, hh = divmod(h, 4)
                if hh == 0:
                    free(pe, f"FO{g_}")
                vh = [val[:, b, FD * h:FD * h + FD] for b in range(TB)]
                mm(bank(f"FO{g_}")[:, FD * hh:FD * hh + FD], probT[hh][:, 0:P], vh[0], start=True, stop=True)
                o = bank(f"FO{g_}")[:, 256 + FD * hh:256 + FD * hh + FD]
                mm(o, probT[hh][:, P:2 * P], vh[0], start=True, stop=False)
                mm(o, probT[hh][:, 2 * P:3 * P], vh[1], start=False,
                   stop=True).then_inc(full_sem(f"FO{g_}") if hh == 3 else sem("fox_heads"), 1)

            for b in range(TB):
                read(pe, f"FV{b}0"), read(pe, f"FV{b}1")
            for h in range(FH):
                free(pe, f"PF{h}")
                pe.wait_ge(sem("fox_exp"), 2 * h + 2)
                for i in range(3):
                    last = nc.tensor.transpose(bank(f"PF{h}")[:, P * i:P * i + P], logits[:, h, P * i:P * i + P], ident)
                last.then_inc(full_sem(f"PF{h}"), 1)
                if h >= 2:
                    fox_output(h - 2)
                if h == 4:
                    memory_outputs("MW", "PN", pmT1, vm1)
            fox_output(FH - 2)
            fox_output(FH - 1)
            read(pe, "FO2"), read(pe, "MW")
            transposes("TP", mixed)
            output_projection("X", ("out1a", "out1b"), "TP")
            transposes("TR", xs, "ffn1_ready")
            project("RL", [(bank("RL")[:, NE * b:NE * b + NE], lambda c, b=b: hT[:, c, tok(b)], lambda c: wr[:, c, :])
                           for b in range(TB)], "TR")
            pe.wait_ge(sem("chosen"), 1)
            free(pe, "POS")
            mm(bank("POS")[:, 0:NE], const("tri"), sel[:, 0, :], start=True, stop=True)
            mm(bank("POS")[:, NE:2 * NE], const("ones"), sel[:, 0, :], start=True, stop=False)
            mm(bank("POS")[:, NE:2 * NE], const("tri"), sel[:, 1, :], start=False, stop=True).then_inc(full_sem("POS"), 1)
            free(pe, "CNT")
            for b in range(TB):
                last = mm(bank("CNT")[0:1, 0:NE], const("ones")[:, 0:1], sel[:, b, :], start=(b == 0), stop=(b == 1))
            last.then_inc(full_sem("CNT"), 1)

            def gather(parts, n_built):
                pe.wait_ge(sem("perm_built"), n_built)
                for name, count in parts:
                    src, i = e_x["HL".index(name[1])], int(name[2])
                    count_read(pe, count)
                    for c in range(4):
                        for b in range(TB):
                            last = mm(psum[count[0]][:, CAP * c:CAP * (c + 1)], by_chunk(src, b, 4 * i + c), perm_r[:, b, :],
                                      start=(b == 0), stop=(b == 1))
                    last.then_inc(sem(f"bank{count[0]}_full"), 1)

            def scatter(parts):
                for q, count in parts:
                    b, half = divmod(q, 2)
                    count_read(pe, count)
                    for i in range(2):
                        last = mm(psum[count[0]][:, :], scat[0:CAP, b, :], e_y[i][0:CAP, 512 * half:512 * half + 512],
                                  start=(i == 0), stop=(i == 1))
                    last.then_inc(sem(f"bank{count[0]}_full"), 1)

            PARTS = ("GH0", "GH1", "GL0", "GL1")

            def former(count):
                return count[0], count[1] - 1

            def up(n, j, count, chunks):
                if 0 in chunks:
                    pe.wait_ge(sem("gu_split"), (chunk_no(n, j) + 1) * GU_PARTS)
                    count_read(pe, former(count))
                for c in chunks:
                    last = three(psum[count[0]][0:CAP, :].rearrange("p (a n) -> p a n", a=2),
                                 [t_[:, c, :] for t_ in e_xT[j // NF % 2]], [t_[:, c] for t_ in gate_up[j % 2]], c == 0, c == KC - 1)
                if KC - 1 in chunks:
                    last.then_inc(sem(f"bank{count[0]}_full"), 1)

            def experts(k):
                def turn(t_, final):
                    T, n = (k, t_), t_ + TURNS * k
                    for j in range(NBODY):
                        u, fc = divmod(j, NF)
                        alone = final and j == NBODY - 1
                        v_ = (j + 1) // NF
                        following = e_count(T, v_, f"G{(j + 1) % NF}")
                        if fc == NF - 1 and not alone:
                            for name in PARTS:
                                e_read(pe, T, u + 1, name)
                        if not alone:
                            up(n, j + 1, following, range(2))
                        e_read(pe, T, u, f"G{fc}")
                        e_free(pe, T, u, f"T{fc}")
                        for i in range(2):
                            last = nc.tensor.transpose(e_bank(f"T{fc}")[:, CAP * i:CAP * (i + 1)], e_h[0:CAP, i::2],
                                                       ident[0:CAP, 0:CAP])
                        last.then_inc(e_full_sem(f"T{fc}"), 1)
                        if not alone:
                            up(n, j + 1, following, range(2, KC))
                        e_read(pe, T, u, f"T{fc}")
                        pe.wait_ge(sem("down_split"), (chunk_no(n, j) + 1) * D_PARTS)
                        for half in range(2):
                            if fc == 0:
                                e_free(pe, T, u, f"D{half}")
                            for i in range(2):
                                last = three(psum[half][0:CAP, :], [t_[:, i, :] for t_ in e_hT],
                                             [t_[:, i, 512 * half:512 * half + 512] for t_ in down_w],
                                             fc == 0 and i == 0, fc == NF - 1 and i == 1)
                            if fc == NF - 1:
                                last.then_inc(sem(f"bank{half}_full"), 1)
                        if fc < NF - 1:
                            last.then_inc(sem("expert_chunks"), 1)
                        if fc in (1, 2):
                            scatter([(q, e_count(T, u, f"SC{q}", less=1)) for q in (2 * fc - 2, 2 * fc - 1)])
                        if fc == 3:
                            e_free(pe, T, u, "ST")
                            for b in range(TB):
                                nc.tensor.transpose(e_bank("ST")[0:CAP, P * b:P * b + P], perm[:, b, :], ident)
                            for b in range(TB):
                                last = mm(e_bank("ST")[0:CAP, S:S + 1], perm[:, b, :], gate[:, b, bass.ds(t_ * 2 + u, 1)],
                                          start=(b == 0), stop=(b == 1))
                            last.then_inc(e_full_sem("ST"), 1)
                        if fc in (5, 6) and not (final and u == 1):
                            names = PARTS[0:2] if fc == 5 else PARTS[2:4]
                            gather([(name, e_count(T, u + 1, name, less=1)) for name in names], t_ * 2 + (NE * k + u + 2))

                pe.wait_ge(sem("x_split"), 2)
                pe.wait_ge(sem("scatter_cleared"), k + 1)
                for half in range(2):
                    count_read(pe, former(around[k][f"D{half}"]))
                    mm(psum[half][0:CAP, :], scat[:, 0, :], e_y[0][:, 512 * half:512 * half + 512], start=True,
                       stop=True).then_inc(sem(f"bank{half}_full"), 1)
                gather([(name, former(around[k][name])) for name in PARTS], NE * k + 1)
                for name in PARTS:
                    count_read(pe, around[k][name])
                up(TURNS * k, 0, around[k]["G0"], range(KC))
                with pe.Fori(0, TURNS - 1) as t_:
                    turn(t_, False)
                turn(TURNS - 1, True)
                e_read(pe, (k, TURNS), -1, "D0"), e_read(pe, (k, TURNS), -1, "D1")
                scatter([(q, former(around[k][f"SC{q}"])) for q in range(4)])

            experts(0)
            overflow(pe, lambda: experts(1))


_INS = ["x", "mem", "norm_mix", "norm_mem", "norm_ffn", "norm_kv", "norm_final", "w_in_a", "w_gla_gate2", "b_gla_gate2",
        "gla_onorm", "w_in_b", "w_kv", "b_forget", "w_mem_kv", "w_out", "w_ff_gate", "w_ff_up", "w_ff_down", "w_router",
        "w_moe_gate", "w_moe_up", "w_moe_down"]


def kernel(**inputs):
    import concourse.bacc as _bacc
    from concourse.bass_utils import run_bass_kernel_spmd as _run

    nc = _bacc.Bacc("TRN2", target_bir_lowering=False, num_devices=1)
    arrays, args = {}, {}
    for name in _INS:
        arr = np.ascontiguousarray(inputs[name])
        arrays[f"in_{name}"] = arr
        args[name] = nc.dram_tensor(f"in_{name}", arr.shape, mybir.dt.from_np(arr.dtype), kind="ExternalInput").ap()
    arrays["in_table"] = constant_table()
    table = nc.dram_tensor("in_table", arrays["in_table"].shape, F32, kind="ExternalInput").ap()
    arrays["in_params"] = packed(inputs)
    params = nc.dram_tensor("in_params", arrays["in_params"].shape, F32, kind="ExternalInput").ap()
    out = nc.dram_tensor("out", (1, S, D), F32, kind="ExternalOutput").ap()
    program(nc, args, table, params, out)
    return _run(nc, [arrays], core_ids=[0]).results[0]["out"]
```
